# Optimizing a Trainium2 kernel written in Bass

```python
import jax, jax.numpy as jnp
from jax import lax
import numpy as np

D_MODEL = 2048
BATCH = 1
SEQ = 256
DEPTH = 2

CHUNK = 64
Q_BLOCK = 128
N_A = DEPTH // 2
N_B = DEPTH - N_A
PLE_DIM = 256
RMS_EPS = 1e-6
NEG_INF = -1e30

SB_HEAD_DIM = 128
SB_HEADS = D_MODEL // SB_HEAD_DIM
SB_WIDTH = SB_HEADS * SB_HEAD_DIM

QK_NOPE_DIM = 128
QK_ROPE_DIM = 64
V_HEAD_DIM = 128
MLA_HEADS = D_MODEL // V_HEAD_DIM
Q_LORA_RANK = D_MODEL // 4
KV_LORA_RANK = D_MODEL // 4
MLA_WIDTH = MLA_HEADS * V_HEAD_DIM
QK_HEAD_DIM = QK_NOPE_DIM + QK_ROPE_DIM
ROPE_THETA = 10000.0


def rms_norm(x, g):
    xf = x.astype(jnp.float32)
    y = xf * lax.rsqrt(jnp.mean(xf * xf, axis=-1, keepdims=True) + RMS_EPS)
    return (y * g.astype(jnp.float32)).astype(x.dtype)

def rope_tables(seq_len):
    inv = 1.0 / (ROPE_THETA ** (jnp.arange(0, QK_ROPE_DIM, 2, dtype=jnp.float32) / QK_ROPE_DIM))
    ang = jnp.arange(seq_len, dtype=jnp.float32)[:, None] * inv[None, :]
    return jnp.cos(ang), jnp.sin(ang)

def apply_rope(t, cos, sin):
    tf = t.astype(jnp.float32)
    t1, t2 = jnp.split(tf, 2, axis=-1)
    return jnp.concatenate([t1 * cos - t2 * sin, t1 * sin + t2 * cos], axis=-1).astype(t.dtype)

def to_blocks(t):
    b, s = t.shape[:2]
    t = t.reshape((b, s // Q_BLOCK, Q_BLOCK) + t.shape[2:])
    return jnp.moveaxis(t, 1, 0)

def from_blocks(t):
    t = jnp.moveaxis(t, 0, 1)
    return t.reshape((t.shape[0], t.shape[1] * t.shape[2]) + t.shape[3:])

def stick_breaking_attention(q, k, v):
    s_len, dh = q.shape[1], q.shape[-1]
    scale = dh ** -0.5
    kpos = jnp.arange(s_len)

    def one_block(args):
        i, qi = args
        qpos = i * Q_BLOCK + jnp.arange(Q_BLOCK)
        z = jnp.einsum('bqhd,bkhd->bhqk', qi, k, preferred_element_type=jnp.float32) * scale
        strict = kpos[None, :] < qpos[:, None]
        log_keep = jnp.where(strict, jax.nn.log_sigmoid(-z), 0.0)
        later = lax.cumsum(log_keep, axis=3, reverse=True) - log_keep
        w = jnp.where(strict, jnp.exp(jax.nn.log_sigmoid(z) + later), 0.0)
        return jnp.einsum('bhqk,bkhd->bqhd', w.astype(v.dtype), v)

    out = lax.map(one_block, (jnp.arange(s_len // Q_BLOCK), to_blocks(q)))
    return from_blocks(out)

def mla_attention(q_nope, q_rope, k_nope, k_rope, v):
    s_len = q_nope.shape[1]
    scale = QK_HEAD_DIM ** -0.5
    kchunk = jnp.arange(s_len) // CHUNK

    def one_block(args):
        i, qn, qr = args
        qchunk = (i * Q_BLOCK + jnp.arange(Q_BLOCK)) // CHUNK
        s = (jnp.einsum('bqhd,bkhd->bhqk', qn, k_nope, preferred_element_type=jnp.float32)
             + jnp.einsum('bqhr,bkr->bhqk', qr, k_rope, preferred_element_type=jnp.float32)) * scale
        s = jnp.where(kchunk[None, :] <= qchunk[:, None], s, NEG_INF)
        prob = jax.nn.softmax(s, axis=-1)
        return jnp.einsum('bhqk,bkhd->bqhd', prob.astype(v.dtype), v)

    out = lax.map(one_block, (jnp.arange(s_len // Q_BLOCK), to_blocks(q_nope), to_blocks(q_rope)))
    return from_blocks(out)

def mixer_a(h, w_in, w_out):
    b, s, _ = h.shape
    q, k, v, g = jnp.split(h @ w_in, 4, axis=-1)
    heads = lambda t: t.reshape(b, s, SB_HEADS, SB_HEAD_DIM)
    o = stick_breaking_attention(heads(q), heads(k), heads(v)).reshape(b, s, SB_WIDTH)
    return (o * jax.nn.silu(g)) @ w_out

def shared_kv(x, kv_norm, w_dkv, kv_latent_norm, w_uk, w_uv, cos, sin):
    b, s, _ = x.shape
    ckv, k_rope = jnp.split(rms_norm(x, kv_norm) @ w_dkv, [KV_LORA_RANK], axis=-1)
    ckv = rms_norm(ckv, kv_latent_norm)
    k_nope = (ckv @ w_uk).reshape(b, s, MLA_HEADS, QK_NOPE_DIM)
    v = (ckv @ w_uv).reshape(b, s, MLA_HEADS, V_HEAD_DIM)
    k_rope = apply_rope(k_rope, cos, sin)
    return k_nope, k_rope, v

def mixer_b(h, kv, w_in, q_latent_norm, w_uq, w_out, cos, sin):
    b, s, _ = h.shape
    k_nope, k_rope, v = kv
    cq, g = jnp.split(h @ w_in, [Q_LORA_RANK], axis=-1)
    q = (rms_norm(cq, q_latent_norm) @ w_uq).reshape(b, s, MLA_HEADS, QK_HEAD_DIM)
    q_nope, q_rope = jnp.split(q, [QK_NOPE_DIM], axis=-1)
    q_rope = apply_rope(q_rope, cos[:, None, :], sin[:, None, :])
    o = mla_attention(q_nope, q_rope, k_nope, k_rope, v).reshape(b, s, MLA_WIDTH)
    return (o * jax.nn.silu(g)) @ w_out

def residual_update(x, out, g_post, p_i, w_pp, w_pg):
    x = x + rms_norm(out, g_post)
    return x + (p_i @ w_pp) * jax.nn.sigmoid(x @ w_pg)

def first_inputs(seed: int = 0) -> dict:
    key = jax.random.key(seed)
    ks = jax.random.split(key, 17)

    def w(k, shape, fan_in):
        return jax.random.normal(k, shape, jnp.float32) * fan_in ** -0.5

    def gain(k, shape):
        return 1.0 + 0.05 * jax.random.normal(k, shape, jnp.float32)

    return {
        "x": jax.random.normal(ks[0], (BATCH, SEQ, D_MODEL), jnp.float32),
        "p": jax.random.normal(ks[1], (DEPTH, BATCH, SEQ, PLE_DIM), jnp.float32),
        "norm_pre": gain(ks[2], (DEPTH, D_MODEL)),
        "norm_post": gain(ks[3], (DEPTH, D_MODEL)),
        "w_in_a": w(ks[4], (N_A, D_MODEL, 4 * SB_WIDTH), D_MODEL),
        "w_out_a": w(ks[5], (N_A, SB_WIDTH, D_MODEL), SB_WIDTH),
        "w_in_b": w(ks[6], (N_B, D_MODEL, Q_LORA_RANK + MLA_WIDTH), D_MODEL),
        "q_latent_norm": gain(ks[7], (N_B, Q_LORA_RANK)),
        "w_uq": w(ks[8], (N_B, Q_LORA_RANK, MLA_HEADS * QK_HEAD_DIM), Q_LORA_RANK),
        "w_out_b": w(ks[9], (N_B, MLA_WIDTH, D_MODEL), MLA_WIDTH),
        "kv_norm": gain(ks[10], (D_MODEL,)),
        "w_dkv": w(ks[11], (D_MODEL, KV_LORA_RANK + QK_ROPE_DIM), D_MODEL),
        "kv_latent_norm": gain(ks[12], (KV_LORA_RANK,)),
        "w_uk": w(ks[13], (KV_LORA_RANK, MLA_HEADS * QK_NOPE_DIM), KV_LORA_RANK),
        "w_uv": w(ks[14], (KV_LORA_RANK, MLA_WIDTH), KV_LORA_RANK),
        "w_ple_proj": w(ks[15], (DEPTH, PLE_DIM, D_MODEL), PLE_DIM),
        "w_ple_gate": w(ks[16], (DEPTH, D_MODEL, D_MODEL), D_MODEL),
    }

def first_block(x, p, norm_pre, norm_post, w_in_a, w_out_a, w_in_b, q_latent_norm, w_uq, w_out_b,
              kv_norm, w_dkv, kv_latent_norm, w_uk, w_uv, w_ple_proj, w_ple_gate):
    cos, sin = rope_tables(x.shape[1])
    for i in range(N_A):
        out = mixer_a(rms_norm(x, norm_pre[i]), w_in_a[i], w_out_a[i])
        x = residual_update(x, out, norm_post[i], p[i], w_ple_proj[i], w_ple_gate[i])
    kv = shared_kv(x, kv_norm, w_dkv, kv_latent_norm, w_uk, w_uv, cos, sin)
    for j in range(N_B):
        i = N_A + j
        out = mixer_b(rms_norm(x, norm_pre[i]), kv, w_in_b[j], q_latent_norm[j], w_uq[j], w_out_b[j], cos, sin)
        x = residual_update(x, out, norm_post[i], p[i], w_ple_proj[i], w_ple_gate[i])
    return x


DEPTH_2 = 1

N_META = 16
MIX_WIDTH = D_MODEL
GLA_WIDTH = MIX_WIDTH // 2
POOL_WIDTH = MIX_WIDTH - GLA_WIDTH
GLA_HEADS = 4
GLA_DV = GLA_WIDTH // GLA_HEADS
GLA_DK = GLA_DV // 2
GLA_KW = GLA_HEADS * GLA_DK
GATE_RANK = 16
GATE_TAU = 16.0
POOL_WINDOWS = (2, 4, 8, 16)
POOL_GROUPS = len(POOL_WINDOWS)
POOL_GC = POOL_WIDTH // POOL_GROUPS
D_FF = 4 * D_MODEL
EPS = 1e-6
SPLIT_POINTS = (
    GLA_KW,
    2 * GLA_KW,
    2 * GLA_KW + GLA_WIDTH,
    2 * GLA_KW + 2 * GLA_WIDTH,
    2 * GLA_KW + 2 * GLA_WIDTH + GATE_RANK,
)
D_IN = 2 * GLA_KW + 2 * GLA_WIDTH + GATE_RANK + POOL_WIDTH


def rmsnorm(x, w):
    xf = x.astype(jnp.float32)
    y = xf * lax.rsqrt(jnp.mean(xf * xf, axis=-1, keepdims=True) + EPS)
    return (y * w.astype(jnp.float32)).astype(x.dtype)

def gla_chunked(q, k, v, logg):
    B, T, H, DK = q.shape
    DV = v.shape[-1]
    N = T // CHUNK

    def chunks(a):
        return a.reshape(B, N, CHUNK, H, a.shape[-1]).transpose(0, 3, 1, 2, 4)

    q, k, v, logg = chunks(q), chunks(k), chunks(v), chunks(logg)
    G = jnp.cumsum(logg, axis=3)
    G_last = G[:, :, :, -1:, :]
    q_dec = q * jnp.exp(G)
    k_inv = k * jnp.exp(-G)
    causal = jnp.tril(jnp.ones((CHUNK, CHUNK), dtype=bool))
    scores = jnp.einsum('bhncd,bhnsd->bhncs', q_dec, k_inv)
    scores = jnp.where(causal, scores, 0.0)
    o_intra = jnp.einsum('bhncs,bhnsv->bhncv', scores, v)
    k_to_end = k * jnp.exp(G_last - G)
    dS = jnp.einsum('bhncd,bhncv->bhndv', k_to_end, v)
    decay = jnp.exp(G_last[:, :, :, 0, :])

    def step(S, inp):
        dec, ds = inp
        return dec[..., None] * S + ds, S

    S0 = jnp.zeros((B, H, DK, DV), jnp.float32)
    _, S_prev = lax.scan(step, S0, (decay.transpose(2, 0, 1, 3), dS.transpose(2, 0, 1, 3, 4)))
    S_prev = S_prev.transpose(1, 2, 0, 3, 4)
    o_inter = jnp.einsum('bhncd,bhndv->bhncv', q_dec, S_prev)
    o = o_intra + o_inter
    return o.transpose(0, 2, 3, 1, 4).reshape(B, T, H, DV)

def multiscale_pool(pu, pool_w, pool_scale):
    B, L, _ = pu.shape
    xg = pu.astype(jnp.float32).reshape(B, L, POOL_GROUPS, POOL_GC)
    cs = jnp.pad(jnp.cumsum(xg, axis=1), ((0, 0), (1, 0), (0, 0), (0, 0)))
    t = jnp.arange(L)
    win = jnp.array(POOL_WINDOWS, dtype=jnp.int32)
    lo = jnp.maximum(t[:, None] + 1 - win[None, :], 0)
    g_idx = jnp.arange(POOL_GROUPS)[None, :]
    window_sum = cs[:, 1:] - cs[:, lo, g_idx]
    count = (t[:, None] + 1 - lo).astype(jnp.float32)[None, :, :, None]
    y = window_sum / count - xg
    y = jnp.einsum('blgc,gcd->blgd', y, pool_w.astype(jnp.float32))
    return y.reshape(B, L, POOL_WIDTH) * pool_scale.astype(jnp.float32)

def hybrid_layer(h, norm1_w, w_in, gate_w2, gate_b, gla_norm_w, pool_w, pool_scale,
                 w_out, norm2_w, mlp_w1, mlp_w2):
    B, L, _ = h.shape
    u = rmsnorm(h, norm1_w)
    proj = u @ w_in
    q, k, v, r, glr, pu = jnp.split(proj, SPLIT_POINTS, axis=-1)

    g_raw = (glr @ gate_w2 + gate_b).astype(jnp.float32)
    logg = jax.nn.log_sigmoid(g_raw) / GATE_TAU
    pad = (-N_META) % CHUNK

    def heads(a, d):
        a = a.astype(jnp.float32).reshape(B, L, GLA_HEADS, d)
        return jnp.pad(a, ((0, 0), (pad, 0), (0, 0), (0, 0)))

    o = gla_chunked(heads(q, GLA_DK) * (GLA_DK ** -0.5), heads(k, GLA_DK),
                    heads(v, GLA_DV), heads(logg, GLA_DK))[:, pad:]
    o = rmsnorm(o, gla_norm_w)
    gate_out = jax.nn.silu(r.astype(jnp.float32)).reshape(B, L, GLA_HEADS, GLA_DV)
    o_gla = (o * gate_out).reshape(B, L, GLA_WIDTH)

    o_pool = multiscale_pool(pu, pool_w, pool_scale)

    mixed = jnp.concatenate([o_gla, o_pool], axis=-1).astype(h.dtype)
    h = h + mixed @ w_out

    z = rmsnorm(h, norm2_w) @ mlp_w1
    h = h + jnp.square(jax.nn.relu(z)) @ mlp_w2
    return h

def second_inputs(seed: int = 0) -> dict:
    key = jax.random.key(seed)
    ks = jax.random.split(key, 16)
    f32 = jnp.float32
    nrm = lambda k, shape, s: jax.random.normal(k, shape, f32) * s
    return {
        "x": nrm(ks[0], (BATCH, SEQ, D_MODEL), 1.0),
        "meta_tokens": nrm(ks[1], (N_META, D_MODEL), 1.0),
        "norm1_w": 1.0 + nrm(ks[2], (DEPTH_2, D_MODEL), 0.02),
        "w_in": nrm(ks[3], (DEPTH_2, D_MODEL, D_IN), D_MODEL ** -0.5),
        "gate_w2": nrm(ks[4], (DEPTH_2, GATE_RANK, GLA_KW), GATE_RANK ** -0.5),
        "gate_b": nrm(ks[5], (DEPTH_2, GLA_KW), 0.1),
        "gla_norm_w": 1.0 + nrm(ks[6], (DEPTH_2, GLA_DV), 0.02),
        "pool_w": nrm(ks[7], (DEPTH_2, POOL_GROUPS, POOL_GC, POOL_GC), POOL_GC ** -0.5),
        "pool_scale": 1.0 + nrm(ks[8], (DEPTH_2, POOL_WIDTH), 0.1),
        "w_out": nrm(ks[9], (DEPTH_2, MIX_WIDTH, D_MODEL), MIX_WIDTH ** -0.5),
        "norm2_w": 1.0 + nrm(ks[10], (DEPTH_2, D_MODEL), 0.02),
        "mlp_w1": nrm(ks[11], (DEPTH_2, D_MODEL, D_FF), D_MODEL ** -0.5),
        "mlp_w2": nrm(ks[12], (DEPTH_2, D_FF, D_MODEL), D_FF ** -0.5),
        "final_norm_w": 1.0 + nrm(ks[13], (D_MODEL,), 0.02),
    }

def second_block(x, meta_tokens, norm1_w, w_in, gate_w2, gate_b, gla_norm_w, pool_w,
              pool_scale, w_out, norm2_w, mlp_w1, mlp_w2, final_norm_w):
    B = x.shape[0]
    meta = jnp.broadcast_to(meta_tokens[None].astype(x.dtype), (B, N_META, D_MODEL))
    h = jnp.concatenate([meta, x], axis=1)
    for i in range(DEPTH_2):
        h = hybrid_layer(h, norm1_w[i], w_in[i], gate_w2[i], gate_b[i], gla_norm_w[i],
                         pool_w[i], pool_scale[i], w_out[i], norm2_w[i], mlp_w1[i], mlp_w2[i])
    h = rmsnorm(h, final_norm_w)
    return h[:, N_META:]


def setup_inputs(seed=0):
    out = dict(first_inputs(seed))
    for name, value in second_inputs(seed + 1).items():
        if name != "x":
            out[name + "_2"] = value
    return out


def reference(
    x, p, norm_pre, norm_post, w_in_a, w_out_a, w_in_b, q_latent_norm, w_uq, w_out_b, kv_norm,
    w_dkv, kv_latent_norm, w_uk, w_uv, w_ple_proj, w_ple_gate, meta_tokens_2, norm1_w_2, w_in_2,
    gate_w2_2, gate_b_2, gla_norm_w_2, pool_w_2, pool_scale_2, w_out_2, norm2_w_2, mlp_w1_2,
    mlp_w2_2, final_norm_w_2,
):
    x = first_block(
        x, p, norm_pre, norm_post, w_in_a, w_out_a, w_in_b, q_latent_norm, w_uq, w_out_b,
        kv_norm, w_dkv, kv_latent_norm, w_uk, w_uv, w_ple_proj, w_ple_gate,
    )
    return second_block(
        x, meta_tokens_2, norm1_w_2, w_in_2, gate_w2_2, gate_b_2, gla_norm_w_2, pool_w_2,
        pool_scale_2, w_out_2, norm2_w_2, mlp_w1_2, mlp_w2_2, final_norm_w_2,
    )


_drawn_inputs = setup_inputs


def setup_inputs(seed=0):
    import zlib

    import numpy as np

    out = dict(_drawn_inputs(seed))
    spreads = {}
    factors = {'norm1_w_2': 5.315,
     'gate_b_2': 6.104,
     'gla_norm_w_2': 8.0,
     'norm2_w_2': 14.298,
     'final_norm_w_2': 7.708,
     'pool_scale_2': 3.217}
    for name, (base, spread) in spreads.items():
        noise = np.random.default_rng([zlib.crc32(name.encode()), seed]).standard_normal(out[name].shape)
        drawn = base * np.exp(spread * noise) if base else spread * noise
        out[name] = __import__('jax').numpy.asarray(drawn.astype(out[name].dtype))
    for name, factor in factors.items():
        out[name] = (out[name] * factor).astype(out[name].dtype)
    return out
```

```python
from contextlib import ExitStack

import numpy as np
import concourse.bass as bass
from concourse import mybir

F32 = mybir.dt.float32
F32R = mybir.dt.float32r
ALU = mybir.AluOpType
ACT = mybir.ActivationFunctionType
AX = mybir.AxisListType.X

P = 128
SEQ = 256
TT = SEQ // P
D = 2048
KT = D // P
CH = 512
NCH = D // CH
QT = CH // P
EPS = 1e-6
NEG = -1e30

HEADS = 16
HD = 128
ROPE = 64
LORA = 512
LK = LORA // P
QHEAD = HD + ROPE
CHUNK = 64

META = 16
GLA_H = 4
DK = 128
DV = 256
GKW = GLA_H * DK
GRANK = 16
TAU = 16.0
WINDOWS = (2, 4, 8, 16)
PGC = 256
DFF = 4 * D

UNIT = 1024
RING = 4


class Stage:

    def __init__(self, name, weight, chunks, units, kt, cols):
        self.name, self.weight, self.chunks, self.units, self.kt, self.cols = name, weight, chunks, units, kt, cols
        self.u0 = self.c0 = 0


def plan():
    deep = KT // 2
    st = [
        Stage("qk", "w_in_a", 8, deep, 2, CH), Stage("v", "w_in_a", 4, deep, 2, CH),
        Stage("g", "w_in_a", 4, deep, 2, CH), Stage("out_a", "w_out_a", 4, deep, 2, CH),
        Stage("ple0", "w_ple_proj", 4, 1, 2, CH), Stage("gate0", "w_ple_gate", 4, deep, 2, CH),
        Stage("ckv", "w_dkv", 1, deep, 2, CH), Stage("krope", "w_dkv", 1, 1, KT, ROPE),
        Stage("cq", "w_in_b", 1, deep, 2, CH), Stage("uk", "w_uk", 4, 2, 2, CH), Stage("uv", "w_uv", 4, 2, 2, CH),
        Stage("uq", "w_uq", 8, 2, 2, 2 * QHEAD), Stage("gb", "w_in_b", 4, deep, 2, CH),
        Stage("out_b", "w_out_b", 4, deep, 2, CH), Stage("ple1", "w_ple_proj", 4, 1, 2, CH),
        Stage("gate1", "w_ple_gate", 4, deep, 2, CH),
        Stage("glr", "w_in_2", 1, 1, KT, GRANK), Stage("k2", "w_in_2", 1, deep, 2, CH),
        Stage("q2", "w_in_2", 1, deep, 2, CH), Stage("v2", "w_in_2", 2, deep, 2, CH),
        Stage("pu", "w_in_2", 2, deep, 2, CH), Stage("r2", "w_in_2", 2, deep, 2, CH),
        Stage("pool", "pool_w_2", 2, 1, 4, PGC), Stage("out2", "w_out_2", 4, deep, 2, CH),
    ]
    for b in range(DFF // D):
        st += [Stage(f"up{b}", "mlp_w1_2", 4, deep, 2, CH), Stage(f"down{b}", "mlp_w2_2", 4, deep, 2, CH)]
    u = c = 0
    for s in st:
        s.u0, s.c0 = u, c
        u += s.units * s.chunks
        c += s.chunks
    return {s.name: s for s in st}, u


def constants():
    s, t = np.arange(P)[:, None], np.arange(P)[None, :]
    t2 = np.arange(SEQ)[None, :]
    inv = (1.0 / (np.float32(10000.0) ** (np.arange(0, ROPE, 2, dtype=np.float32) / np.float32(ROPE)))).astype(np.float32)
    ang = np.arange(SEQ, dtype=np.float32)[:, None] * inv[None, :]
    two = lambda a: np.concatenate([np.repeat(a[i * P:(i + 1) * P, None, :], 2, 1).reshape(P, ROPE) for i in range(TT)], 1)
    same = s // CHUNK == t // CHUNK
    hole = NEG * ((s < CHUNK) & (t >= CHUNK))
    meta_s = s - META
    parts = {
        "ident": s == t,
        "suffix": s >= t,
        "ones": np.ones((P, P)),
        "strict": s < t,
        "strict_neg": NEG * (s >= t),
        "chunk_neg": np.concatenate([hole, np.zeros((P, P)), hole], 1),
        "cos": two(np.cos(ang)), "sin": two(np.sin(ang)),
        "gla_causal": same & (s <= t),
        "gla_after": same & (s > t),
        "gla_half": np.concatenate([s // CHUNK == 0, s // CHUNK == 1], 1),
        "band": np.concatenate([((t2 >= s) & (t2 - s < w)) / w - (t2 == s) * 1.0 for w in WINDOWS], 1),
        "band_meta": np.concatenate([((s < META) & (t - meta_s < w)) / w for w in WINDOWS], 1),
    }
    where, at = {}, 0
    for name, a in parts.items():
        where[name] = (at, a.shape[1])
        at += a.shape[1]
    return np.ascontiguousarray(np.concatenate([np.asarray(a, np.float32) for a in parts.values()], 1), np.float32), where


def build(nc, w, const, out):
    S, units = plan()
    table, where = constants()
    ctx = ExitStack()
    with ctx:
        place = [(nc.sbuf_base + 63) // 64 * 64]

        def region(nbytes):
            at = place[0]
            place[0] = at + (nbytes + 63) // 64 * 64
            assert place[0] <= nc.sbuf_usable_end, place[0]
            return at

        def sb(name, shape, dt, at):
            return nc.alloc_sbuf_tensor_at(name, shape, dt, offset=at)

        KB = 1024
        raw = sb("raw", [P, RING, UNIT], F32, region(16 * KB))
        whi = sb("whi", [P, RING, UNIT], F32R, region(16 * KB))
        wlo = sb("wlo", [P, RING, UNIT], F32R, region(16 * KB))
        x = sb("x", [P, TT, D], F32, region(16 * KB))
        nat = sb("nat", [P, TT, D], F32, region(16 * KB))
        r0, r1, r2 = region(32 * KB), region(32 * KB), region(16 * KB)
        stg_at = region(8 * KB)
        r3 = region(8 * KB)
        r4 = region(9 * KB)
        ahi = sb("ahi", [P, KT, SEQ], F32R, r0)
        alo = sb("alo", [P, KT, SEQ], F32R, r0 + 16 * KB)
        bhi = sb("bhi", [P, KT, SEQ], F32R, r1)
        blo = sb("blo", [P, KT, SEQ], F32R, r1 + 16 * KB)
        stg = sb("stg", [P, 2, TT, CH], F32, stg_at)
        gains = sb("gains", [P, D], F32, r3)
        tab = sb("tab", [P, table.shape[1]], F32, region(table.shape[1] * 4))
        p_at = region(8 * KB)
        phi = sb("phi", [P, 2, 2, SEQ], F32R, p_at)
        plo = sb("plo", [P, 2, 2, SEQ], F32R, p_at + 4 * KB)
        gcol = sb("gcol", [P, P], F32, region(512))
        st_at = region(1024)
        ssq = sb("ssq", [P, TT, 4], F32, st_at)
        ssum = sb("ssum", [P, 8], F32, st_at + 64)
        root = sb("root", [P, 8], F32, st_at + 128)
        rs = sb("rs", [P, 8, 8], F32, st_at + 192)
        mx = sb("mx", [P, 2, 4], F32, st_at + 512)
        den = sb("den", [P, 2, 4], F32, st_at + 576)
        rden = sb("rden", [P, 2, 4], F32, st_at + 640)
        eps = sb("eps", [P, 1], F32, st_at + 704)
        qkT = sb("qkT", [P, 2 * HEADS, SEQ], F32, r1)
        vA = sb("vA", [P, TT, D], F32, r2)
        zA = sb("zA", [P, 2, 3 * P], F32, r3)
        tA = sb("tA", [P, 2, 3 * P], F32, r3 + 3 * KB)
        pp = sb("pp", [P, TT, D], F32, r2)
        knT = sb("knT", [P, HEADS, SEQ], F32, r1)
        vB = sb("vB", [P, TT, D], F32, r1 + 16 * KB)
        kvhi = sb("kvhi", [P, LK, SEQ], F32R, r2)
        kvlo = sb("kvlo", [P, LK, SEQ], F32R, r2 + 4 * KB)
        cqhi = sb("cqhi", [P, LK, SEQ], F32R, r2 + 8 * KB)
        cqlo = sb("cqlo", [P, LK, SEQ], F32R, r2 + 12 * KB)
        sB = sb("sB", [P, 2, 3 * P], F32, r3)
        pB = sb("pB", [P, 2, 3 * P], F32, r3 + 3 * KB)
        qn = sb("qn", [P, 2, 2, SEQ], F32, r4)
        qr = sb("qr", [P, 2, SEQ], F32, r4 + 4 * KB)
        krT = sb("krT", [P, SEQ], F32, r4 + 6 * KB)
        roped = sb("roped", [P, TT, 2 * ROPE], F32, r4 + 7 * KB)
        turn = sb("turn", [P, TT, 2, ROPE // 2], F32, r4 + 8 * KB)
        kraw = sb("kraw", [P, TT, 2, ROPE], F32, r4)
        vC = sb("vC", [P, TT, GLA_H * DV], F32, r0)
        vM = sb("vM", [P, GLA_H * DV], F32, r0 + 8 * KB)
        kend = sb("kend", [P, TT, GKW], F32, r0 + 12 * KB)
        kendM = sb("kendM", [P, GKW], F32, r0 + 16 * KB)
        kTc = sb("kTc", [P, GLA_H, SEQ], F32, r0 + 18 * KB)
        qA = sb("qA", [P, GLA_H, TT, P], F32, r0 + 22 * KB)
        qB = sb("qB", [P, GLA_H, TT, P], F32, r0 + 26 * KB)
        oneM = sb("oneM", [P, CH], F32, r0 + 30 * KB)
        metaT = sb("metaT", [P, KT, P], F32R, r2)
        logg = sb("logg", [P, TT, GKW], F32, r2 + 8 * KB)
        loggM = sb("loggM", [P, GKW], F32, r2 + 12 * KB)
        msc = sb("msc", [P, GKW], F32, r2 + 14 * KB)
        yhi = sb("yhi", [P, 8, SEQ], F32R, r2)
        ylo = sb("ylo", [P, 8, SEQ], F32R, r2 + 8 * KB)
        puM = sb("puM", [P, 2 * CH], F32, p_at)
        metax = sb("metax", [P, D], F32, r3)
        state = sb("state", [P, 2, 4, DV], F32, r3)
        glr = sb("glr", [P, TT, P], F32, r4)
        glrM = sb("glrM", [P, P], F32, r4 + 1 * KB)
        glrT = sb("glrT", [P, SEQ + META], F32, r4 + 1536)
        gw2 = sb("gw2", [P, GKW], F32, r4 + 3 * KB)
        brow = sb("brow", [P, GKW], F32, r4 + 5 * KB)
        decay = sb("decay", [P, GLA_H, 4], F32, r4 + 7 * KB)
        sc = sb("sc", [P, TT, P], F32, r4 + 7 * KB + 512)

        acc = [[ctx.enter_context(nc.psum_tensor(f"acc{p}{t}", [P, CH], F32)) for t in range(TT)] for p in range(2)]
        tp = [ctx.enter_context(nc.psum_tensor(f"tp{p}", [P, CH], F32)) for p in range(2)]
        xb = [ctx.enter_context(nc.psum_tensor(f"xb{p}", [P, CH], F32)) for p in range(2)]

        def const_of(name, rows=P):
            a, n = where[name]
            return tab[0:rows, a:a + n]

        ident = const_of("ident")
        GC = {"pre0": 0, "pre1": 16, "kv": 32, "norm1": 48, "norm2": 64, "kvl": 80, "ql": 84, "gla": 88, "pool": 90}
        RS = {"pre0": 0, "post": 1, "pre1": 2, "kvl": 3, "ql": 4, "norm1": 5, "norm2": 0, "final": 1}

        sems = {}

        def sem(name):
            if name not in sems:
                sems[name] = ctx.enter_context(nc.semaphore(name))
            return sems[name]

        raw_full = [sem(f"raw_full{i}") for i in range(RING)]
        hi_done, lo_done = sem("hi_done"), sem("lo_done")
        unit_used = sem("unit_used")
        evac_act, evac_dve = sem("evac_act"), sem("evac_dve")
        tp_full, tp_hi, tp_done = sem("tp_full"), sem("tp_hi"), sem("tp_done")
        x_done = sem("x_done")

        order = [("gcol", 1), ("p", 2), ("x0", 8), ("qk", 16), ("ogA", 8), ("x1", 8), ("x2a", 8), ("x2b", 8), ("ckv", 2), ("kr", 1),
                 ("cq", 2), ("uk", 8), ("uq", 16), ("ogB", 8), ("x3", 8), ("x4", 8), ("meta", 1), ("glr", 1), ("kinv", 2),
                 ("qdec", 2), ("pool", 4), ("mixed", 8), ("x5", 8)] + [(f"mlp{q}", 8) for q in range(DFF // D)]
        whole = ("gcol", "qk", "kr", "uk", "uq", "glr", "kinv", "qdec")
        BATCH, n_all, n_split = {}, 0, 0
        for name, n in order:
            BATCH[name] = (n_all, n_split)
            n_all += n
            n_split += 0 if name in whole else n

        def shape_of(u):
            s = max((s for s in S.values() if s.u0 <= u), key=lambda s: s.u0)
            return s.kt, s.cols

        def unit_source(s, j, uu):
            if s.name == "pool":
                return w["pool_w_2"][0, 2 * j:2 * j + 2].rearrange("g (k p) n -> p (g k) n", p=P)
            base = {"v": 2 * D, "g": 3 * D, "krope": LORA, "gb": LORA, "q2": 0, "k2": GKW, "v2": 2 * GKW,
                    "r2": 2 * GKW + GLA_H * DV, "glr": 2 * GKW + 2 * GLA_H * DV,
                    "pu": 2 * GKW + 2 * GLA_H * DV + GRANK}.get(s.name, 0)
            t = w[s.weight]
            if len(t.shape) == 3:
                t = t[1 if s.name in ("ple1", "gate1") else 0]
            row = uu * s.kt * P
            if s.name.startswith("down"):
                row = row + int(s.name[4:]) * D
            if s.name.startswith("up"):
                base = int(s.name[2:]) * D
            col = base + j * s.cols
            return t[row:row + s.kt * P, bass.ds(col, s.cols)].rearrange("(k p) n -> p k n", p=P)

        def x_rows(ap):
            return ap.rearrange("(t p) d -> p t d", p=P)

        block = ctx.enter_context(nc.Block())

        @block.sync
        def _(sp):
            def load(s, j, uu, r=0):
                u = s.u0 + j * s.units + uu if isinstance(j, int) else s.u0 + uu
                if u >= RING or not isinstance(r, int):
                    sp.wait_ge(lo_done, u - RING + 1 + r)
                dst = raw[:, u % RING, 0:s.kt * s.cols].rearrange("p (k n) -> p k n", k=s.kt)
                sp.dma_start(dst, unit_source(s, j, uu)).then_inc(raw_full[u % RING], 16)

            def stage(name, lo=0, hi=None):
                s = S[name]
                for j in range(lo, s.chunks if hi is None else hi):
                    for uu in range(s.units):
                        load(s, j, uu)

            sp.dma_start(tab[:, :], const).then_inc(sem("tab_in"), 16)
            rows = [("norm_pre", 0, "pre0", 16), ("norm_pre", 1, "pre1", 16), ("kv_norm", None, "kv", 16),
                    ("norm1_w_2", 0, "norm1", 16), ("norm2_w_2", 0, "norm2", 16), ("kv_latent_norm", None, "kvl", 4),
                    ("q_latent_norm", 0, "ql", 4), ("gla_norm_w_2", 0, "gla", 2), ("pool_scale_2", 0, "pool", 8)]
            for name, i, key, n in rows:
                src = w[name] if i is None else w[name][i]
                sp.dma_start(gains[GC[key]:GC[key] + n, 0:P], src.rearrange("(a b) -> a b", b=P)).then_inc(sem("gain_rows_in"), 16)
            for l in range(2):
                sp.dma_start(stg[:, l, :, 0:2 * P], x_rows(w["p"][l, 0])).then_inc(sem(f"p_in{l}"), 16)
            for j in range(NCH):
                c = slice(j * CH, (j + 1) * CH)
                sp.dma_start(x[:, :, c], x_rows(w["x"][0])[:, :, c]).then_inc(sem(f"x_in{j}"), 16)
            stage("qk", 0, 1)
            s = S["qk"]
            with sp.Fori(1, s.chunks) as j:
                for uu in range(s.units):
                    load(s, j, uu, r=j * s.units)
            stage("v")
            stage("g")
            stage("out_a", 0, 1)
            sp.wait_ge(sem("attA_d"), HEADS)
            sp.wait_ge(sem("attA_w"), HEADS)
            sp.dma_start(gains[:, :], w["norm_post"][0:1, :].to_broadcast((P, D))).then_inc(sem("post_in0"), 16)
            stage("out_a", 1)
            for name in ("ple0", "gate0", "ckv", "krope", "cq", "uk", "uv", "uq", "gb"):
                stage(name)
            stage("out_b", 0, 1)
            sp.wait_ge(sem("attB_o"), HEADS // 2)
            sp.dma_start(gains[:, :], w["norm_post"][1:2, :].to_broadcast((P, D))).then_inc(sem("post_in1"), 16)
            stage("out_b", 1)
            stage("ple1")
            stage("gate1", 0, 1)
            sp.wait_ge(sem("post1_y"), 8)
            sp.dma_start(metax[0:META, :], w["meta_tokens_2"]).then_inc(sem("meta_in"), 16)
            sp.dma_start(gw2[0:GRANK, :], w["gate_w2_2"][0]).then_inc(sem("gate_in"), 16)
            sp.dma_start(brow[0:1, :], w["gate_b_2"]).then_inc(sem("gate_in2"), 16)
            stage("gate1", 1)
            for name in ("glr", "k2", "q2", "v2", "pu", "r2", "pool"):
                stage(name)
            sp.wait_ge(sem("gla_rs"), 1)
            sp.dma_start(gains[:, :], w["final_norm_w_2"].rearrange("(a b) -> a b", a=1).to_broadcast((P, D))).then_inc(sem("final_in"), 16)
            stage("out2")
            for b in range(DFF // D):
                stage(f"up{b}")
                stage(f"down{b}")
            for j in range(NCH):
                sp.wait_ge(sem("final_y"), TT * (j + 1))
                c = slice(j * CH, (j + 1) * CH)
                sp.dma_start(x_rows(out[0])[:, :, c], nat[:, :, c]).then_inc(sem("stored"), 16)
            sp.wait_ge(sem("stored"), 16 * NCH)

        @block.tensor
        def _(pe):
            b = [0]

            def product(s, j, hi, lo, r=0, rc=0, mid=None, mid_at=4, banks=None, meta=False, behind=1, before=None):
                u, c = s.u0 + j * s.units, s.c0 + j
                bank = banks or acc[c % 2]
                if c >= 2:
                    pe.wait_ge(evac_act, c - behind + rc)
                    pe.wait_ge(evac_dve, c - behind + rc)
                if before:
                    before()
                for uu in range(s.units):
                    pe.wait_ge(lo_done, u + uu + 1 + r)
                    slot = (u + uu) % RING
                    for k in range(s.kt):
                        kt = uu * s.kt + k
                        cols = slice(k * s.cols, (k + 1) * s.cols)
                        first, last = kt == 0, kt == s.units * s.kt - 1
                        for t in range(TT):
                            tok = slice(t * P, (t + 1) * P)
                            o = bank[t][:, 0:s.cols]
                            pe.matmul(o, hi[:, kt, tok], whi[:, slot, cols], start=first, stop=False)
                            pe.matmul(o, hi[:, kt, tok], wlo[:, slot, cols], start=False, stop=False)
                            mm = pe.matmul(o, lo[:, kt, tok], whi[:, slot, cols], start=False, stop=last)
                        if meta:
                            o = xb[c % 2][:, 0:s.cols]
                            pe.matmul(o, metaT[:, kt, :], whi[:, slot, cols], start=first, stop=False)
                            mm = pe.matmul(o, metaT[:, kt, :], wlo[:, slot, cols], start=False, stop=last)
                    mm.then_inc(unit_used, 1)
                    if mid and uu == mid_at - 1:
                        mid()

            def batch(parts, r=0):
                n = b[0]
                b[0] += 1
                if n >= 2:
                    pe.wait_ge(tp_done, n - 1 + r)
                for src, k, o in parts:
                    mm = pe.transpose(tp[n % 2][:, o:o + k], src, ident[0:k, 0:k])
                mm.then_inc(tp_full, 1)

            def pair(src, f):
                batch([(src[:, t, (2 * f + i) * P:(2 * f + i + 1) * P], P, i * SEQ + t * P) for i in range(2) for t in range(TT)])

            def staged(par, r=0, b_r=0):
                for f in range(2):
                    batch([(stg[:, par, t, (2 * f + i) * P:(2 * f + i + 1) * P], P, i * SEQ + t * P)
                           for i in range(2) for t in range(TT)], r=b_r)

            def x_batches(done, quarters=range(NCH)):
                for j in quarters:
                    if done is None:
                        pe.wait_ge(sem(f"x_in{j}"), 16)
                    elif isinstance(done, Stage):
                        pe.wait_ge(evac_dve, done.c0 + j + 1)
                    else:
                        pe.wait_ge(x_done, done + j + 1)
                    pair(x, 2 * j)
                    pair(x, 2 * j + 1)

            def evacuated(c, r=0):
                pe.wait_ge(evac_act, c + 1 + r)
                pe.wait_ge(evac_dve, c + 1 + r)

            pe.wait_ge(sem("tab_in"), 16)
            pe.wait_ge(sem("gain_rows_in"), 9 * 16)
            batch([(gains[0:98, 0:P], 98, 0)])
            for l in range(2):
                pe.wait_ge(sem(f"p_in{l}"), 16)
                batch([(stg[:, l, t, k * P:(k + 1) * P], P, k * SEQ + t * P) for k in range(2) for t in range(TT)])
            x_batches(None)

            pe.wait_ge(tp_done, b[0])
            s = S["qk"]
            product(s, 0, ahi, alo)
            with pe.Fori(0, 3) as i:
                b_start = b[0]
                for q in (1, 2):
                    rc, r = i * 2, i * (2 * s.units)

                    def turn_last(q=q, rc=rc):
                        evacuated(s.c0 + q - 1, rc)
                        staged((s.c0 + q - 1) % 2, b_r=i * 4)
                    product(s, q, ahi, alo, r=r, rc=rc, mid=turn_last)
            b[0] = b_start + 4 * 3

            def turn_chunk(c):
                def go():
                    evacuated(c)
                    staged(c % 2)
                return go
            product(s, 7, ahi, alo, mid=turn_chunk(6))
            s = S["v"]
            for j in range(4):
                product(s, j, ahi, alo, mid=turn_chunk(7) if j == 0 else None)

            evacuated(S["g"].c0 - 1)
            pe.wait_ge(tp_done, b[0])

            def logits(h):
                if h >= 2:
                    pe.wait_ge(sem("attA_z"), h - 1)
                z = acc[0][h % 2]
                pe.matmul(z[:, 0:SEQ], qkT[:, HEADS + h, 0:P], qkT[:, h, :], start=True, stop=True)
                pe.matmul(z[:, SEQ:SEQ + P], qkT[:, HEADS + h, P:SEQ], qkT[:, h, P:SEQ], start=True, stop=True).then_inc(sem("attA_logits"), 1)

            def later_sums(h):
                pe.wait_ge(sem("attA_sp"), h + 1)
                if h >= 2:
                    pe.wait_ge(sem("attA_d"), h - 1)
                sums = acc[1][h % 2]
                pe.matmul(sums[:, 0:3 * P], const_of("suffix"), tA[:, h % 2, :], start=True, stop=False)
                pe.matmul(sums[:, P:2 * P], const_of("ones"), tA[:, h % 2, 2 * P:3 * P], start=False, stop=True).then_inc(sem("attA_sums"), 1)

            def values(h):
                pe.wait_ge(sem("attA_w"), h + 1)
                if h >= 2:
                    pe.wait_ge(sem("attA_o"), h - 1)
                o = xb[h % 2]
                c = slice(h * HD, (h + 1) * HD)
                pe.matmul(o[:, 0:P], zA[:, h % 2, 0:P], vA[:, 0, c], start=True, stop=True)
                pe.matmul(o[:, P:2 * P], zA[:, h % 2, P:2 * P], vA[:, 0, c], start=True, stop=False)
                pe.matmul(o[:, P:2 * P], zA[:, h % 2, 2 * P:3 * P], vA[:, 1, c], start=False, stop=True).then_inc(sem("attA_out"), 1)

            logits(0)
            for h in range(HEADS):
                if h + 1 < HEADS:
                    logits(h + 1)
                later_sums(h)
                if h >= 1:
                    values(h - 1)
            values(HEADS - 1)

            def att_out():
                pe.wait_ge(sem("attA_d"), HEADS)
                pe.wait_ge(sem("attA_z"), HEADS)

            def og_batches(j, c):
                def go():
                    evacuated(c)
                    pair(nat, 2 * j)
                    pair(nat, 2 * j + 1)
                return go
            s = S["g"]
            for j in range(4):
                product(s, j, ahi, alo, mid=og_batches(j - 1, s.c0 + j - 1) if j else None, before=att_out if j == 0 else None)
            og_batches(3, s.c0 + 3)()

            def post(layer, x0):
                ab = "ab"[layer]
                pe.wait_ge(tp_done, b[0])
                for j in range(4):
                    product(S[f"out_{ab}"], j, bhi, blo)
                for j in range(4):
                    product(S[f"ple{layer}"], j, phi[:, layer], plo[:, layer])
                    if j:
                        x_batches(x0, [j - 1])
                x_batches(x0, [3])
                pe.wait_ge(tp_done, b[0])
                for j in range(4):
                    product(S[f"gate{layer}"], j, ahi, alo, mid=(lambda j=j: x_batches(x0 + 4, [j - 1])) if j else None)
                x_batches(x0 + 4, [3])

            post(0, 0)
            pe.wait_ge(tp_done, b[0])

            product(S["ckv"], 0, bhi, blo)
            x_batches(4)
            product(S["krope"], 0, bhi, blo)
            evacuated(S["ckv"].c0)
            staged(0)
            pe.wait_ge(tp_done, b[0])
            product(S["cq"], 0, ahi, alo)
            pe.wait_ge(sem("k_roped"), 1)
            batch([(roped[:, t, :], P, t * P) for t in range(TT)])
            s = S["uk"]
            for j in range(4):
                product(s, j, kvhi, kvlo)
                if j == 0:
                    evacuated(S["cq"].c0)
                    staged(S["cq"].c0 % 2)
                else:
                    turn_chunk(s.c0 + j - 1)()
            s = S["uv"]
            for j in range(4):
                product(s, j, kvhi, kvlo)
                if j == 0:
                    turn_chunk(s.c0 - 1)()

            s = S["uq"]

            def queries(j, r=0):
                product(s, j, cqhi, cqlo, banks=acc[0], behind=0)
                evacuated(s.c0 + j)
                batch([(stg[:, j % 2, t, i * QHEAD:i * QHEAD + HD], P, i * SEQ + t * P) for i in range(2) for t in range(TT)])
                pe.wait_ge(sem("q_roped"), j + 1)
                batch([(roped[:, t, :], P, t * P) for t in range(TT)])

            def scores(h):
                p, i = (h // 2) % 2, h % 2
                rows = slice(i * ROPE, (i + 1) * ROPE)
                sB_ps = xb[i]
                for o, qt, n in ((0, 0, P), (P, 1, SEQ)):
                    q = slice(qt * P, (qt + 1) * P)
                    pe.matmul(sB_ps[:, o:o + n], qn[:, p, i, q], knT[:, h, 0:n], start=True, stop=False)
                    mm = pe.matmul(sB_ps[:, o:o + n], qr[rows, p, q], krT[rows, 0:n], start=False, stop=True)
                mm.then_inc(sem("attB_s"), 1)

            def turned(h):
                i = h % 2
                pe.wait_ge(sem("attB_p"), h + 1)
                if i == 0 and h >= 2:
                    pe.wait_ge(sem("attB_o"), h // 2)
                for k in range(3):
                    mm = pe.transpose(acc[1][i][:, k * P:(k + 1) * P], sB[:, i, k * P:(k + 1) * P], ident)
                mm.then_inc(sem("attB_t"), 1)

            def outputs(c):
                for i in range(2):
                    h = 2 * c + i
                    pe.wait_ge(sem("attB_pt"), h + 1)
                    o, cols = acc[1][0][:, i * SEQ:(i + 1) * SEQ], slice(h * HD, (h + 1) * HD)
                    pe.matmul(o[:, 0:P], pB[:, i, 0:P], vB[:, 0, cols], start=True, stop=True)
                    pe.matmul(o[:, P:SEQ], pB[:, i, P:2 * P], vB[:, 0, cols], start=True, stop=False)
                    mm = pe.matmul(o[:, P:SEQ], pB[:, i, 2 * P:3 * P], vB[:, 1, cols], start=False, stop=True)
                mm.then_inc(sem("attB_out"), 1)

            evacuated(s.c0 - 1)
            pe.wait_ge(tp_done, b[0])
            queries(0)
            for c in range(8):
                pe.wait_ge(tp_done, b[0])
                scores(2 * c)
                scores(2 * c + 1)
                if c < 7:
                    queries(c + 1)
                turned(2 * c)
                turned(2 * c + 1)
                outputs(c)

            s = S["gb"]
            for j in range(4):
                product(s, j, ahi, alo, mid=og_batches(j - 1, s.c0 + j - 1) if j else None, behind=0 if j == 0 else 1,
                        before=(lambda: pe.wait_ge(sem("attB_o"), 8)) if j == 0 else None)
            og_batches(3, s.c0 + 3)()
            post(1, 8)

            pe.wait_ge(sem("meta_in"), 16)
            batch([(metax[0:META, k * P:(k + 1) * P], META, k * META) for k in range(KT)])
            pe.wait_ge(tp_done, b[0])
            product(S["glr"], 0, bhi, blo, meta=True)
            product(S["k2"], 0, bhi, blo, meta=True)
            evacuated(S["glr"].c0)
            batch([(glr[:, t, :], P, t * P) for t in range(TT)] + [(glrM[0:META, :], META, SEQ)])
            product(S["q2"], 0, bhi, blo)
            pe.wait_ge(tp_done, b[0])
            pe.wait_ge(sem("gate_in"), 16)
            pe.wait_ge(sem("gate_in2"), 16)
            for t in range(TT + 1):
                n = P if t < TT else META
                o = (tp[0], tp[1], xb[1])[t]
                if t == TT:
                    pe.wait_ge(evac_dve, S["k2"].c0 + 1)
                pe.matmul(o[0:n, :], glrT[0:GRANK, t * P:t * P + n], gw2[0:GRANK, :], start=True, stop=False)
                pe.matmul(o[0:n, :], const_of("ones")[0:1, 0:n], brow[0:1, :], start=False, stop=True).then_inc(sem("graw"), 1)
            s = S["v2"]
            product(s, 0, bhi, blo, meta=True, before=lambda: pe.wait_ge(sem("logg"), 3))
            for t in range(TT):
                pe.matmul(tp[t][:, :], const_of("gla_causal"), logg[:, t, :], start=True, stop=True).then_inc(sem("G"), 1)
            for t in range(TT):
                pe.wait_ge(sem("eG"), 2 * (t + 1))
                pe.matmul(tp[t][:, :], const_of("gla_after"), logg[:, t, :], start=True, stop=True).then_inc(sem("G"), 1)
            pe.wait_ge(evac_dve, s.c0 + 1)
            pe.wait_ge(evac_act, s.c0 + 1)
            pe.matmul(xb[0][0:META, :], const_of("gla_after")[0:META, 0:META], loggM[0:META, :], start=True, stop=True).then_inc(sem("G"), 1)
            product(s, 1, bhi, blo, meta=True)
            pe.wait_ge(sem("eG"), 7)
            for h in range(GLA_H):
                for t in range(TT):
                    mm = pe.matmul(xb[0][:, (h * TT + t) * 2:(h * TT + t) * 2 + 2], logg[:, t, h * DK:(h + 1) * DK],
                                   const_of("gla_half"), start=True, stop=True)
            mm.then_inc(sem("G"), 1)
            pe.wait_ge(sem("kinv"), 1)
            for f in range(2):
                pair(nat, f)
            pe.wait_ge(sem("qdec"), 1)
            for f in range(2):
                batch([(stg[:, 0, t, (2 * f + i) * P:(2 * f + i + 1) * P], P, i * SEQ + t * P) for i in range(2) for t in range(TT)])
            s = S["pu"]
            product(s, 0, bhi, blo, meta=True, before=lambda: pe.wait_ge(sem("decay"), 1))
            product(s, 1, bhi, blo, meta=True)

            pe.wait_ge(evac_dve, s.c0 + 2)
            pe.wait_ge(evac_act, s.c0 + 2)
            pe.wait_ge(tp_done, b[0])
            for h in range(GLA_H):
                dk, dv = slice(h * DK, (h + 1) * DK), slice(h * DV, (h + 1) * DV)
                if h:
                    pe.wait_ge(sem("gla_sc"), h)
                for t in range(TT):
                    k_ = kTc[:, h, t * P:(t + 1) * P]
                    pe.matmul(tp[0][:, t * P:t * P + 64], k_, qA[:, h, t, 0:64], start=True, stop=True)
                    mm = pe.matmul(tp[0][:, t * P + 64:t * P + P], k_, qB[:, h, t, 64:P], start=True, stop=True)
                mm.then_inc(sem("gla_scores"), 1)
                if h:
                    pe.wait_ge(sem("gla_state"), h)
                pe.matmul(xb[0][:, 0:DV], kend[0:64, 0, dk], vC[0:64, 0, dv], start=True, stop=True)
                pe.matmul(xb[0][:, DV:2 * DV], kend[0:64, 1, dk], vC[0:64, 1, dv], start=True, stop=True)
                pe.matmul(xb[1][:, 0:DV], kend[64:P, 0, dk], vC[64:P, 0, dv], start=True, stop=True)
                pe.matmul(xb[1][:, DV:2 * DV], kendM[0:META, dk], vM[0:META, dv], start=True, stop=True).then_inc(sem("gla_ds"), 1)
                pe.wait_ge(sem("gla_sc"), h + 1)
                pe.wait_ge(sem("gla_state"), h + 1)
                if h:
                    pe.wait_ge(sem("gla_o"), h)
                for t in range(TT):
                    o = tp[1][:, t * DV:(t + 1) * DV]
                    pe.matmul(o, sc[:, t, :], vC[:, t, dv], start=True, stop=False)
                    pe.matmul(o, qA[:, h, t, :], state[:, h % 2, 2 * t, :], start=False, stop=False)
                    mm = pe.matmul(o, qB[:, h, t, :], state[:, h % 2, 2 * t + 1, :], start=False, stop=True)
                mm.then_inc(sem("gla_out"), 1)
            s = S["r2"]
            product(s, 0, bhi, blo)
            pe.wait_ge(sem("gla_o"), GLA_H)
            for f in range(4):
                n = b[0]
                b[0] += 1
                if f >= 2:
                    pe.wait_ge(tp_done, n - 1)
                band, bm = const_of("band"), const_of("band_meta")
                for i in range(2):
                    ct = 2 * f + i
                    g, cs = ct // 2, slice(NCH // 2 * CH + ct * P, NCH // 2 * CH + (ct + 1) * P)
                    o = tp[n % 2][:, i * SEQ:(i + 1) * SEQ]
                    pe.matmul(o, nat[:, 0, cs], band[:, g * SEQ:(g + 1) * SEQ], start=True, stop=False)
                    pe.matmul(o[:, P:SEQ], nat[:, 1, cs], band[:, g * SEQ:g * SEQ + P], start=False, stop=False)
                    mm = pe.matmul(o[:, 0:P], puM[0:META, ct * P:(ct + 1) * P], bm[0:META, g * P:(g + 1) * P], start=False, stop=True)
                mm.then_inc(tp_full, 1)
            product(s, 1, bhi, blo)
            pe.wait_ge(tp_done, b[0])
            s = S["pool"]
            for j in range(2):
                u, c = s.u0 + j, s.c0 + j
                pe.wait_ge(evac_act, c - 1)
                pe.wait_ge(evac_dve, c - 1)
                pe.wait_ge(lo_done, u + 1)
                for g in range(2):
                    for t in range(TT):
                        for k in range(2):
                            ct, tok = 4 * j + 2 * g + k, slice(t * P, (t + 1) * P)
                            o = acc[c % 2][t][:, g * PGC:(g + 1) * PGC]
                            cols = slice((2 * g + k) * PGC, (2 * g + k + 1) * PGC)
                            pe.matmul(o, yhi[:, ct, tok], whi[:, u % RING, cols], start=(k == 0), stop=False)
                            pe.matmul(o, yhi[:, ct, tok], wlo[:, u % RING, cols], start=False, stop=False)
                            mm = pe.matmul(o, ylo[:, ct, tok], whi[:, u % RING, cols], start=False, stop=(k == 1))
                mm.then_inc(unit_used, 1)
            evacuated(S["r2"].c0 + 1)
            for f in range(4):
                pair(nat, f)
            evacuated(s.c0 + 1)
            for f in range(4, 8):
                pair(nat, f)
            pe.wait_ge(tp_done, b[0])
            s = S["out2"]
            for j in range(4):
                product(s, j, ahi, alo, mid=(lambda j=j: x_batches(s, [j - 1])) if j else None)
            x_batches(s, [3])
            pe.wait_ge(tp_done, b[0])

            for q in range(DFF // D):
                s = S[f"up{q}"]
                for j in range(4):
                    product(s, j, bhi, blo, mid=turn_chunk(s.c0 + j - 1) if j else None)
                turn_chunk(s.c0 + 3)()
                pe.wait_ge(tp_done, b[0])
                for j in range(4):
                    product(S[f"down{q}"], j, ahi, alo)

        @block.scalar
        def _(act):
            ptr = [0]

            def split_to(target, r=0):
                for u in range(ptr[0], target):
                    kt, cols = shape_of(u)
                    act.wait_ge(raw_full[u % RING], 16 * (u // RING + 1) + r * 16 // RING if isinstance(r, int) else 16 * (u // RING + 1) + r * (16 // RING))
                    if u >= RING:
                        act.wait_ge(unit_used, u - RING + 1 + r)
                    n = kt * cols
                    act.activation(whi[:, u % RING, 0:n], raw[:, u % RING, 0:n], ACT.Copy).then_inc(hi_done, 1)
                ptr[0] = max(ptr[0], target)

            def ended(s, j, r=0):
                act.wait_ge(unit_used, s.u0 + (j + 1) * s.units + r)

            def hi_batch(name, f, dst, gain=None, at=None):
                n, k = BATCH[name][0] + f, f if at is None else at
                act.wait_ge(tp_full, n + 1)
                src = tp[n % 2][:, :].rearrange("p (i t) -> p i t", i=2)
                if gain is None:
                    m = act.activation(dst[:, 2 * k:2 * k + 2, :], src, ACT.Copy)
                else:
                    for i in range(2):
                        m = act.activation(dst[:, 2 * k + i, :], src[:, i, :], ACT.Copy, scale=gcol[:, gain + 2 * k + i:gain + 2 * k + i + 1])
                m.then_inc(tp_hi, 1)

            def squares(norm, j, src, first_wait=None):
                for t in range(TT):
                    n = sq[0]
                    sq[0] += 1
                    if n >= 2:
                        act.wait_ge(sem("squares"), n - 1)
                    act.activation(xb[n % 2][:, 0:CH], src[:, t, j * CH:(j + 1) * CH], ACT.Square,
                                   accum_out=ssq[:, t, j:j + 1]).then_inc(sem("squares"), 1)
            sq = [0]

            def sqrt_of(norm, n=TT, width=D):
                act.wait_ge(sem(f"{norm}_ssum"), 1)
                act.activation(root[:, 0:n], ssum[:, 0:n], ACT.Sqrt, scale=1.0 / width, bias=eps_col).then_inc(sem(f"{norm}_root"), 1)
            eps_col = eps[:, 0:1]

            def scaled(dst, src, norm, t):
                return act.activation(dst, src, ACT.Copy, scale=rs[:, RS[norm], t:t + 1])

            act.wait_ge(sem("eps_set"), 1)
            split_to(3)
            act.wait_ge(tp_done, 1)
            for l in range(2):
                n = BATCH["p"][0] + l
                act.wait_ge(tp_full, n + 1)
                act.activation(phi[:, l], tp[n % 2][:, :].rearrange("p (i t) -> p i t", i=2), ACT.Copy).then_inc(tp_hi, 1)
            for j in range(NCH):
                act.wait_ge(sem(f"x_in{j}"), 16)
                squares("pre0", j, x)
                for f in (2 * j, 2 * j + 1):
                    hi_batch("x0", f, ahi, GC["pre0"])
            sqrt_of("pre0")
            s = S["qk"]
            act.wait_ge(sem("pre0_rs"), 1)

            def qk_chunk(q, i=None):
                r = 0 if i is None else i * (2 * s.units)
                split_to(s.u0 + q * s.units + s.units + 3, r)
                ended(s, q, r)
                scaled(stg[:, q % 2, 0, :], acc[q % 2][0][:, :], "pre0", 0).then_inc(evac_act, 1)

            qk_chunk(0)
            qk_chunk(1)
            with act.Fori(0, 3) as i:
                first = ptr[0]
                for q in (2, 3):
                    qk_chunk(q, i)
            ptr[0] = first + 3 * 2 * s.units
            s = S["v"]
            for j in range(4):
                c = s.c0 + j
                split_to(s.u0 + (j + 1) * s.units + 3)
                ended(s, j)
                scaled(vA[:, 0, j * CH:(j + 1) * CH], acc[c % 2][0][:, :], "pre0", 0).then_inc(evac_act, 1)
            split_to(S["g"].u0 + 4)

            def softplus_terms(h, r=0):
                p = h % 2
                act.wait_ge(sem("attA_logits"), h + 1 + r)
                if h >= 2:
                    act.wait_ge(sem("attA_out"), h - 1 + r)
                    act.wait_ge(sem("attA_sums"), h - 1 + r)
                act.activation(zA[:, p, :], acc[0][p][:, 0:3 * P], ACT.Copy, scale=HD ** -0.5).then_inc(sem("attA_z"), 1)
                act.wait_ge(sem("attA_z"), h + 1 + r)
                act.activation(tA[:, p, :], zA[:, p, :], ACT.Abs).then_inc(sem("attA_t"), 1)
                act.wait_ge(sem("attA_t"), 3 * h + 1 + 3 * r)
                act.activation(tA[:, p, :], tA[:, p, :], ACT.Exp, scale=-1.0).then_inc(sem("attA_t"), 1)
                act.wait_ge(sem("attA_t"), 3 * h + 2 + 3 * r)
                act.activation(tA[:, p, :], tA[:, p, :], ACT.Ln, bias=1.0).then_inc(sem("attA_t"), 1)

            def weights(h, r=0):
                act.wait_ge(sem("attA_d"), h + 1 + r)
                act.activation(zA[:, h % 2, :], zA[:, h % 2, :], ACT.Exp).then_inc(sem("attA_w"), 1)

            softplus_terms(0)
            softplus_terms(1)
            weights(0)
            with act.Fori(0, 7) as i:
                for h in (2, 3):
                    softplus_terms(h, i * 2)
                    weights(h - 1, i * 2)
            weights(HEADS - 1)

            def gate_chunks(s, norm, og):
                for j in range(4):
                    c, p = s.c0 + j, (s.c0 + j) % 2
                    if j:
                        split_to(s.u0 + j * s.units + 7)
                        for f in (2 * j - 2, 2 * j - 1):
                            hi_batch(og, f, bhi)
                    split_to(s.u0 + (j + 1) * s.units + 3)
                    ended(s, j)
                    for t in range(TT):
                        m = act.activation(stg[:, p, t, :], acc[p][t][:, :], ACT.Silu, scale=rs[:, RS[norm], t:t + 1])
                    m.then_inc(evac_act, 1)
                split_to(s.u0 + 4 * s.units + 4)
                for f in (6, 7):
                    hi_batch(og, f, bhi)

            gate_chunks(S["g"], "pre0", "ogA")

            def post(layer, x1, x2, gain, norms):
                s = S[f"out_{'ab'[layer]}"]
                for j in range(4):
                    p = (s.c0 + j) % 2
                    split_to(s.u0 + (j + 1) * s.units + 3)
                    ended(s, j)
                    act.activation(nat[:, 0, j * CH:(j + 1) * CH], acc[p][0][:, :], ACT.Copy).then_inc(evac_act, 1)
                    act.wait_ge(evac_act, s.c0 + j + 1)
                    act.wait_ge(evac_dve, s.c0 + j + 1)
                    squares("post", j, nat)
                sqrt_of(f"post{layer}")
                s = S[f"ple{layer}"]
                for j in range(4):
                    p = (s.c0 + j) % 2
                    split_to(s.u0 + j + 4)
                    ended(s, j)
                    act.activation(pp[:, 0, j * CH:(j + 1) * CH], acc[p][0][:, :], ACT.Copy).then_inc(evac_act, 1)
                    if j:
                        for f in (2 * j - 2, 2 * j - 1):
                            hi_batch(x1, f, ahi)
                for f in (6, 7):
                    hi_batch(x1, f, ahi)
                s = S[f"gate{layer}"]
                for j in range(4):
                    c, p = s.c0 + j, (s.c0 + j) % 2
                    if j:
                        split_to(s.u0 + j * s.units + 7)
                        act.wait_ge(x_done, 8 * layer + 4 + j)
                        squares(norms, j - 1, x)
                        for f in (2 * j - 2, 2 * j - 1):
                            hi_batch(x2, f, bhi, gain)
                    split_to(s.u0 + (j + 1) * s.units + 3)
                    ended(s, j)
                    for t in range(TT):
                        m = act.activation(stg[:, p, t, :], acc[p][t][:, :], ACT.Sigmoid)
                    m.then_inc(evac_act, 1)
                split_to(s.u0 + 4 * s.units + 4)
                for f in (6, 7):
                    hi_batch(x2, f, bhi, gain)
                act.wait_ge(x_done, 8 * layer + 8)
                squares(norms, 3, x)
                sqrt_of(norms)

            post(0, "x1", "x2a", GC["kv"], "pre1")
            act.wait_ge(sem("pre1_rs"), 1)

            def latent(s):
                p = s.c0 % 2
                ended(s, 0)
                scaled(stg[:, p, 0, :], acc[p][0][:, :], "pre1", 0).then_inc(evac_act, 1)

            def latent_squares(s, norm):
                p = s.c0 % 2
                act.wait_ge(evac_act, s.c0 + 1)
                act.wait_ge(evac_dve, s.c0 + 1)
                squares(norm, 0, stg[:, p])
                sqrt_of(norm, width=LORA)

            s = S["ckv"]
            split_to(s.u0 + 8 + 3)
            latent(s)
            latent_squares(s, "kvl")
            for f in range(8):
                hi_batch("x2b", f, ahi, GC["pre1"])
            s = S["krope"]
            split_to(s.u0 + 1 + 3)
            ended(s, 0)
            scaled(kraw[:, 0, 0, :], acc[s.c0 % 2][0][:, 0:ROPE], "pre1", 0)
            scaled(kraw[:, 0, 1, :], acc[s.c0 % 2][0][:, 0:ROPE], "pre1", 0).then_inc(evac_act, 1)
            for f in range(2):
                hi_batch("ckv", f, kvhi, GC["kvl"])
            s = S["cq"]
            split_to(s.u0 + 8 + 3)
            latent(s)
            latent_squares(s, "ql")
            act.wait_ge(sem("kvl_rs"), 1)
            s = S["uk"]
            for j in range(4):
                p = (s.c0 + j) % 2
                split_to(s.u0 + (j + 1) * 2 + 3)
                ended(s, j)
                scaled(stg[:, p, 0, :], acc[p][0][:, :], "kvl", 0).then_inc(evac_act, 1)
                if j == 0:
                    for f in range(2):
                        hi_batch("cq", f, cqhi, GC["ql"])
            s = S["uv"]
            for j in range(4):
                p = (s.c0 + j) % 2
                split_to(s.u0 + (j + 1) * 2 + 3)
                ended(s, j)
                scaled(vB[:, 0, j * CH:(j + 1) * CH], acc[p][0][:, :], "kvl", 0).then_inc(evac_act, 1)

            s = S["uq"]
            act.wait_ge(sem("ql_rs"), 1)

            def q_chunk(j):
                split_to(s.u0 + (j + 1) * 2 + 3)
                ended(s, j)
                if j >= 2:
                    act.wait_ge(sem("q_roped"), j - 1)
                scaled(stg[:, j % 2, 0, 0:2 * QHEAD], acc[0][0][:, 0:2 * QHEAD], "ql", 0).then_inc(evac_act, 1)

            q_chunk(0)
            for c in range(8):
                for i in range(2):
                    h = 2 * c + i
                    act.wait_ge(sem("attB_mx"), h + 1)
                    act.activation(sB[:, i, 0:P], sB[:, i, 0:P], ACT.Exp, bias=mx[:, i, 0:1], accum_out=den[:, c % 2, 2 * i:2 * i + 1])
                    act.activation(sB[:, i, P:3 * P], sB[:, i, P:3 * P], ACT.Exp, bias=mx[:, i, 1:2],
                                   accum_out=den[:, c % 2, 2 * i + 1:2 * i + 2]).then_inc(sem("attB_p"), 1)
                if c < 7:
                    q_chunk(c + 1)
                for i in range(2):
                    act.wait_ge(sem("attB_t"), 2 * c + i + 1)
                    act.activation(pB[:, i, :], acc[1][i][:, 0:3 * P], ACT.Copy).then_inc(sem("attB_pt"), 1)
            gate_chunks(S["gb"], "pre1", "ogB")
            post(1, "x3", "x4", GC["norm1"], "norm1")

            for i in range(4):
                n = sq[0]
                sq[0] += 1
                if i == 0:
                    act.wait_ge(sem("meta_in"), 16)
                    act.wait_ge(sem("norm1_rs"), 1)
                act.wait_ge(sem("squares"), n - 1)
                act.activation(xb[n % 2][0:META, 0:CH], metax[0:META, i * CH:(i + 1) * CH], ACT.Square,
                               accum_out=ssq[0:META, 0, i:i + 1]).then_inc(sem("squares"), 1)
            act.wait_ge(sem("metan_ssum"), 1)
            act.activation(root[0:META, 0:1], ssum[0:META, 0:1], ACT.Sqrt, scale=1.0 / D, bias=eps[0:META, 0:1]).then_inc(sem("metan_root"), 1)
            act.wait_ge(sem("meta_zero"), 1)
            act.wait_ge(sem("meta_scaled"), 1)
            act.activation(metaT[:, :, 0:META], stg[:, 1, 0, 0:KT * META].rearrange("p (k m) -> p k m", m=META), ACT.Copy).then_inc(tp_hi, 1)

            def plain(name, j, dst, norm="norm1"):
                s = S[name]
                c = s.c0 + j
                split_to(s.u0 + (j + 1) * s.units + 3)
                ended(s, j)
                scaled(dst, acc[c % 2][0][:, 0:s.cols], norm, 0).then_inc(evac_act, 1)

            act.wait_ge(sem("glr_zero"), 1)
            plain("glr", 0, glr[:, 0, 0:GRANK])
            plain("k2", 0, kend[:, 0, :])
            plain("q2", 0, stg[:, 0, 0, :])
            for t in range(TT + 1):
                n = P if t < TT else META
                src = (tp[0], tp[1], xb[1])[t][0:n, :]
                dst = stg[:, 1, t, :] if t < TT else msc[0:META, :]
                act.wait_ge(sem("graw"), t + 1)
                act.activation(dst, src, ACT.Abs).then_inc(sem("lg"), 1)
                act.wait_ge(sem("lg"), 3 * t + 1)
                act.activation(dst, dst, ACT.Exp, scale=-1.0).then_inc(sem("lg"), 1)
                act.wait_ge(sem("lg"), 3 * t + 2)
                act.activation(dst, dst, ACT.Ln, bias=1.0).then_inc(sem("lg"), 1)
            plain("v2", 0, vC[:, 0, 0:CH])
            for t in range(TT):
                act.wait_ge(sem("G"), t + 1)
                act.wait_ge(sem("logg"), t + 1)
                act.activation(stg[:, 1, t, :], tp[t][:, :], ACT.Exp, scale=1.0 / TAU).then_inc(sem("eG"), 1)
                act.activation(nat[:, t, 0:CH], tp[t][:, :], ACT.Exp, scale=-1.0 / TAU).then_inc(sem("eG"), 1)
            for t in range(TT):
                act.wait_ge(sem("G"), 3 + t)
                act.activation(nat[:, t, CH:2 * CH], tp[t][:, :], ACT.Exp, scale=1.0 / TAU).then_inc(sem("eG"), 1)
            act.wait_ge(sem("G"), 5)
            act.activation(oneM[0:META, :], xb[0][0:META, :], ACT.Exp, scale=1.0 / TAU).then_inc(sem("eG"), 1)
            plain("v2", 1, vC[:, 0, CH:2 * CH])
            act.wait_ge(sem("G"), 6)
            act.activation(decay[:, :, :], xb[0][:, 0:4 * GLA_H].rearrange("p (h n) -> p h n", h=GLA_H), ACT.Exp, scale=1.0 / TAU).then_inc(sem("decay"), 1)
            for j in range(2):
                plain("pu", j, nat[:, 0, (2 + j) * CH:(3 + j) * CH])
            for h in range(GLA_H):
                act.wait_ge(sem("gla_o"), h + 1)
                for t in range(TT):
                    n = sq[0]
                    sq[0] += 1
                    act.wait_ge(sem("squares"), n)
                    act.activation(stg[:, 0, 0, 0:DV], nat[:, t, h * DV:(h + 1) * DV], ACT.Square,
                                   accum_out=ssum[:, t * GLA_H + h:t * GLA_H + h + 1]).then_inc(sem("squares"), 1)
            act.wait_ge(sem("squares"), sq[0])
            act.activation(root[:, :], ssum[:, :], ACT.Sqrt, scale=1.0 / DV, bias=eps_col).then_inc(sem("gla_root"), 1)
            s = S["r2"]
            for j in range(2):
                c, p = s.c0 + j, (s.c0 + j) % 2
                if j == 1:
                    split_to(s.u0 + s.units + 4)
                    for f in range(4):
                        hi_batch("pool", f, yhi)
                split_to(s.u0 + (j + 1) * s.units + 3)
                ended(s, j)
                for t in range(TT):
                    m = act.activation(stg[:, p, t, :], acc[p][t][:, :], ACT.Silu, scale=rs[:, RS["norm1"], t:t + 1])
                m.then_inc(evac_act, 1)
            s = S["pool"]
            for j in range(2):
                c = s.c0 + j
                split_to(s.u0 + j + 1 + 3)
                ended(s, j)
                act.activation(nat[:, 0, (2 + j) * CH:(3 + j) * CH], acc[c % 2][0][:, :], ACT.Copy).then_inc(evac_act, 1)
            for f in range(8):
                n = BATCH["mixed"][0] + f
                act.wait_ge(tp_full, n + 1)
                src = tp[n % 2][:, :].rearrange("p (i t) -> p i t", i=2)
                for i in range(2):
                    g = GC["gla"] + i if f < 4 else GC["pool"] + 2 * (f - 4) + i
                    m = act.activation(ahi[:, 2 * f + i, :], src[:, i, :], ACT.Copy, scale=gcol[:, g:g + 1])
                m.then_inc(tp_hi, 1)

            def added(s, j):
                c, p = s.c0 + j, (s.c0 + j) % 2
                split_to(min(s.u0 + (j + 1) * s.units + 3, units))
                ended(s, j)
                act.activation(stg[:, p, 0, :], acc[p][0][:, :], ACT.Copy).then_inc(evac_act, 1)

            s = S["out2"]
            for j in range(4):
                if j:
                    split_to(s.u0 + j * s.units + 7)
                    act.wait_ge(evac_dve, s.c0 + j)
                    squares("norm2", j - 1, x)
                    for f in (2 * j - 2, 2 * j - 1):
                        hi_batch("x5", f, bhi, GC["norm2"])
                added(s, j)
            split_to(s.u0 + 4 * s.units + 4)
            for f in (6, 7):
                hi_batch("x5", f, bhi, GC["norm2"])
            act.wait_ge(evac_dve, s.c0 + 4)
            squares("norm2", 3, x)
            sqrt_of("norm2")
            act.wait_ge(sem("norm2_rs"), 1)
            for q in range(DFF // D):
                s = S[f"up{q}"]
                for j in range(4):
                    p = (s.c0 + j) % 2
                    if j:
                        split_to(s.u0 + j * s.units + 7)
                        for f in (2 * j - 2, 2 * j - 1):
                            hi_batch(f"mlp{q}", f, ahi)
                    split_to(s.u0 + (j + 1) * s.units + 3)
                    ended(s, j)
                    n = 4 * q + j
                    act.activation(stg[:, p, 0, :], acc[p][0][:, :], ACT.Relu, scale=rs[:, RS["norm2"], 0:1]).then_inc(sem("relu"), 1)
                    act.wait_ge(sem("relu"), n + 1)
                    act.activation(stg[:, p, 0, :], stg[:, p, 0, :], ACT.Square).then_inc(evac_act, 1)
                split_to(s.u0 + 4 * s.units + 4)
                for f in (6, 7):
                    hi_batch(f"mlp{q}", f, ahi)
                for j in range(4):
                    added(S[f"down{q}"], j)
                    if q == DFF // D - 1:
                        act.wait_ge(evac_dve, S[f"down{q}"].c0 + j + 1)
                        squares("final", j, x)
            sqrt_of("final")

        @block.vector
        def _(dve):
            ptr = [0]
            def split_to(target, r=0):
                for u in range(ptr[0], target):
                    kt, cols = shape_of(u)
                    n = kt * cols
                    dve.wait_ge(hi_done, u + 1 + r)
                    dve.tensor_tensor(wlo[:, u % RING, 0:n], raw[:, u % RING, 0:n], whi[:, u % RING, 0:n].bitcast(F32),
                                      ALU.subtract).then_inc(lo_done, 1)
                ptr[0] = max(ptr[0], target)

            def ended(s, j, r=0):
                dve.wait_ge(unit_used, s.u0 + (j + 1) * s.units + r)

            def bank(n):
                return tp[n % 2][:, :].rearrange("p (i t) -> p i t", i=2)

            def lo_batch(name, f, hi, lo, gain=None):
                n, k = BATCH[name][0] + f, BATCH[name][1] + f
                dve.wait_ge(tp_hi, k + 1)
                tiles = slice(2 * f, 2 * f + 2)
                if gain is None:
                    m = dve.tensor_tensor(lo[:, tiles, :], bank(n), hi[:, tiles, :].bitcast(F32), ALU.subtract)
                else:
                    for i in range(2):
                        g = gain(f, i) if callable(gain) else gain + 2 * f + i
                        m = dve.scalar_tensor_tensor(out=lo[:, 2 * f + i, :], in0=bank(n)[:, i, :], scalar=gcol[:, g:g + 1],
                                                     in1=hi[:, 2 * f + i, :].bitcast(F32), op0=ALU.mult, op1=ALU.subtract)
                m.then_inc(tp_done, 1)

            def copy_batch(name, f, dst, r=0):
                n = BATCH[name][0] + f
                dve.wait_ge(tp_full, n + 1 + r)
                dve.tensor_copy(dst, bank(n)).then_inc(tp_done, 1)

            def scaled(dst, src, norm, t):
                return dve.tensor_scalar(dst, src, rs[:, RS[norm], t:t + 1], None, ALU.mult)

            def sum_squares(norm, squares_done, quarters=4):
                dve.wait_ge(sem("squares"), squares_done)
                dve.tensor_reduce(ssum[:, 0:TT], ssq[:, :, 0:quarters], AX, ALU.add).then_inc(sem(f"{norm}_ssum"), 1)

            def inverse_root(norm):
                dve.wait_ge(sem(f"{norm}_root"), 1)
                dve.reciprocal(rs[:, RS[norm.rstrip("01") if norm.startswith("post") else norm], 0:TT], root[:, 0:TT]).then_inc(sem(f"{norm}_rs"), 1)

            sq = [0]

            def norm_of(norm, n=8, quarters=4):
                sq[0] += n
                sum_squares(norm, sq[0], quarters)
                inverse_root(norm)

            dve.memset(eps[:, :], EPS).then_inc(sem("eps_set"), 1)
            n = BATCH["gcol"][0]
            dve.wait_ge(tp_full, n + 1)
            dve.tensor_copy(gcol[:, 0:98], tp[n % 2][:, 0:98]).then_inc(tp_done, 1)
            dve.wait_ge(tp_done, 1)
            for l in range(2):
                n = BATCH["p"][0] + l
                dve.wait_ge(tp_hi, BATCH["p"][1] + l + 1)
                dve.tensor_tensor(plo[:, l], bank(n), phi[:, l].bitcast(F32), ALU.subtract).then_inc(tp_done, 1)
            for f in range(8):
                if f in (3, 5, 7):
                    split_to((f - 1) // 2)
                lo_batch("x0", f, ahi, alo, GC["pre0"])
            norm_of("pre0")
            dve.wait_ge(sem("pre0_rs"), 1)

            s = S["qk"]

            def qk_chunk(q, i=None):
                r = 0 if i is None else i * (2 * s.units)
                rb = 0 if i is None else i * 4
                if q:
                    split_to(s.u0 + q * s.units + 7, r)
                    for f in (2 * q - 2, 2 * q - 1):
                        at = 2 * f if i is None else 2 * f + i * 8
                        copy_batch("qk", f, qkT[:, bass.ds(at, 2), :], rb)
                split_to(s.u0 + (q + 1) * s.units + 3, r)
                ended(s, q, r)
                scaled(stg[:, q % 2, 1, :], acc[q % 2][1][:, :], "pre0", 1).then_inc(evac_dve, 1)

            qk_chunk(0)
            qk_chunk(1)
            with dve.Fori(0, 3) as i:
                first = ptr[0]
                for q in (2, 3):
                    qk_chunk(q, i)
            ptr[0] = first + 3 * 2 * s.units
            s = S["v"]
            for j in range(4):
                c = s.c0 + j
                if j == 0:
                    split_to(s.u0 + 7)
                    for f in (14, 15):
                        copy_batch("qk", f, qkT[:, 2 * f:2 * f + 2, :])
                split_to(s.u0 + (j + 1) * s.units + 3)
                ended(s, j)
                scaled(vA[:, 1, j * CH:(j + 1) * CH], acc[c % 2][1][:, :], "pre0", 1).then_inc(evac_dve, 1)
            split_to(S["g"].u0 + 4)

            def diagonal(a, p):
                return a[:, p, :].rearrange("p (b q) -> p b q", b=3)[:, 0:3:2, :]

            def blocks(name):
                return const_of(name)[:, None, :].to_broadcast((P, 2, P))

            def softplus(h, r=0):
                p = h % 2
                dve.wait_ge(sem("attA_t"), 3 * (h + 1) + 3 * r)
                dve.scalar_tensor_tensor(out=tA[:, p, :], in0=zA[:, p, :], scalar=0.0, in1=tA[:, p, :], op0=ALU.max,
                                         op1=ALU.add).then_inc(sem("attA_m"), 1)
                dve.wait_ge(sem("attA_m"), h + 1 + r)
                dve.tensor_tensor(diagonal(tA, p), diagonal(tA, p), blocks("strict"), ALU.mult).then_inc(sem("attA_sp"), 1)
                dve.tensor_tensor(diagonal(zA, p), diagonal(zA, p), blocks("strict_neg"), ALU.add).then_inc(sem("attA_n"), 1)

            def less_sums(h, r=0):
                p = h % 2
                dve.wait_ge(sem("attA_sums"), h + 1 + r)
                dve.wait_ge(sem("attA_n"), h + 1 + r)
                dve.tensor_tensor(zA[:, p, :], zA[:, p, :], acc[1][p][:, 0:3 * P], ALU.subtract).then_inc(sem("attA_d"), 1)

            def head_out(h, r=0):
                dve.wait_ge(sem("attA_out"), h + 1 + r)
                at = h * HD if isinstance(r, int) else r * HD + h * HD
                dve.tensor_copy(nat[:, :, bass.ds(at, HD)], xb[h % 2][:, 0:SEQ].rearrange("p (t d) -> p t d", t=TT)).then_inc(sem("attA_o"), 1)

            softplus(0)
            softplus(1)
            less_sums(0)
            with dve.Fori(0, 7) as i:
                for h in (2, 3):
                    softplus(h, i * 2)
                    less_sums(h - 1, i * 2)
                    head_out(h - 2, i * 2)
            less_sums(HEADS - 1)
            head_out(HEADS - 2)
            head_out(HEADS - 1)

            def gate_chunks(s, og):
                for j in range(4):
                    c, p = s.c0 + j, (s.c0 + j) % 2
                    if j:
                        split_to(s.u0 + j * s.units + 7)
                        for f in (2 * j - 2, 2 * j - 1):
                            lo_batch(og, f, bhi, blo)
                    split_to(s.u0 + (j + 1) * s.units + 3)
                    dve.wait_ge(evac_act, c + 1)
                    dve.wait_ge(sem("attA_o" if og == "ogA" else "attB_o"), HEADS if og == "ogA" else HEADS // 2)
                    cols = slice(j * CH, (j + 1) * CH)
                    dve.tensor_tensor(nat[:, :, cols], nat[:, :, cols], stg[:, p, :, :], ALU.mult).then_inc(evac_dve, 1)
                split_to(s.u0 + 4 * s.units + 4)
                for f in (6, 7):
                    lo_batch(og, f, bhi, blo)

            gate_chunks(S["g"], "ogA")

            def post(layer, x1, x2, gain, norms):
                s = S[f"out_{'ab'[layer]}"]
                for j in range(4):
                    p = (s.c0 + j) % 2
                    split_to(s.u0 + (j + 1) * s.units + 3)
                    ended(s, j)
                    dve.tensor_copy(nat[:, 1, j * CH:(j + 1) * CH], acc[p][1][:, :]).then_inc(evac_dve, 1)
                norm_of(f"post{layer}")
                dve.wait_ge(sem(f"post{layer}_rs"), 1)
                dve.wait_ge(sem(f"post_in{layer}"), 16)
                s = S[f"ple{layer}"]
                for j in range(4):
                    p = (s.c0 + j) % 2
                    split_to(s.u0 + j + 4)
                    ended(s, j)
                    dve.tensor_copy(pp[:, 1, j * CH:(j + 1) * CH], acc[p][1][:, :]).then_inc(evac_dve, 1)
                    for t in range(TT):
                        y = nat[:, t, j * CH:(j + 1) * CH]
                        dve.scalar_tensor_tensor(out=y, in0=y, scalar=rs[:, RS["post"], t:t + 1], in1=gains[:, j * CH:(j + 1) * CH],
                                                 op0=ALU.mult, op1=ALU.mult).then_inc(sem(f"post{layer}_y"), 1)
                    for t in range(TT):
                        xq = x[:, t, j * CH:(j + 1) * CH]
                        dve.wait_ge(sem(f"post{layer}_y"), TT * j + t + 1)
                        m = dve.tensor_tensor(xq, xq, nat[:, t, j * CH:(j + 1) * CH], ALU.add)
                    m.then_inc(x_done, 1)
                    if j:
                        for f in (2 * j - 2, 2 * j - 1):
                            lo_batch(x1, f, ahi, alo)
                for f in (6, 7):
                    lo_batch(x1, f, ahi, alo)
                s = S[f"gate{layer}"]
                for j in range(4):
                    c, p = s.c0 + j, (s.c0 + j) % 2
                    if j:
                        split_to(s.u0 + j * s.units + 7)
                        for f in (2 * j - 2, 2 * j - 1):
                            lo_batch(x2, f, bhi, blo, gain)
                    split_to(s.u0 + (j + 1) * s.units + 3)
                    dve.wait_ge(evac_act, c + 1)
                    cols = slice(j * CH, (j + 1) * CH)
                    dve.tensor_tensor(pp[:, :, cols], pp[:, :, cols], stg[:, p, :, :], ALU.mult).then_inc(evac_dve, 1)
                    dve.wait_ge(evac_dve, c + 1)
                    dve.tensor_tensor(x[:, :, cols], x[:, :, cols], pp[:, :, cols], ALU.add).then_inc(x_done, 1)
                split_to(s.u0 + 4 * s.units + 4)
                for f in (6, 7):
                    lo_batch(x2, f, bhi, blo, gain)
                norm_of(norms)

            post(0, "x1", "x2a", GC["kv"], "pre1")
            dve.wait_ge(sem("pre1_rs"), 1)

            def latent(s, norm):
                p = s.c0 % 2
                ended(s, 0)
                scaled(stg[:, p, 1, :], acc[p][1][:, :], "pre1", 1).then_inc(evac_dve, 1)
                norm_of(norm, 2, 1)

            s = S["ckv"]
            split_to(s.u0 + 8 + 3)
            latent(s, "kvl")
            for f in range(8):
                lo_batch("x2b", f, ahi, alo, GC["pre1"])
            s = S["krope"]
            split_to(s.u0 + 1 + 3)
            ended(s, 0)
            scaled(kraw[:, 1, 0, :], acc[s.c0 % 2][1][:, 0:ROPE], "pre1", 1)
            scaled(kraw[:, 1, 1, :], acc[s.c0 % 2][1][:, 0:ROPE], "pre1", 1).then_inc(evac_dve, 1)
            for f in range(2):
                lo_batch("ckv", f, kvhi, kvlo, GC["kvl"])
            s = S["cq"]
            split_to(s.u0 + 8 + 3)
            latent(s, "ql")
            n = BATCH["kr"][0]
            dve.wait_ge(tp_full, n + 1)
            dve.tensor_copy(krT[:, :], tp[n % 2][:, 0:SEQ]).then_inc(tp_done, 1)
            s = S["uk"]
            for j in range(4):
                p = (s.c0 + j) % 2
                split_to(s.u0 + (j + 1) * 2 + 3)
                ended(s, j)
                scaled(stg[:, p, 1, :], acc[p][1][:, :], "kvl", 1).then_inc(evac_dve, 1)
                for f in range(2):
                    if j == 0:
                        lo_batch("cq", f, cqhi, cqlo, GC["ql"])
                    else:
                        f += 2 * j - 2
                        copy_batch("uk", f, knT[:, 2 * f:2 * f + 2, :])
            s = S["uv"]
            for j in range(4):
                p = (s.c0 + j) % 2
                split_to(s.u0 + (j + 1) * 2 + 3)
                ended(s, j)
                scaled(vB[:, 1, j * CH:(j + 1) * CH], acc[p][1][:, :], "kvl", 1).then_inc(evac_dve, 1)
                if j == 0:
                    for f in (6, 7):
                        copy_batch("uk", f, knT[:, 2 * f:2 * f + 2, :])

            s = S["uq"]

            def q_chunk(j):
                split_to(s.u0 + (j + 1) * 2 + 3)
                ended(s, j)
                if j >= 2:
                    dve.wait_ge(sem("q_roped"), j - 1)
                scaled(stg[:, j % 2, 1, 0:2 * QHEAD], acc[0][1][:, 0:2 * QHEAD], "ql", 1).then_inc(evac_dve, 1)
                if j >= 2:
                    dve.wait_ge(sem("attB_s"), 2 * (j - 1))
                copy_batch("uq", 2 * j, qn[:, j % 2])
                n = BATCH["uq"][0] + 2 * j + 1
                dve.wait_ge(tp_full, n + 1)
                dve.tensor_copy(qr[:, j % 2, :], tp[n % 2][:, 0:SEQ]).then_inc(tp_done, 1)

            q_chunk(0)
            for c in range(8):
                for i in range(2):
                    h = 2 * c + i
                    dve.wait_ge(sem("attB_s"), 2 * c + i + 1)
                    if h >= 2:
                        dve.wait_ge(sem("attB_t"), h - 1)
                    dve.scalar_tensor_tensor(out=sB[:, i, :], in0=xb[i][:, 0:3 * P], scalar=QHEAD ** -0.5, in1=const_of("chunk_neg"),
                                             op0=ALU.mult, op1=ALU.add).then_inc(sem("attB_m"), 1)
                    dve.wait_ge(sem("attB_m"), h + 1)
                    dve.tensor_reduce(mx[:, i, 0:1], sB[:, i, 0:P], AX, ALU.max, negate=True)
                    dve.tensor_reduce(mx[:, i, 1:2], sB[:, i, P:3 * P], AX, ALU.max, negate=True).then_inc(sem("attB_mx"), 1)
                if c < 7:
                    q_chunk(c + 1)
                dve.wait_ge(sem("attB_out"), c + 1)
                dve.reciprocal(rden[:, c % 2, :], den[:, c % 2, :]).then_inc(sem("attB_r"), 1)
                dve.wait_ge(sem("attB_r"), c + 1)
                dve.tensor_tensor(nat[:, :, c * 2 * HD:(c + 1) * 2 * HD].rearrange("p t (i d) -> p i t d", i=2),
                                  acc[1][0][:, :].rearrange("p (i t d) -> p i t d", i=2, t=TT),
                                  rden[:, c % 2, :].rearrange("p (i t) -> p i t", i=2)[:, :, :, None].to_broadcast((P, 2, TT, HD)),
                                  ALU.mult).then_inc(sem("attB_o"), 1)
            gate_chunks(S["gb"], "ogB")
            post(1, "x3", "x4", GC["norm1"], "norm1")

            sq[0] += 4
            dve.wait_ge(sem("squares"), sq[0])
            dve.tensor_reduce(ssum[0:META, 0:1], ssq[0:META, 0, :], AX, ALU.add).then_inc(sem("metan_ssum"), 1)
            dve.wait_ge(sem("metan_root"), 1)
            rsM = rs[0:META, 7, 0:1]
            dve.reciprocal(rsM, root[0:META, 0:1]).then_inc(sem("metan_rs"), 1)
            n, k = BATCH["meta"]
            dve.wait_ge(tp_full, n + 1)
            scaledM = stg[:, 1, 0, 0:KT * META].rearrange("p (k m) -> p k m", m=META)
            dve.tensor_tensor(scaledM, tp[n % 2][:, 0:KT * META].rearrange("p (k m) -> p k m", m=META),
                              gcol[:, GC["norm1"]:GC["norm1"] + KT][:, :, None].to_broadcast((P, KT, META)), ALU.mult).then_inc(sem("meta_scaled"), 1)
            dve.wait_ge(tp_hi, k + 1)
            dve.tensor_tensor(metaT[:, :, 32:32 + META], scaledM, metaT[:, :, 0:META].bitcast(F32), ALU.subtract).then_inc(tp_done, 1)
            dve.wait_ge(sem("metan_rs"), 1)
            dve.wait_ge(sem("norm1_rs"), 1)
            metas = [0]

            def plain(name, j, dst, meta=None):
                s = S[name]
                c = s.c0 + j
                split_to(s.u0 + (j + 1) * s.units + 3)
                ended(s, j)
                m = scaled(dst, acc[c % 2][1][:, 0:s.cols], "norm1", 1)
                if meta is not None:
                    k = metas[0]
                    metas[0] += 1
                    tmp = msc[0:META, 0:s.cols]
                    if k:
                        dve.wait_ge(evac_dve, c)
                    dve.tensor_copy(tmp, xb[c % 2][32:32 + META, 0:s.cols]).then_inc(sem("meta_step"), 1)
                    dve.wait_ge(sem("meta_step"), 2 * k + 1)
                    dve.tensor_tensor(tmp, xb[c % 2][0:META, 0:s.cols], tmp, ALU.add).then_inc(sem("meta_step"), 1)
                    dve.wait_ge(sem("meta_step"), 2 * k + 2)
                    m = dve.tensor_scalar(meta, tmp, rsM, None, ALU.mult)
                m.then_inc(evac_dve, 1)

            dve.wait_ge(sem("glr_zero"), 1)
            plain("glr", 0, glr[:, 1, 0:GRANK], glrM[0:META, 0:GRANK])
            plain("k2", 0, kend[:, 1, :], kendM[0:META, :])
            n = BATCH["glr"][0]
            dve.wait_ge(tp_full, n + 1)
            dve.tensor_copy(glrT[:, :], tp[n % 2][:, 0:SEQ + META]).then_inc(tp_done, 1)
            plain("q2", 0, stg[:, 0, 1, :])
            for t in range(TT + 1):
                n = P if t < TT else META
                src = (tp[0], tp[1], xb[1])[t][0:n, :]
                soft = stg[:, 1, t, :] if t < TT else msc[0:META, :]
                dst = logg[:, t, :] if t < TT else loggM[0:META, :]
                dve.wait_ge(sem("lg"), 3 * t + 3)
                dve.scalar_tensor_tensor(out=dst, in0=src, scalar=0.0, in1=soft, op0=ALU.min, op1=ALU.subtract).then_inc(sem("logg"), 1)
            plain("v2", 0, vC[:, 1, 0:CH], vM[0:META, 0:CH])
            dve.wait_ge(sem("eG"), 4)
            dve.wait_ge(evac_act, S["q2"].c0 + 1)
            dve.tensor_tensor(nat[:, :, 0:CH], nat[:, :, 0:CH], kend[:, :, :], ALU.mult).then_inc(sem("kinv"), 1)
            dve.scalar_tensor_tensor(out=stg[:, 0, :, :], in0=stg[:, 0, :, :], scalar=DK ** -0.5, in1=stg[:, 1, :, :],
                                     op0=ALU.mult, op1=ALU.mult).then_inc(sem("qdec"), 1)
            dve.wait_ge(sem("eG"), 7)
            dve.tensor_tensor(kend[:, :, :], kend[:, :, :], nat[:, :, CH:2 * CH], ALU.mult).then_inc(sem("kend"), 1)
            dve.tensor_tensor(kendM[0:META, :], kendM[0:META, :], oneM[0:META, :], ALU.mult).then_inc(sem("kend"), 1)
            plain("v2", 1, vC[:, 1, CH:2 * CH], vM[0:META, CH:2 * CH])
            for f in range(2):
                copy_batch("kinv", f, kTc[:, 2 * f:2 * f + 2, :])
            dve.wait_ge(sem("q_zero"), 1)
            for f in range(2):
                n = BATCH["qdec"][0] + f
                dve.wait_ge(tp_full, n + 1)
                src = tp[n % 2][:, :].rearrange("p (i t q) -> p i t q", i=2, t=TT)
                dve.tensor_copy(qA[:, 2 * f:2 * f + 2, :, 0:64], src[:, :, :, 0:64])
                dve.tensor_copy(qB[:, 2 * f:2 * f + 2, :, 64:P], src[:, :, :, 64:P]).then_inc(tp_done, 1)
            for j in range(2):
                plain("pu", j, nat[:, 1, (2 + j) * CH:(3 + j) * CH], puM[0:META, j * CH:(j + 1) * CH])

            dve.wait_ge(sem("decay"), 1)
            for h in range(GLA_H):
                dve.wait_ge(sem("gla_scores"), h + 1)
                if h:
                    dve.wait_ge(sem("gla_out"), h)
                dve.tensor_scalar(sc[:, :, :], tp[0][:, 0:SEQ].rearrange("p (t c) -> p t c", t=TT), 3e38, -3e38, ALU.min, ALU.max).then_inc(sem("gla_clip"), 1)
                dve.wait_ge(sem("gla_clip"), h + 1)
                dve.tensor_tensor(sc[:, :, :], sc[:, :, :], const_of("gla_causal")[:, None, :].to_broadcast((P, TT, P)), ALU.mult).then_inc(sem("gla_sc"), 1)
                dve.wait_ge(sem("gla_ds"), h + 1)
                st = state[:, h % 2]
                dve.tensor_copy(st[:, 0, :], xb[1][:, DV:2 * DV]).then_inc(sem("gla_step"), 1)
                for n, (src, half) in enumerate(((xb[0], 0), (xb[1], 0), (xb[0], 1))):
                    dve.wait_ge(sem("gla_step"), 3 * h + n + 1)
                    m = dve.scalar_tensor_tensor(out=st[:, n + 1, :], in0=st[:, n, :], scalar=decay[:, h, n:n + 1],
                                                 in1=src[:, half * DV:(half + 1) * DV], op0=ALU.mult, op1=ALU.add)
                    m.then_inc(sem("gla_step") if n < 2 else sem("gla_state"), 1)
                dve.wait_ge(sem("gla_out"), h + 1)
                dve.tensor_copy(nat[:, :, h * DV:(h + 1) * DV], tp[1][:, :].rearrange("p (t d) -> p t d", t=TT)).then_inc(sem("gla_o"), 1)
            sq[0] += 2 * GLA_H
            dve.wait_ge(sem("gla_root"), 1)
            dve.reciprocal(rs[:, 6, :], root[:, :]).then_inc(sem("gla_rs"), 1)
            dve.wait_ge(sem("gla_rs"), 1)
            s = S["r2"]
            for j in range(2):
                c, p = s.c0 + j, (s.c0 + j) % 2
                if j == 1:
                    split_to(s.u0 + s.units + 4)
                    for f in range(4):
                        lo_batch("pool", f, yhi, ylo)
                split_to(s.u0 + (j + 1) * s.units + 3)
                dve.wait_ge(evac_act, c + 1)
                for t in range(TT):
                    for i in range(2):
                        h = 2 * j + i
                        o = nat[:, t, h * DV:(h + 1) * DV]
                        dve.wait_ge(sem("squares"), sq[0])
                        m = dve.scalar_tensor_tensor(out=o, in0=o, scalar=rs[:, 6, t * GLA_H + h:t * GLA_H + h + 1],
                                                     in1=stg[:, p, t, i * DV:(i + 1) * DV], op0=ALU.mult, op1=ALU.mult)
                m.then_inc(evac_dve, 1)
            s = S["pool"]
            for j in range(2):
                c = s.c0 + j
                split_to(s.u0 + j + 1 + 3)
                ended(s, j)
                dve.tensor_copy(nat[:, 1, (2 + j) * CH:(3 + j) * CH], acc[c % 2][1][:, :]).then_inc(evac_dve, 1)
            for f in range(8):
                lo_batch("mixed", f, ahi, alo, lambda f, i: GC["gla"] + i if f < 4 else GC["pool"] + 2 * (f - 4) + i)

            def added(s, j):
                c, p = s.c0 + j, (s.c0 + j) % 2
                split_to(min(s.u0 + (j + 1) * s.units + 3, units))
                dve.wait_ge(evac_act, c + 1)
                x0, x1 = (x[:, t, j * CH:(j + 1) * CH] for t in range(TT))
                dve.tensor_tensor(x0, x0, stg[:, p, 0, :], ALU.add)
                dve.tensor_tensor(x1, x1, acc[p][1][:, :], ALU.add).then_inc(evac_dve, 1)

            s = S["out2"]
            for j in range(4):
                if j:
                    split_to(s.u0 + j * s.units + 7)
                    for f in (2 * j - 2, 2 * j - 1):
                        lo_batch("x5", f, bhi, blo, GC["norm2"])
                added(s, j)
            split_to(s.u0 + 4 * s.units + 4)
            for f in (6, 7):
                lo_batch("x5", f, bhi, blo, GC["norm2"])
            norm_of("norm2")
            dve.wait_ge(sem("norm2_rs"), 1)
            for q in range(DFF // D):
                s = S[f"up{q}"]
                for j in range(4):
                    p = (s.c0 + j) % 2
                    if j:
                        split_to(s.u0 + j * s.units + 7)
                        for f in (2 * j - 2, 2 * j - 1):
                            lo_batch(f"mlp{q}", f, ahi, alo)
                    split_to(s.u0 + (j + 1) * s.units + 3)
                    ended(s, j)
                    n = 4 * q + j
                    dve.tensor_scalar(stg[:, p, 1, :], acc[p][1][:, :], rs[:, RS["norm2"], 1:2], 0.0, ALU.mult, ALU.max).then_inc(sem("relu_dve"), 1)
                    dve.wait_ge(sem("relu_dve"), n + 1)
                    dve.tensor_tensor(stg[:, p, 1, :], stg[:, p, 1, :], stg[:, p, 1, :], ALU.mult).then_inc(evac_dve, 1)
                split_to(s.u0 + 4 * s.units + 4)
                for f in (6, 7):
                    lo_batch(f"mlp{q}", f, ahi, alo)
                for j in range(4):
                    added(S[f"down{q}"], j)
            norm_of("final")
            dve.wait_ge(sem("final_rs"), 1)
            dve.wait_ge(sem("final_in"), 16)
            for j in range(NCH):
                for t in range(TT):
                    dve.scalar_tensor_tensor(out=nat[:, t, j * CH:(j + 1) * CH], in0=x[:, t, j * CH:(j + 1) * CH],
                                             scalar=rs[:, RS["final"], t:t + 1], in1=gains[:, j * CH:(j + 1) * CH],
                                             op0=ALU.mult, op1=ALU.mult).then_inc(sem("final_y"), 1)

        @block.gpsimd
        def _(pool):
            step = [0]
            cos = const_of("cos").rearrange("p (t i c) -> p t i c", t=TT, i=2)
            sin = const_of("sin").rearrange("p (t i c) -> p t i c", t=TT, i=2)
            dst = roped[:, :, :].rearrange("p t (i c) -> p t i c", i=2)
            half = ROPE // 2

            def op(out_, a, b_, f):
                pool.tensor_tensor(out_, a, b_, f).then_inc(sem("rope_step"), 1)
                step[0] += 1
                pool.wait_ge(sem("rope_step"), step[0])

            def rotate(a, b_):
                op(dst[:, :, :, 0:half], a, cos, ALU.mult)
                op(turn[:, :, :, :], b_, sin, ALU.mult)
                op(dst[:, :, :, 0:half], dst[:, :, :, 0:half], turn[:, :, :, :], ALU.subtract)
                op(dst[:, :, :, half:ROPE], a, sin, ALU.mult)
                op(turn[:, :, :, :], b_, cos, ALU.mult)
                return pool.tensor_tensor(dst[:, :, :, half:ROPE], dst[:, :, :, half:ROPE], turn[:, :, :, :], ALU.add)

            pool.wait_ge(sem("tab_in"), 16)
            s = S["krope"]
            pool.wait_ge(evac_act, s.c0 + 1)
            pool.wait_ge(evac_dve, s.c0 + 1)
            rotate(kraw[:, :, :, 0:half], kraw[:, :, :, half:ROPE]).then_inc(sem("k_roped"), 1)
            s = S["uq"]
            for j in range(s.chunks):
                pool.wait_ge(evac_act, s.c0 + j + 1)
                pool.wait_ge(evac_dve, s.c0 + j + 1)
                pool.wait_ge(sem("q_roped") if j else sem("k_roped"), max(j, 1))
                pool.wait_ge(tp_full, BATCH["uq"][0] + 2 * j if j else BATCH["kr"][0] + 1)
                q = stg[:, j % 2, :, 0:2 * QHEAD].rearrange("p t (i c) -> p t i c", i=2)
                rotate(q[:, :, :, HD:HD + half], q[:, :, :, HD + half:QHEAD]).then_inc(sem("q_roped"), 1)
            pool.wait_ge(x_done, 16)
            pool.memset(metaT[:, :, :].bitcast(F32), 0.0).then_inc(sem("meta_zero"), 1)
            pool.memset(glr[:, :, :], 0.0)
            pool.memset(glrM[:, :], 0.0).then_inc(sem("glr_zero"), 1)
            pool.memset(qA[:, :, :, :], 0.0)
            pool.memset(qB[:, :, :, :], 0.0).then_inc(sem("q_zero"), 1)


_INS = ["x", "p", "norm_pre", "norm_post", "w_in_a", "w_out_a", "w_in_b", "q_latent_norm", "w_uq", "w_out_b", "kv_norm",
        "w_dkv", "kv_latent_norm", "w_uk", "w_uv", "w_ple_proj", "w_ple_gate", "meta_tokens_2", "norm1_w_2", "w_in_2",
        "gate_w2_2", "gate_b_2", "gla_norm_w_2", "pool_w_2", "pool_scale_2", "w_out_2", "norm2_w_2", "mlp_w1_2",
        "mlp_w2_2", "final_norm_w_2"]


def kernel(**inputs):
    import numpy as _np
    import concourse.bacc as _bacc
    from concourse import mybir as _mybir
    from concourse.bass_utils import run_bass_kernel_spmd as _run

    nc = _bacc.Bacc("TRN2", target_bir_lowering=False, num_devices=1)
    arrays, w = {}, {}
    for name in _INS:
        a = _np.ascontiguousarray(inputs[name])
        arrays[f"in_{name}"] = a
        w[name] = nc.dram_tensor(f"in_{name}", a.shape, _mybir.dt.from_np(a.dtype), kind="ExternalInput").ap()
    table, _ = constants()
    arrays["tables"] = table
    const = nc.dram_tensor("tables", table.shape, F32, kind="ExternalInput").ap()
    out = nc.dram_tensor("out_0", (1, SEQ, D), F32, kind="ExternalOutput").ap()
    build(nc, w, const, out)
    r = _run(nc, [arrays], core_ids=[0])
    return r.results[0]["out_0"]
```

```python
from contextlib import ExitStack

import numpy as np
import concourse.bass as bass
from concourse import mybir

F32 = mybir.dt.float32
F32R = mybir.dt.float32r
ALU = mybir.AluOpType
ACT = mybir.ActivationFunctionType
AX = mybir.AxisListType.X

P = 128
SEQ = 256
TT = SEQ // P
D = 2048
KT = D // P
CH = 512
NCH = D // CH
QT = CH // P
EPS = 1e-6
NEG = -1e30

HEADS = 16
HD = 128
ROPE = 64
LORA = 512
LK = LORA // P
QHEAD = HD + ROPE
CHUNK = 64

META = 16
GLA_H = 4
DK = 128
DV = 256
GKW = GLA_H * DK
GRANK = 16
TAU = 16.0
WINDOWS = (2, 4, 8, 16)
PGC = 256
DFF = 4 * D

LAST = {3: [6], 4: [7]}
SPREAD = {1: [3], 2: [4], 3: [5], 4: [6], 5: [7]}
OG_EARLY, OG_LATE = {4: [0], 5: [1], 6: [2], 7: [3]}, {0: [4], 1: [5], 3: [6], 4: [7]}
ALONG = {1: {4: [0], 5: [1]}, 2: {4: [2], 5: [3]}, 3: {4: [4], 5: [5]}}

UNIT = 1024
RING = 4


class Stage:

    def __init__(self, name, weight, chunks, units, kt, cols):
        self.name, self.weight, self.chunks, self.units, self.kt, self.cols = name, weight, chunks, units, kt, cols
        self.u0 = self.c0 = 0


def plan():
    deep = KT // 2
    st = [
        Stage("qk", "w_in_a", 8, deep, 2, CH), Stage("v", "w_in_a", 4, deep, 2, CH),
        Stage("g", "w_in_a", 4, deep, 2, CH), Stage("out_a", "w_out_a", 4, deep, 2, CH),
        Stage("ple0", "w_ple_proj", 4, 1, 2, CH), Stage("gate0", "w_ple_gate", 4, deep, 2, CH),
        Stage("ckv", "w_dkv", 1, deep, 2, CH), Stage("krope", "w_dkv", 1, 1, KT, ROPE),
        Stage("cq", "w_in_b", 1, deep, 2, CH), Stage("uk", "w_uk", 4, 2, 2, CH), Stage("uv", "w_uv", 4, 2, 2, CH),
        Stage("uq", "w_uq", 8, 2, 2, 2 * QHEAD), Stage("gb", "w_in_b", 4, deep, 2, CH),
        Stage("out_b", "w_out_b", 4, deep, 2, CH), Stage("ple1", "w_ple_proj", 4, 1, 2, CH),
        Stage("gate1", "w_ple_gate", 4, deep, 2, CH),
        Stage("glr", "w_in_2", 1, 1, KT, GRANK), Stage("k2", "w_in_2", 1, deep, 2, CH),
        Stage("q2", "w_in_2", 1, deep, 2, CH), Stage("v2", "w_in_2", 2, deep, 2, CH),
        Stage("pu", "w_in_2", 2, deep, 2, CH), Stage("r2", "w_in_2", 2, deep, 2, CH),
        Stage("pool", "pool_w_2", 2, 1, 4, PGC), Stage("out2", "w_out_2", 4, deep, 2, CH),
    ]
    for b in range(DFF // D):
        st += [Stage(f"up{b}", "mlp_w1_2", 4, deep, 2, CH), Stage(f"down{b}", "mlp_w2_2", 4, deep, 2, CH)]
    u = c = 0
    for s in st:
        s.u0, s.c0 = u, c
        u += s.units * s.chunks
        c += s.chunks
    return {s.name: s for s in st}, u


def join(*hooks):
    return {u: [f for h in hooks for f in h.get(u, [])] for u in sorted({u for h in hooks for u in h})}


def constants():
    s, t = np.arange(P)[:, None], np.arange(P)[None, :]
    t2 = np.arange(SEQ)[None, :]
    inv = (1.0 / (np.float32(10000.0) ** (np.arange(0, ROPE, 2, dtype=np.float32) / np.float32(ROPE)))).astype(np.float32)
    ang = np.arange(SEQ, dtype=np.float32)[:, None] * inv[None, :]
    two = lambda a: np.concatenate([np.repeat(a[i * P:(i + 1) * P, None, :], 2, 1).reshape(P, ROPE) for i in range(TT)], 1)
    same = s // CHUNK == t // CHUNK
    hole = NEG * ((s < CHUNK) & (t >= CHUNK))
    meta_s = s - META
    parts = {
        "ident": s == t,
        "suffix": s >= t,
        "ones": np.ones((P, P)),
        "strict": s < t,
        "strict_neg": NEG * (s >= t),
        "chunk_neg": np.concatenate([hole, np.zeros((P, P)), hole], 1),
        "cos": two(np.cos(ang)), "sin": two(np.sin(ang)),
        "gla_causal": same & (s <= t),
        "gla_after": same & (s > t),
        "gla_half": np.concatenate([s // CHUNK == 0, s // CHUNK == 1], 1),
        "band": np.concatenate([((t2 >= s) & (t2 - s < w)) / w - (t2 == s) * 1.0 for w in WINDOWS], 1),
        "band_meta": np.concatenate([((s < META) & (t - meta_s < w)) / w for w in WINDOWS], 1),
    }
    where, at = {}, 0
    for name, a in parts.items():
        where[name] = (at, a.shape[1])
        at += a.shape[1]
    return np.ascontiguousarray(np.concatenate([np.asarray(a, np.float32) for a in parts.values()], 1), np.float32), where


def build(nc, w, const, out):
    S, units = plan()
    table, where = constants()
    ctx = ExitStack()
    with ctx:
        place = [(nc.sbuf_base + 63) // 64 * 64]

        def region(nbytes):
            at = place[0]
            place[0] = at + (nbytes + 63) // 64 * 64
            assert place[0] <= nc.sbuf_usable_end, place[0]
            return at

        def sb(name, shape, dt, at):
            return nc.alloc_sbuf_tensor_at(name, shape, dt, offset=at)

        KB = 1024
        raw = sb("raw", [P, RING, UNIT], F32, region(16 * KB))
        whi = sb("whi", [P, RING, UNIT], F32R, region(16 * KB))
        wlo = sb("wlo", [P, RING, UNIT], F32R, region(16 * KB))
        x = sb("x", [P, TT, D], F32, region(16 * KB))
        nat = sb("nat", [P, TT, D], F32, region(16 * KB))
        r0, r1, r2 = region(32 * KB), region(32 * KB), region(16 * KB)
        stg_at = region(8 * KB)
        r3 = region(8 * KB)
        r4 = region(9 * KB)
        ahi = sb("ahi", [P, KT, SEQ], F32R, r0)
        alo = sb("alo", [P, KT, SEQ], F32R, r0 + 16 * KB)
        bhi = sb("bhi", [P, KT, SEQ], F32R, r1)
        blo = sb("blo", [P, KT, SEQ], F32R, r1 + 16 * KB)
        stg = sb("stg", [P, 2, TT, CH], F32, stg_at)
        gains = sb("gains", [P, D], F32, r3)
        tab = sb("tab", [P, table.shape[1]], F32, region(table.shape[1] * 4))
        p_at = region(8 * KB)
        phi = sb("phi", [P, 2, 2, SEQ], F32R, p_at)
        plo = sb("plo", [P, 2, 2, SEQ], F32R, p_at + 4 * KB)
        gcol = sb("gcol", [P, P], F32, region(512))
        st_at = region(1024)
        ssq = sb("ssq", [P, TT, 4], F32, st_at)
        ssum = sb("ssum", [P, 8], F32, st_at + 64)
        root = sb("root", [P, 8], F32, st_at + 128)
        rs = sb("rs", [P, 8, 8], F32, st_at + 192)
        mx = sb("mx", [P, 2, 4], F32, st_at + 512)
        den = sb("den", [P, 2, 4], F32, st_at + 576)
        rden = sb("rden", [P, 2, 4], F32, st_at + 640)
        eps = sb("eps", [P, 1], F32, st_at + 704)
        psrc = sb("psrc", [P, 2, TT, 2 * P], F32, r2)
        qkT = sb("qkT", [P, 2 * HEADS, SEQ], F32, r1)
        vA = sb("vA", [P, TT, D], F32, r2)
        zA = sb("zA", [P, 2, 3 * P], F32, r3)
        tA = sb("tA", [P, 2, 3 * P], F32, r3 + 3 * KB)
        pp = sb("pp", [P, TT, D], F32, r2)
        knT = sb("knT", [P, HEADS, SEQ], F32, r1)
        vB = sb("vB", [P, TT, D], F32, r1 + 16 * KB)
        kvhi = sb("kvhi", [P, LK, SEQ], F32R, r2)
        kvlo = sb("kvlo", [P, LK, SEQ], F32R, r2 + 4 * KB)
        cqhi = sb("cqhi", [P, LK, SEQ], F32R, r2 + 8 * KB)
        cqlo = sb("cqlo", [P, LK, SEQ], F32R, r2 + 12 * KB)
        sB = sb("sB", [P, 2, 3 * P], F32, r3)
        pB = sb("pB", [P, 2, 3 * P], F32, r3 + 3 * KB)
        qn = sb("qn", [P, 2, 2, SEQ], F32, r4)
        qr = sb("qr", [P, 2, SEQ], F32, r4 + 4 * KB)
        krT = sb("krT", [P, SEQ], F32, r4 + 6 * KB)
        roped = sb("roped", [P, TT, 2 * ROPE], F32, r4 + 7 * KB)
        turn = sb("turn", [P, TT, 2, ROPE // 2], F32, r4 + 8 * KB)
        kraw = sb("kraw", [P, TT, 2, ROPE], F32, r4)
        vC = sb("vC", [P, TT, GLA_H * DV], F32, r0)
        vM = sb("vM", [P, GLA_H * DV], F32, r0 + 8 * KB)
        kend = sb("kend", [P, TT, GKW], F32, r0 + 12 * KB)
        kendM = sb("kendM", [P, GKW], F32, r0 + 16 * KB)
        kTc = sb("kTc", [P, GLA_H, SEQ], F32, r0 + 18 * KB)
        qA = sb("qA", [P, GLA_H, TT, P], F32, r0 + 22 * KB)
        qB = sb("qB", [P, GLA_H, TT, P], F32, r0 + 26 * KB)
        oneM = sb("oneM", [P, CH], F32, r0 + 30 * KB)
        metaT = sb("metaT", [P, KT, P], F32R, r2)
        logg = sb("logg", [P, TT, GKW], F32, r2 + 8 * KB)
        loggM = sb("loggM", [P, GKW], F32, r2 + 12 * KB)
        msc = sb("msc", [P, GKW], F32, r2 + 14 * KB)
        yhi = sb("yhi", [P, 8, SEQ], F32R, r2)
        ylo = sb("ylo", [P, 8, SEQ], F32R, r2 + 8 * KB)
        puM = sb("puM", [P, 2 * CH], F32, p_at)
        metax = sb("metax", [P, D], F32, r3)
        state = sb("state", [P, 2, 4, DV], F32, r3)
        glr = sb("glr", [P, TT, P], F32, r4)
        glrM = sb("glrM", [P, P], F32, r4 + 1 * KB)
        glrT = sb("glrT", [P, SEQ + META], F32, r4 + 1536)
        gw2 = sb("gw2", [P, GKW], F32, r4 + 3 * KB)
        brow = sb("brow", [P, GKW], F32, r4 + 5 * KB)
        decay = sb("decay", [P, GLA_H, 4], F32, r4 + 7 * KB)
        sc = sb("sc", [P, TT, P], F32, r4 + 7 * KB + 512)

        acc = [[ctx.enter_context(nc.psum_tensor(f"acc{p}{t}", [P, CH], F32)) for t in range(TT)] for p in range(2)]
        tp = [ctx.enter_context(nc.psum_tensor(f"tp{p}", [P, CH], F32)) for p in range(2)]
        xb = [ctx.enter_context(nc.psum_tensor(f"xb{p}", [P, CH], F32)) for p in range(2)]

        def const_of(name, rows=P):
            a, n = where[name]
            return tab[0:rows, a:a + n]

        ident = const_of("ident")
        GC = {"pre0": 0, "pre1": 16, "kv": 32, "norm1": 48, "norm2": 64, "kvl": 80, "ql": 84, "gla": 88, "pool": 90}
        RS = {"pre0": 0, "post": 1, "pre1": 2, "kvl": 3, "ql": 4, "norm1": 5, "norm2": 0, "final": 1}

        sems = {}

        def sem(name):
            if name not in sems:
                sems[name] = ctx.enter_context(nc.semaphore(name))
            return sems[name]

        raw_full = [sem(f"raw_full{i}") for i in range(RING)]
        hi_done, lo_done = sem("hi_done"), sem("lo_done")
        unit_used = sem("unit_used")
        evac_act, evac_dve = sem("evac_act"), sem("evac_dve")
        tp_full, tp_hi, tp_done = sem("tp_full"), sem("tp_hi"), sem("tp_done")
        x_done = sem("x_done")

        order = [("gcol", 1), ("x0", 8), ("p", 2), ("qk", 16), ("ogA", 8), ("x1", 8), ("x2a", [0, 1, 2, 3, 4, 5]),
                 ("x2b", [0, 1, 2, 3]), ("x2a", [6, 7]), ("x2b", [4, 5, 6, 7]), ("ckv", 2), ("kr", 1),
                 ("cq", 2), ("uk", 8), ("uq", 16), ("ogB", 8), ("x3", 8), ("x4", 8), ("meta", 1), ("glr", 1), ("kinv", 2),
                 ("qdec", 2), ("pool", 4), ("mixed", 8), ("x5", 8)] + [(f"mlp{q}", 8) for q in range(DFF // D)]
        whole = ("gcol", "qk", "kr", "uk", "uq", "glr", "kinv", "qdec")
        BATCH, n_all, n_split = {}, 0, 0
        for name, fs in order:
            for f in range(fs) if isinstance(fs, int) else fs:
                BATCH[name, f] = (n_all, n_split)
                n_all += 1
                n_split += 0 if name in whole else 1

        def shape_of(u):
            s = max((s for s in S.values() if s.u0 <= u), key=lambda s: s.u0)
            return s.kt, s.cols

        def unit_source(s, j, uu):
            if s.name == "pool":
                return w["pool_w_2"][0, 2 * j:2 * j + 2].rearrange("g (k p) n -> p (g k) n", p=P)
            base = {"v": 2 * D, "g": 3 * D, "krope": LORA, "gb": LORA, "q2": 0, "k2": GKW, "v2": 2 * GKW,
                    "r2": 2 * GKW + GLA_H * DV, "glr": 2 * GKW + 2 * GLA_H * DV,
                    "pu": 2 * GKW + 2 * GLA_H * DV + GRANK}.get(s.name, 0)
            t = w[s.weight]
            if len(t.shape) == 3:
                t = t[1 if s.name in ("ple1", "gate1") else 0]
            row = uu * s.kt * P
            if s.name.startswith("down"):
                row = row + int(s.name[4:]) * D
            if s.name.startswith("up"):
                base = int(s.name[2:]) * D
            col = base + j * s.cols
            return t[row:row + s.kt * P, bass.ds(col, s.cols)].rearrange("(k p) n -> p k n", p=P)

        def x_rows(ap):
            return ap.rearrange("(t p) d -> p t d", p=P)

        block = ctx.enter_context(nc.Block())

        @block.sync
        def _(sp):
            def load(s, j, uu, r=0):
                u = s.u0 + j * s.units + uu if isinstance(j, int) else s.u0 + uu
                if u >= RING or not isinstance(r, int):
                    sp.wait_ge(lo_done, u - RING + 1 + r)
                dst = raw[:, u % RING, 0:s.kt * s.cols].rearrange("p (k n) -> p k n", k=s.kt)
                sp.dma_start(dst, unit_source(s, j, uu)).then_inc(raw_full[u % RING], 16)

            def stage(name, lo=0, hi=None):
                s = S[name]
                for j in range(lo, s.chunks if hi is None else hi):
                    for uu in range(s.units):
                        load(s, j, uu)

            sp.dma_start(tab[:, 0:P], const[:, 0:P]).then_inc(sem("ident_in"), 16)
            rows = [("norm_pre", 0, "pre0", 16), ("norm_pre", 1, "pre1", 16), ("kv_norm", None, "kv", 16),
                    ("norm1_w_2", 0, "norm1", 16), ("norm2_w_2", 0, "norm2", 16), ("kv_latent_norm", None, "kvl", 4),
                    ("q_latent_norm", 0, "ql", 4), ("gla_norm_w_2", 0, "gla", 2), ("pool_scale_2", 0, "pool", 8)]
            for name, i, key, n in rows:
                src = w[name] if i is None else w[name][i]
                sp.dma_start(gains[GC[key]:GC[key] + n, 0:P], src.rearrange("(a b) -> a b", b=P)).then_inc(sem("gain_rows_in"), 16)
            s = S["qk"]
            for uu in range(s.units):
                if uu < NCH:
                    c = slice(uu * CH, (uu + 1) * CH)
                    sp.dma_start(x[:, :, c], x_rows(w["x"][0])[:, :, c]).then_inc(sem(f"x_in{uu}"), 16)
                if uu == NCH:
                    for l in range(2):
                        sp.dma_start(psrc[:, l], x_rows(w["p"][l, 0])).then_inc(sem(f"p_in{l}"), 16)
                load(s, 0, uu)
            sp.dma_start(tab[:, P:], const[:, P:]).then_inc(sem("tab_in"), 16)
            s = S["qk"]
            with sp.Fori(1, s.chunks) as j:
                for uu in range(s.units):
                    load(s, j, uu, r=j * s.units)
            stage("v")
            stage("g")
            stage("out_a", 0, 1)
            sp.wait_ge(sem("attA_o"), HEADS)
            sp.dma_start(gains[:, :], w["norm_post"][0:1, :].to_broadcast((P, D))).then_inc(sem("post_in0"), 16)
            stage("out_a", 1)
            for name in ("ple0", "gate0", "ckv", "krope", "cq", "uk", "uv", "uq", "gb"):
                stage(name)
            stage("out_b", 0, 1)
            sp.wait_ge(sem("attB_o"), HEADS // 2)
            sp.dma_start(gains[:, :], w["norm_post"][1:2, :].to_broadcast((P, D))).then_inc(sem("post_in1"), 16)
            stage("out_b", 1)
            stage("ple1")
            stage("gate1", 0, 1)
            sp.wait_ge(sem("post1_y"), 8)
            sp.dma_start(metax[0:META, :], w["meta_tokens_2"]).then_inc(sem("meta_in"), 16)
            sp.dma_start(gw2[0:GRANK, :], w["gate_w2_2"][0]).then_inc(sem("gate_in"), 16)
            sp.dma_start(brow[0:1, :], w["gate_b_2"]).then_inc(sem("gate_in2"), 16)
            stage("gate1", 1)
            for name in ("glr", "k2", "q2", "v2", "pu", "r2", "pool"):
                stage(name)
            sp.wait_ge(sem("gla_rs"), 1)
            sp.dma_start(gains[:, :], w["final_norm_w_2"].rearrange("(a b) -> a b", a=1).to_broadcast((P, D))).then_inc(sem("final_in"), 16)
            stage("out2")
            for b in range(DFF // D):
                stage(f"up{b}")
                stage(f"down{b}")
            for j in range(NCH):
                sp.wait_ge(sem("final_y"), TT * (j + 1))
                c = slice(j * CH, (j + 1) * CH)
                sp.dma_start(x_rows(out[0])[:, :, c], nat[:, :, c]).then_inc(sem("stored"), 16)
            sp.wait_ge(sem("stored"), 16 * NCH)

        @block.tensor
        def _(pe):
            b = [0]

            def product(s, j, hi, lo, r=0, rc=0, hooks={}, need=None, banks=None, meta=False, behind=1, before=None):
                u, c = s.u0 + j * s.units, s.c0 + j
                bank = banks or acc[c % 2]
                if c >= 2:
                    pe.wait_ge(evac_act, c - behind + rc)
                    pe.wait_ge(evac_dve, c - behind + rc)
                if before:
                    before()
                for uu in range(s.units):
                    for hook in hooks.get(uu, []):
                        hook()
                    if need:
                        pe.wait_ge(tp_done, BATCH[need, uu][0] + 1)
                    pe.wait_ge(lo_done, u + uu + 1 + r)
                    slot = (u + uu) % RING
                    for k in range(s.kt):
                        kt = uu * s.kt + k
                        cols = slice(k * s.cols, (k + 1) * s.cols)
                        first, last = kt == 0, kt == s.units * s.kt - 1
                        for t in range(TT):
                            tok = slice(t * P, (t + 1) * P)
                            o = bank[t][:, 0:s.cols]
                            pe.matmul(o, hi[:, kt, tok], whi[:, slot, cols], start=first, stop=False)
                            pe.matmul(o, hi[:, kt, tok], wlo[:, slot, cols], start=False, stop=False)
                            mm = pe.matmul(o, lo[:, kt, tok], whi[:, slot, cols], start=False, stop=last)
                        if meta:
                            o = xb[c % 2][:, 0:s.cols]
                            pe.matmul(o, metaT[:, kt, :], whi[:, slot, cols], start=first, stop=False)
                            mm = pe.matmul(o, metaT[:, kt, :], wlo[:, slot, cols], start=False, stop=last)
                    mm.then_inc(unit_used, 1)

            def batch(parts, r=0):
                n = b[0]
                b[0] += 1
                if n >= 2:
                    pe.wait_ge(tp_done, n - 1 + r)
                for src, k, o in parts:
                    mm = pe.transpose(tp[n % 2][:, o:o + k], src, ident[0:k, 0:k])
                mm.then_inc(tp_full, 1)

            def pair(src, f):
                batch([(src[:, t, (2 * f + i) * P:(2 * f + i + 1) * P], P, i * SEQ + t * P) for i in range(2) for t in range(TT)])

            def staged(par, r=0, b_r=0):
                for f in range(2):
                    batch([(stg[:, par, t, (2 * f + i) * P:(2 * f + i + 1) * P], P, i * SEQ + t * P)
                           for i in range(2) for t in range(TT)], r=b_r)

            def ready(name, f):
                j = f // 2
                if name == "x0":
                    pe.wait_ge(sem(f"x_in{j}"), 16)
                elif name in X_DONE:
                    pe.wait_ge(x_done, X_DONE[name] + j + 1)
                elif name == "x5":
                    pe.wait_ge(evac_dve, S["out2"].c0 + j + 1)
                else:
                    evacuated(S["g" if name == "ogA" else "gb"].c0 + j)

            def turn(name, f):
                ready(name, f)
                assert BATCH[name, f][0] == b[0], (name, f)
                pair(nat if name.startswith("og") else x, f)

            def turns(name, plan):
                return {uu: [lambda f=f: turn(name, f) for f in fs] for uu, fs in plan.items()}

            def turn_part(name, f, c):
                evacuated(c)
                assert BATCH[name, f][0] == b[0], (name, f)
                batch([(stg[:, c % 2, t, (2 * (f % 2) + i) * P:(2 * (f % 2) + i + 1) * P], P, i * SEQ + t * P)
                       for i in range(2) for t in range(TT)])

            def turns_staged(name, plan, c):
                return {uu: [lambda f=f: turn_part(name, f, c) for f in fs] for uu, fs in plan.items()}
            X_DONE = {"x1": 0, "x2a": 4, "x2b": 4, "x3": 8, "x4": 12}

            def evacuated(c, r=0):
                pe.wait_ge(evac_act, c + 1 + r)
                pe.wait_ge(evac_dve, c + 1 + r)

            pe.wait_ge(sem("ident_in"), 16)
            pe.wait_ge(sem("gain_rows_in"), 9 * 16)
            batch([(gains[0:98, 0:P], 98, 0)])
            for f in range(3):
                turn("x0", f)

            def turn_p(l):
                pe.wait_ge(sem(f"p_in{l}"), 16)
                batch([(psrc[:, l, t, k * P:(k + 1) * P], P, k * SEQ + t * P) for k in range(2) for t in range(TT)])
            s = S["qk"]
            product(s, 0, ahi, alo, need="x0", hooks=join(turns("x0", SPREAD), {6 + l: [lambda l=l: turn_p(l)] for l in range(2)}))
            with pe.Fori(0, 3) as i:
                b_start = b[0]
                for q in (1, 2):
                    rc, r = i * 2, i * (2 * s.units)

                    def turn_last(q=q, rc=rc):
                        evacuated(s.c0 + q - 1, rc)
                        staged((s.c0 + q - 1) % 2, b_r=i * 4)
                    product(s, q, ahi, alo, r=r, rc=rc, hooks={4: [turn_last]})
            b[0] = b_start + 4 * 3
            product(s, 7, ahi, alo, hooks=turns_staged("qk", {4: [12, 13]}, 6))
            product(S["v"], 0, ahi, alo, hooks=turns_staged("qk", {4: [14, 15]}, 7))

            def logits(h):
                if h == 0:
                    pe.wait_ge(sem("tab_in"), 16)
                    pe.wait_ge(tp_done, b[0])
                else:
                    pe.wait_ge(sem("attA_z"), h)
                z = xb[0]
                pe.matmul(z[:, 0:SEQ], qkT[:, HEADS + h, 0:P], qkT[:, h, :], start=True, stop=True)
                pe.matmul(z[:, SEQ:SEQ + P], qkT[:, HEADS + h, P:SEQ], qkT[:, h, P:SEQ], start=True, stop=True).then_inc(sem("attA_logits"), 1)

            def later_sums(h):
                pe.wait_ge(sem("attA_sp"), h + 1)
                if h:
                    pe.wait_ge(sem("attA_d"), h)
                sums = xb[1]
                pe.matmul(sums[:, 0:3 * P], const_of("suffix"), tA[:, h % 2, :], start=True, stop=False)
                pe.matmul(sums[:, P:2 * P], const_of("ones"), tA[:, h % 2, 2 * P:3 * P], start=False, stop=True).then_inc(sem("attA_sums"), 1)

            def values(h):
                pe.wait_ge(sem("attA_w"), h + 1)
                if h >= 2:
                    pe.wait_ge(sem("attA_o"), h - 1)
                if h % 4 == 0:
                    pe.wait_ge(evac_act, S["v"].c0 + h // 4 + 1)
                    pe.wait_ge(evac_dve, S["v"].c0 + h // 4 + 1)
                o = tp[h % 2]
                c = slice(h * HD, (h + 1) * HD)
                pe.matmul(o[:, 0:P], zA[:, h % 2, 0:P], vA[:, 0, c], start=True, stop=True)
                pe.matmul(o[:, P:2 * P], zA[:, h % 2, P:2 * P], vA[:, 0, c], start=True, stop=False)
                pe.matmul(o[:, P:2 * P], zA[:, h % 2, 2 * P:3 * P], vA[:, 1, c], start=False, stop=True).then_inc(sem("attA_out"), 1)

            def attention_part(m):
                h = m // 3
                if m % 3 == 0 and 1 <= h <= HEADS:
                    later_sums(h - 1)
                if m % 3 == 0 and h < HEADS:
                    logits(h)
                if m % 3 == 2 and 1 <= h <= HEADS:
                    values(h - 1)

            def attention_of(n):
                return {uu: [lambda m=8 * n + uu: attention_part(m)] for uu in range(8)}
            for j in range(1, 4):
                product(S["v"], j, ahi, alo, hooks=attention_of(j - 1))

            for j in range(4):
                hooks = attention_of(3 + j)
                if j == 3:
                    hooks = join(hooks, {4: [lambda: pe.wait_ge(sem("attA_o"), HEADS)]}, turns("ogA", OG_EARLY))
                product(S["g"], j, ahi, alo, hooks=hooks)

            def post(layer, y, x1, x2):
                ab = "ab"[layer]
                for j in range(4):
                    product(S[f"out_{ab}"], j, bhi, blo, need=y if j == 0 else None, hooks=turns(y, OG_LATE if layer == 0 else SPREAD) if j == 0 else {})
                for j in range(4):
                    product(S[f"ple{layer}"], j, phi[:, layer], plo[:, layer])
                for f in range(3):
                    turn(x1, f)
                for j in range(4):
                    product(S[f"gate{layer}"], j, ahi, alo, need=x1 if j == 0 else None, hooks=turns(x2, ALONG[j]) if j else turns(x1, SPREAD))

            post(0, "ogA", "x1", "x2a")

            product(S["ckv"], 0, bhi, blo, need="x2a", hooks=join(turns("x2b", {0: [0, 1], 1: [2, 3]}), turns("x2a", LAST), turns("x2b", {5: [4], 6: [5]})))
            product(S["krope"], 0, bhi, blo)
            c = S["ckv"].c0

            def turn_k_rope():
                pe.wait_ge(sem("k_roped"), 1)
                batch([(roped[:, t, :], P, t * P) for t in range(TT)])
            product(S["cq"], 0, ahi, alo, need="x2b", hooks=join(turns("x2b", {0: [6], 1: [7]}), turns_staged("ckv", {4: [0], 5: [1]}, c), {7: [turn_k_rope]}))
            pe.wait_ge(tp_done, b[0])
            s = S["uk"]
            for j in range(4):
                product(s, j, kvhi, kvlo)
                if j:
                    for f in (2 * j - 2, 2 * j - 1):
                        turn_part("uk", f, s.c0 + j - 1)
                if j == 0:
                    for f in range(2):
                        turn_part("cq", f, S["cq"].c0)
            s = S["uv"]
            for j in range(4):
                product(s, j, kvhi, kvlo)
                if j == 0:
                    for f in (6, 7):
                        turn_part("uk", f, s.c0 - 1)

            s = S["uq"]

            def queries(j, r=0):
                product(s, j, cqhi, cqlo, banks=acc[0], behind=0)
                evacuated(s.c0 + j)
                batch([(stg[:, j % 2, t, i * QHEAD:i * QHEAD + HD], P, i * SEQ + t * P) for i in range(2) for t in range(TT)])
                pe.wait_ge(sem("q_roped"), j + 1)
                batch([(roped[:, t, :], P, t * P) for t in range(TT)])

            def scores(h):
                p, i = (h // 2) % 2, h % 2
                rows = slice(i * ROPE, (i + 1) * ROPE)
                sB_ps = xb[i]
                for o, qt, n in ((0, 0, P), (P, 1, SEQ)):
                    q = slice(qt * P, (qt + 1) * P)
                    pe.matmul(sB_ps[:, o:o + n], qn[:, p, i, q], knT[:, h, 0:n], start=True, stop=False)
                    mm = pe.matmul(sB_ps[:, o:o + n], qr[rows, p, q], krT[rows, 0:n], start=False, stop=True)
                mm.then_inc(sem("attB_s"), 1)

            def turned(h):
                i = h % 2
                pe.wait_ge(sem("attB_p"), h + 1)
                if i == 0 and h >= 2:
                    pe.wait_ge(sem("attB_o"), h // 2)
                for k in range(3):
                    mm = pe.transpose(acc[1][i][:, k * P:(k + 1) * P], sB[:, i, k * P:(k + 1) * P], ident)
                mm.then_inc(sem("attB_t"), 1)

            def outputs(c):
                for i in range(2):
                    h = 2 * c + i
                    pe.wait_ge(sem("attB_pt"), h + 1)
                    o, cols = acc[1][0][:, i * SEQ:(i + 1) * SEQ], slice(h * HD, (h + 1) * HD)
                    pe.matmul(o[:, 0:P], pB[:, i, 0:P], vB[:, 0, cols], start=True, stop=True)
                    pe.matmul(o[:, P:SEQ], pB[:, i, P:2 * P], vB[:, 0, cols], start=True, stop=False)
                    mm = pe.matmul(o[:, P:SEQ], pB[:, i, 2 * P:3 * P], vB[:, 1, cols], start=False, stop=True)
                mm.then_inc(sem("attB_out"), 1)

            evacuated(s.c0 - 1)
            pe.wait_ge(tp_done, b[0])
            queries(0)
            for c in range(8):
                pe.wait_ge(tp_done, b[0])
                scores(2 * c)
                scores(2 * c + 1)
                if c < 7:
                    queries(c + 1)
                turned(2 * c)
                turned(2 * c + 1)
                outputs(c)

            s = S["gb"]
            for j in range(4):
                product(s, j, ahi, alo, behind=0 if j == 0 else 1, before=(lambda: pe.wait_ge(sem("attB_o"), 8)) if j == 0 else None)
            for f in range(3):
                turn("ogB", f)
            post(1, "ogB", "x3", "x4")
            for f in (6, 7):
                turn("x4", f)

            pe.wait_ge(sem("meta_in"), 16)
            batch([(metax[0:META, k * P:(k + 1) * P], META, k * META) for k in range(KT)])
            pe.wait_ge(tp_done, b[0])
            product(S["glr"], 0, bhi, blo, meta=True)
            product(S["k2"], 0, bhi, blo, meta=True)
            evacuated(S["glr"].c0)
            batch([(glr[:, t, :], P, t * P) for t in range(TT)] + [(glrM[0:META, :], META, SEQ)])
            product(S["q2"], 0, bhi, blo)
            pe.wait_ge(tp_done, b[0])
            pe.wait_ge(sem("gate_in"), 16)
            pe.wait_ge(sem("gate_in2"), 16)
            for t in range(TT + 1):
                n = P if t < TT else META
                o = (tp[0], tp[1], xb[1])[t]
                if t == TT:
                    pe.wait_ge(evac_dve, S["k2"].c0 + 1)
                pe.matmul(o[0:n, :], glrT[0:GRANK, t * P:t * P + n], gw2[0:GRANK, :], start=True, stop=False)
                pe.matmul(o[0:n, :], const_of("ones")[0:1, 0:n], brow[0:1, :], start=False, stop=True).then_inc(sem("graw"), 1)
            s = S["v2"]
            product(s, 0, bhi, blo, meta=True, before=lambda: pe.wait_ge(sem("logg"), 3))
            for t in range(TT):
                pe.matmul(tp[t][:, :], const_of("gla_causal"), logg[:, t, :], start=True, stop=True).then_inc(sem("G"), 1)
            for t in range(TT):
                pe.wait_ge(sem("eG"), 2 * (t + 1))
                pe.matmul(tp[t][:, :], const_of("gla_after"), logg[:, t, :], start=True, stop=True).then_inc(sem("G"), 1)
            pe.wait_ge(evac_dve, s.c0 + 1)
            pe.wait_ge(evac_act, s.c0 + 1)
            pe.matmul(xb[0][0:META, :], const_of("gla_after")[0:META, 0:META], loggM[0:META, :], start=True, stop=True).then_inc(sem("G"), 1)
            product(s, 1, bhi, blo, meta=True)
            pe.wait_ge(sem("eG"), 7)
            for h in range(GLA_H):
                for t in range(TT):
                    mm = pe.matmul(xb[0][:, (h * TT + t) * 2:(h * TT + t) * 2 + 2], logg[:, t, h * DK:(h + 1) * DK],
                                   const_of("gla_half"), start=True, stop=True)
            mm.then_inc(sem("G"), 1)
            pe.wait_ge(sem("kinv"), 1)
            for f in range(2):
                pair(nat, f)
            pe.wait_ge(sem("qdec"), 1)
            for f in range(2):
                batch([(stg[:, 0, t, (2 * f + i) * P:(2 * f + i + 1) * P], P, i * SEQ + t * P) for i in range(2) for t in range(TT)])
            s = S["pu"]
            product(s, 0, bhi, blo, meta=True, before=lambda: pe.wait_ge(sem("decay"), 1))
            product(s, 1, bhi, blo, meta=True)

            pe.wait_ge(evac_dve, s.c0 + 2)
            pe.wait_ge(evac_act, s.c0 + 2)
            pe.wait_ge(tp_done, b[0])
            for h in range(GLA_H):
                dk, dv = slice(h * DK, (h + 1) * DK), slice(h * DV, (h + 1) * DV)
                if h:
                    pe.wait_ge(sem("gla_sc"), h)
                for t in range(TT):
                    k_ = kTc[:, h, t * P:(t + 1) * P]
                    pe.matmul(tp[0][:, t * P:t * P + 64], k_, qA[:, h, t, 0:64], start=True, stop=True)
                    mm = pe.matmul(tp[0][:, t * P + 64:t * P + P], k_, qB[:, h, t, 64:P], start=True, stop=True)
                mm.then_inc(sem("gla_scores"), 1)
                if h:
                    pe.wait_ge(sem("gla_state"), h)
                pe.matmul(xb[0][:, 0:DV], kend[0:64, 0, dk], vC[0:64, 0, dv], start=True, stop=True)
                pe.matmul(xb[0][:, DV:2 * DV], kend[0:64, 1, dk], vC[0:64, 1, dv], start=True, stop=True)
                pe.matmul(xb[1][:, 0:DV], kend[64:P, 0, dk], vC[64:P, 0, dv], start=True, stop=True)
                pe.matmul(xb[1][:, DV:2 * DV], kendM[0:META, dk], vM[0:META, dv], start=True, stop=True).then_inc(sem("gla_ds"), 1)
                pe.wait_ge(sem("gla_sc"), h + 1)
                pe.wait_ge(sem("gla_state"), h + 1)
                if h:
                    pe.wait_ge(sem("gla_o"), h)
                for t in range(TT):
                    o = tp[1][:, t * DV:(t + 1) * DV]
                    pe.matmul(o, sc[:, t, :], vC[:, t, dv], start=True, stop=False)
                    pe.matmul(o, qA[:, h, t, :], state[:, h % 2, 2 * t, :], start=False, stop=False)
                    mm = pe.matmul(o, qB[:, h, t, :], state[:, h % 2, 2 * t + 1, :], start=False, stop=True)
                mm.then_inc(sem("gla_out"), 1)
            s = S["r2"]
            product(s, 0, bhi, blo)
            pe.wait_ge(sem("gla_o"), GLA_H)
            for f in range(4):
                n = b[0]
                b[0] += 1
                if f >= 2:
                    pe.wait_ge(tp_done, n - 1)
                band, bm = const_of("band"), const_of("band_meta")
                for i in range(2):
                    ct = 2 * f + i
                    g, cs = ct // 2, slice(NCH // 2 * CH + ct * P, NCH // 2 * CH + (ct + 1) * P)
                    o = tp[n % 2][:, i * SEQ:(i + 1) * SEQ]
                    pe.matmul(o, nat[:, 0, cs], band[:, g * SEQ:(g + 1) * SEQ], start=True, stop=False)
                    pe.matmul(o[:, P:SEQ], nat[:, 1, cs], band[:, g * SEQ:g * SEQ + P], start=False, stop=False)
                    mm = pe.matmul(o[:, 0:P], puM[0:META, ct * P:(ct + 1) * P], bm[0:META, g * P:(g + 1) * P], start=False, stop=True)
                mm.then_inc(tp_full, 1)
            product(s, 1, bhi, blo)
            pe.wait_ge(tp_done, b[0])
            s = S["pool"]
            for j in range(2):
                u, c = s.u0 + j, s.c0 + j
                pe.wait_ge(evac_act, c - 1)
                pe.wait_ge(evac_dve, c - 1)
                pe.wait_ge(lo_done, u + 1)
                for g in range(2):
                    for t in range(TT):
                        for k in range(2):
                            ct, tok = 4 * j + 2 * g + k, slice(t * P, (t + 1) * P)
                            o = acc[c % 2][t][:, g * PGC:(g + 1) * PGC]
                            cols = slice((2 * g + k) * PGC, (2 * g + k + 1) * PGC)
                            pe.matmul(o, yhi[:, ct, tok], whi[:, u % RING, cols], start=(k == 0), stop=False)
                            pe.matmul(o, yhi[:, ct, tok], wlo[:, u % RING, cols], start=False, stop=False)
                            mm = pe.matmul(o, ylo[:, ct, tok], whi[:, u % RING, cols], start=False, stop=(k == 1))
                mm.then_inc(unit_used, 1)
            evacuated(S["r2"].c0 + 1)
            for f in range(4):
                pair(nat, f)
            evacuated(s.c0 + 1)
            for f in range(4, 8):
                pair(nat, f)
            pe.wait_ge(tp_done, b[0])
            for j in range(4):
                product(S["out2"], j, ahi, alo, hooks=turns("x5", ALONG[j]) if j else {})

            for q in range(DFF // D):
                s = S[f"up{q}"]
                for j in range(4):
                    first_x = q == 0 and j == 0
                    product(s, j, bhi, blo, need="x5" if first_x else None,
                            hooks=turns_staged(f"mlp{q}", ALONG[j], s.c0 + j - 1) if j else turns("x5", LAST) if first_x else {})
                for j in range(4):
                    product(S[f"down{q}"], j, ahi, alo, need=f"mlp{q}" if j == 0 else None,
                            hooks=turns_staged(f"mlp{q}", LAST, s.c0 + 3) if j == 0 else {})

        @block.scalar
        def _(act):
            ptr = [0]

            def split_to(target, r=0):
                for u in range(ptr[0], target):
                    kt, cols = shape_of(u)
                    act.wait_ge(raw_full[u % RING], 16 * (u // RING + 1) + r * 16 // RING if isinstance(r, int) else 16 * (u // RING + 1) + r * (16 // RING))
                    if u >= RING:
                        act.wait_ge(unit_used, u - RING + 1 + r)
                    n = kt * cols
                    act.activation(whi[:, u % RING, 0:n], raw[:, u % RING, 0:n], ACT.Copy).then_inc(hi_done, 1)
                ptr[0] = max(ptr[0], target)

            def along(s, j, hooks={}, r=0):
                for uu in range(s.units):
                    split_to(min(s.u0 + j * s.units + uu + 4, units), r)
                    for hook in hooks.get(uu, []):
                        hook()

            def his(name, dst, gain, plan):
                return {uu: [lambda f=f: hi_batch(name, f, dst, gain) for f in fs] for uu, fs in plan.items()}

            def ended(s, j, r=0):
                act.wait_ge(unit_used, s.u0 + (j + 1) * s.units + r)

            def hi_batch(name, f, dst, gain=None, at=None):
                n, k = BATCH[name, f][0], f if at is None else at
                act.wait_ge(tp_full, n + 1)
                src = tp[n % 2][:, :].rearrange("p (i t) -> p i t", i=2)
                if gain is None:
                    m = act.activation(dst[:, 2 * k:2 * k + 2, :], src, ACT.Copy)
                else:
                    for i in range(2):
                        m = act.activation(dst[:, 2 * k + i, :], src[:, i, :], ACT.Copy, scale=gcol[:, gain + 2 * k + i:gain + 2 * k + i + 1])
                m.then_inc(tp_hi, 1)

            def squares(norm, j, src, first_wait=None):
                for t in range(TT):
                    n = sq[0]
                    sq[0] += 1
                    if n >= 2:
                        act.wait_ge(sem("squares"), n - 1)
                    act.activation(xb[n % 2][:, 0:CH], src[:, t, j * CH:(j + 1) * CH], ACT.Square,
                                   accum_out=ssq[:, t, j:j + 1]).then_inc(sem("squares"), 1)
            sq = [0]

            def sqrt_of(norm, n=TT, width=D):
                act.wait_ge(sem(f"{norm}_ssum"), 1)
                act.activation(root[:, 0:n], ssum[:, 0:n], ACT.Sqrt, scale=1.0 / width, bias=eps_col).then_inc(sem(f"{norm}_root"), 1)
            eps_col = eps[:, 0:1]

            def scaled(dst, src, norm, t):
                return act.activation(dst, src, ACT.Copy, scale=rs[:, RS[norm], t:t + 1])

            act.wait_ge(sem("eps_set"), 1)
            act.wait_ge(tp_done, 1)
            for f in range(3):
                hi_batch("x0", f, ahi, GC["pre0"])
                split_to(f + 1)
            squares("pre0", 0, x)
            s = S["qk"]
            for uu in range(1, s.units):
                if uu < 6:
                    hi_batch("x0", uu + 2, ahi, GC["pre0"])
                else:
                    n = BATCH["p", uu - 6][0]
                    act.wait_ge(tp_full, n + 1)
                    act.activation(phi[:, uu - 6], tp[n % 2][:, :].rearrange("p (i t) -> p i t", i=2), ACT.Copy).then_inc(tp_hi, 1)
                split_to(s.u0 + uu + 3)
                if uu % 2 == 0:
                    squares("pre0", uu // 2, x)
            sqrt_of("pre0")
            s = S["qk"]
            act.wait_ge(sem("pre0_rs"), 1)

            def qk_chunk(q, i=None):
                r = 0 if i is None else i * (2 * s.units)
                along(s, q, r=r)
                ended(s, q, r)
                scaled(stg[:, q % 2, 0, :], acc[q % 2][0][:, :], "pre0", 0).then_inc(evac_act, 1)

            qk_chunk(0)
            qk_chunk(1)
            with act.Fori(0, 3) as i:
                first = ptr[0]
                for q in (2, 3):
                    qk_chunk(q, i)
            ptr[0] = first + 3 * 2 * s.units

            def softplus_terms(h, r=0):
                p = h % 2
                act.wait_ge(sem("attA_logits"), h + 1 + r)
                if h >= 2:
                    act.wait_ge(sem("attA_out"), h - 1 + r)
                    act.wait_ge(sem("attA_sums"), h - 1 + r)
                act.activation(zA[:, p, :], xb[0][:, 0:3 * P], ACT.Copy, scale=HD ** -0.5).then_inc(sem("attA_z"), 1)
                act.wait_ge(sem("attA_z"), h + 1 + r)
                act.activation(tA[:, p, :], zA[:, p, :], ACT.Abs).then_inc(sem("attA_t"), 1)
                act.wait_ge(sem("attA_t"), 3 * h + 1 + 3 * r)
                act.activation(tA[:, p, :], tA[:, p, :], ACT.Exp, scale=-1.0).then_inc(sem("attA_t"), 1)
                act.wait_ge(sem("attA_t"), 3 * h + 2 + 3 * r)
                act.activation(tA[:, p, :], tA[:, p, :], ACT.Ln, bias=1.0).then_inc(sem("attA_t"), 1)

            def weights(h, r=0):
                act.wait_ge(sem("attA_d"), h + 1 + r)
                act.activation(zA[:, h % 2, :], zA[:, h % 2, :], ACT.Exp).then_inc(sem("attA_w"), 1)

            def attention_of(n):
                def part(m):
                    h = m // 3
                    if m % 3 == 0 and h < HEADS:
                        softplus_terms(h)
                    if m % 3 == 1 and 1 <= h <= HEADS:
                        weights(h - 1)
                return {uu: [lambda m=8 * n + uu: part(m)] for uu in range(8)}

            s = S["v"]
            for j in range(4):
                along(s, j, attention_of(j - 1) if j else {})
                ended(s, j)
                scaled(vA[:, 0, j * CH:(j + 1) * CH], acc[(s.c0 + j) % 2][0][:, :], "pre0", 0).then_inc(evac_act, 1)

            def silu_chunk(s, j, norm):
                p = (s.c0 + j) % 2
                ended(s, j)
                if j >= 2:
                    act.wait_ge(evac_dve, s.c0 + j - 1)
                for t in range(TT):
                    m = act.activation(stg[:, p, t, :], acc[p][t][:, :], ACT.Silu, scale=rs[:, RS[norm], t:t + 1])
                m.then_inc(evac_act, 1)

            s = S["g"]
            for j in range(4):
                along(s, j, join(attention_of(3 + j), his("ogA", bhi, None, OG_EARLY) if j == 3 else {}))
                silu_chunk(s, j, "pre0")

            def post(layer, y, x1, x2, gain, norms):
                s = S[f"out_{'ab'[layer]}"]
                for j in range(4):
                    p = (s.c0 + j) % 2
                    along(s, j, his(y, bhi, None, OG_LATE if layer == 0 else SPREAD) if j == 0 else {})
                    ended(s, j)
                    act.activation(nat[:, 0, j * CH:(j + 1) * CH], acc[p][0][:, :], ACT.Copy).then_inc(evac_act, 1)
                    act.wait_ge(evac_act, s.c0 + j + 1)
                    act.wait_ge(evac_dve, s.c0 + j + 1)
                    squares("post", j, nat)
                sqrt_of(f"post{layer}")
                s = S[f"ple{layer}"]
                for j in range(4):
                    p = (s.c0 + j) % 2
                    split_to(s.u0 + j + 4)
                    ended(s, j)
                    act.activation(pp[:, 0, j * CH:(j + 1) * CH], acc[p][0][:, :], ACT.Copy).then_inc(evac_act, 1)
                for f in range(3):
                    hi_batch(x1, f, ahi)
                s = S[f"gate{layer}"]
                for j in range(4):
                    c, p = s.c0 + j, (s.c0 + j) % 2

                    def last_squares(j=j):
                        act.wait_ge(x_done, 8 * layer + 4 + j)
                        squares(norms, j - 1, x)
                    along(s, j, join({4: [last_squares]}, his(x2, bhi, gain, ALONG[j])) if j else his(x1, ahi, None, SPREAD))
                    ended(s, j)
                    for t in range(TT):
                        m = act.activation(stg[:, p, t, :], acc[p][t][:, :], ACT.Sigmoid)
                    m.then_inc(evac_act, 1)

            def x_norm(layer, norms):
                act.wait_ge(x_done, 8 * layer + 8)
                squares(norms, 3, x)
                sqrt_of(norms)

            post(0, "ogA", "x1", "x2a", GC["kv"], "pre1")

            def latent(s, norm):
                p = s.c0 % 2
                ended(s, 0)
                scaled(stg[:, p, 0, :], acc[p][0][:, :], "pre1", 0).then_inc(evac_act, 1)
                act.wait_ge(evac_act, s.c0 + 1)
                act.wait_ge(evac_dve, s.c0 + 1)
                squares(norm, 0, stg[:, p])
                sqrt_of(norm, width=LORA)

            s = S["ckv"]
            along(s, 0, join(his("x2b", ahi, GC["pre1"], {0: [0, 1], 1: [2, 3]}), his("x2a", bhi, GC["kv"], LAST), {4: [lambda: x_norm(0, "pre1")]},
                             his("x2b", ahi, GC["pre1"], {5: [4], 6: [5]})))
            act.wait_ge(sem("pre1_rs"), 1)
            latent(s, "kvl")
            s = S["krope"]
            along(s, 0)
            ended(s, 0)
            scaled(kraw[:, 0, 0, :], acc[s.c0 % 2][0][:, 0:ROPE], "pre1", 0)
            scaled(kraw[:, 0, 1, :], acc[s.c0 % 2][0][:, 0:ROPE], "pre1", 0).then_inc(evac_act, 1)
            s = S["cq"]
            along(s, 0, join(his("x2b", ahi, GC["pre1"], {0: [6], 1: [7]}), his("ckv", kvhi, GC["kvl"], {4: [0], 5: [1]})))
            latent(s, "ql")
            act.wait_ge(sem("kvl_rs"), 1)
            s = S["uk"]
            for j in range(4):
                p = (s.c0 + j) % 2
                along(s, j)
                ended(s, j)
                scaled(stg[:, p, 0, :], acc[p][0][:, :], "kvl", 0).then_inc(evac_act, 1)
                if j == 0:
                    for f in range(2):
                        hi_batch("cq", f, cqhi, GC["ql"])
            s = S["uv"]
            for j in range(4):
                p = (s.c0 + j) % 2
                along(s, j)
                ended(s, j)
                scaled(vB[:, 0, j * CH:(j + 1) * CH], acc[p][0][:, :], "kvl", 0).then_inc(evac_act, 1)

            s = S["uq"]
            act.wait_ge(sem("ql_rs"), 1)

            def q_chunk(j):
                split_to(s.u0 + (j + 1) * 2 + 3)
                ended(s, j)
                if j >= 2:
                    act.wait_ge(sem("q_roped"), j - 1)
                scaled(stg[:, j % 2, 0, 0:2 * QHEAD], acc[0][0][:, 0:2 * QHEAD], "ql", 0).then_inc(evac_act, 1)

            q_chunk(0)
            for c in range(8):
                for i in range(2):
                    h = 2 * c + i
                    act.wait_ge(sem("attB_mx"), h + 1)
                    act.activation(sB[:, i, 0:P], sB[:, i, 0:P], ACT.Exp, bias=mx[:, i, 0:1], accum_out=den[:, c % 2, 2 * i:2 * i + 1])
                    act.activation(sB[:, i, P:3 * P], sB[:, i, P:3 * P], ACT.Exp, bias=mx[:, i, 1:2],
                                   accum_out=den[:, c % 2, 2 * i + 1:2 * i + 2]).then_inc(sem("attB_p"), 1)
                if c < 7:
                    q_chunk(c + 1)
                for i in range(2):
                    act.wait_ge(sem("attB_t"), 2 * c + i + 1)
                    act.activation(pB[:, i, :], acc[1][i][:, 0:3 * P], ACT.Copy).then_inc(sem("attB_pt"), 1)
            s = S["gb"]
            for j in range(4):
                along(s, j)
                silu_chunk(s, j, "pre1")
            for f in range(3):
                hi_batch("ogB", f, bhi)
            post(1, "ogB", "x3", "x4", GC["norm1"], "norm1")
            for f in (6, 7):
                hi_batch("x4", f, bhi, GC["norm1"])
            x_norm(1, "norm1")

            for i in range(4):
                n = sq[0]
                sq[0] += 1
                if i == 0:
                    act.wait_ge(sem("meta_in"), 16)
                    act.wait_ge(sem("norm1_rs"), 1)
                act.wait_ge(sem("squares"), n - 1)
                act.activation(xb[n % 2][0:META, 0:CH], metax[0:META, i * CH:(i + 1) * CH], ACT.Square,
                               accum_out=ssq[0:META, 0, i:i + 1]).then_inc(sem("squares"), 1)
            act.wait_ge(sem("metan_ssum"), 1)
            act.activation(root[0:META, 0:1], ssum[0:META, 0:1], ACT.Sqrt, scale=1.0 / D, bias=eps[0:META, 0:1]).then_inc(sem("metan_root"), 1)
            act.wait_ge(sem("meta_zero"), 1)
            act.wait_ge(sem("meta_scaled"), 1)
            act.activation(metaT[:, :, 0:META], stg[:, 1, 0, 0:KT * META].rearrange("p (k m) -> p k m", m=META), ACT.Copy).then_inc(tp_hi, 1)

            def plain(name, j, dst, norm="norm1"):
                s = S[name]
                c = s.c0 + j
                split_to(s.u0 + (j + 1) * s.units + 3)
                ended(s, j)
                scaled(dst, acc[c % 2][0][:, 0:s.cols], norm, 0).then_inc(evac_act, 1)

            act.wait_ge(sem("glr_zero"), 1)
            plain("glr", 0, glr[:, 0, 0:GRANK])
            plain("k2", 0, kend[:, 0, :])
            plain("q2", 0, stg[:, 0, 0, :])
            for t in range(TT + 1):
                n = P if t < TT else META
                src = (tp[0], tp[1], xb[1])[t][0:n, :]
                dst = stg[:, 1, t, :] if t < TT else msc[0:META, :]
                act.wait_ge(sem("graw"), t + 1)
                act.activation(dst, src, ACT.Abs).then_inc(sem("lg"), 1)
                act.wait_ge(sem("lg"), 3 * t + 1)
                act.activation(dst, dst, ACT.Exp, scale=-1.0).then_inc(sem("lg"), 1)
                act.wait_ge(sem("lg"), 3 * t + 2)
                act.activation(dst, dst, ACT.Ln, bias=1.0).then_inc(sem("lg"), 1)
            plain("v2", 0, vC[:, 0, 0:CH])
            for t in range(TT):
                act.wait_ge(sem("G"), t + 1)
                act.wait_ge(sem("logg"), t + 1)
                act.activation(stg[:, 1, t, :], tp[t][:, :], ACT.Exp, scale=1.0 / TAU).then_inc(sem("eG"), 1)
                act.activation(nat[:, t, 0:CH], tp[t][:, :], ACT.Exp, scale=-1.0 / TAU).then_inc(sem("eG"), 1)
            for t in range(TT):
                act.wait_ge(sem("G"), 3 + t)
                act.activation(nat[:, t, CH:2 * CH], tp[t][:, :], ACT.Exp, scale=1.0 / TAU).then_inc(sem("eG"), 1)
            act.wait_ge(sem("G"), 5)
            act.activation(oneM[0:META, :], xb[0][0:META, :], ACT.Exp, scale=1.0 / TAU).then_inc(sem("eG"), 1)
            plain("v2", 1, vC[:, 0, CH:2 * CH])
            act.wait_ge(sem("G"), 6)
            act.activation(decay[:, :, :], xb[0][:, 0:4 * GLA_H].rearrange("p (h n) -> p h n", h=GLA_H), ACT.Exp, scale=1.0 / TAU).then_inc(sem("decay"), 1)
            for j in range(2):
                plain("pu", j, nat[:, 0, (2 + j) * CH:(3 + j) * CH])
            for h in range(GLA_H):
                act.wait_ge(sem("gla_o"), h + 1)
                for t in range(TT):
                    n = sq[0]
                    sq[0] += 1
                    act.wait_ge(sem("squares"), n)
                    act.activation(stg[:, 0, 0, 0:DV], nat[:, t, h * DV:(h + 1) * DV], ACT.Square,
                                   accum_out=ssum[:, t * GLA_H + h:t * GLA_H + h + 1]).then_inc(sem("squares"), 1)
            act.wait_ge(sem("squares"), sq[0])
            act.activation(root[:, :], ssum[:, :], ACT.Sqrt, scale=1.0 / DV, bias=eps_col).then_inc(sem("gla_root"), 1)
            s = S["r2"]
            for j in range(2):
                c, p = s.c0 + j, (s.c0 + j) % 2
                if j == 1:
                    split_to(s.u0 + s.units + 4)
                    for f in range(4):
                        hi_batch("pool", f, yhi)
                split_to(s.u0 + (j + 1) * s.units + 3)
                ended(s, j)
                for t in range(TT):
                    m = act.activation(stg[:, p, t, :], acc[p][t][:, :], ACT.Silu, scale=rs[:, RS["norm1"], t:t + 1])
                m.then_inc(evac_act, 1)
            s = S["pool"]
            for j in range(2):
                c = s.c0 + j
                split_to(s.u0 + j + 1 + 3)
                ended(s, j)
                act.activation(nat[:, 0, (2 + j) * CH:(3 + j) * CH], acc[c % 2][0][:, :], ACT.Copy).then_inc(evac_act, 1)
            for f in range(8):
                n = BATCH["mixed", f][0]
                act.wait_ge(tp_full, n + 1)
                src = tp[n % 2][:, :].rearrange("p (i t) -> p i t", i=2)
                for i in range(2):
                    g = GC["gla"] + i if f < 4 else GC["pool"] + 2 * (f - 4) + i
                    m = act.activation(ahi[:, 2 * f + i, :], src[:, i, :], ACT.Copy, scale=gcol[:, g:g + 1])
                m.then_inc(tp_hi, 1)

            def added(s, j):
                c, p = s.c0 + j, (s.c0 + j) % 2
                split_to(min(s.u0 + (j + 1) * s.units + 3, units))
                ended(s, j)
                act.activation(stg[:, p, 0, :], acc[p][0][:, :], ACT.Copy).then_inc(evac_act, 1)

            s = S["out2"]
            for j in range(4):
                def last_squares(j=j):
                    act.wait_ge(evac_dve, s.c0 + j)
                    squares("norm2", j - 1, x)
                along(s, j, join({4: [last_squares]}, his("x5", bhi, GC["norm2"], ALONG[j])) if j else {})
                added(s, j)

            def x5_norm():
                act.wait_ge(evac_dve, S["out2"].c0 + 4)
                squares("norm2", 3, x)
                sqrt_of("norm2")
            for q in range(DFF // D):
                s = S[f"up{q}"]
                for j in range(4):
                    p = (s.c0 + j) % 2
                    first_x = q == 0 and j == 0
                    along(s, j, his(f"mlp{q}", ahi, None, ALONG[j]) if j else join(his("x5", bhi, GC["norm2"], LAST), {4: [x5_norm]}) if first_x else {})
                    if first_x:
                        act.wait_ge(sem("norm2_rs"), 1)
                    ended(s, j)
                    n = 4 * q + j
                    act.activation(stg[:, p, 0, :], acc[p][0][:, :], ACT.Relu, scale=rs[:, RS["norm2"], 0:1]).then_inc(sem("relu"), 1)
                    act.wait_ge(sem("relu"), n + 1)
                    act.activation(stg[:, p, 0, :], stg[:, p, 0, :], ACT.Square).then_inc(evac_act, 1)
                for j in range(4):
                    along(S[f"down{q}"], j, his(f"mlp{q}", ahi, None, LAST) if j == 0 else {})
                    added(S[f"down{q}"], j)
                    if q == DFF // D - 1:
                        act.wait_ge(evac_dve, S[f"down{q}"].c0 + j + 1)
                        squares("final", j, x)
            sqrt_of("final")

        @block.vector
        def _(dve):
            ptr = [0]
            def split_to(target, r=0):
                for u in range(ptr[0], target):
                    kt, cols = shape_of(u)
                    n = kt * cols
                    dve.wait_ge(hi_done, u + 1 + r)
                    dve.tensor_tensor(wlo[:, u % RING, 0:n], raw[:, u % RING, 0:n], whi[:, u % RING, 0:n].bitcast(F32),
                                      ALU.subtract).then_inc(lo_done, 1)
                ptr[0] = max(ptr[0], target)

            def along(s, j, hooks={}, r=0):
                for uu in range(s.units):
                    split_to(min(s.u0 + j * s.units + uu + 4, units), r)
                    for hook in hooks.get(uu, []):
                        hook()

            def los(name, hi, lo, gain, plan):
                return {uu: [lambda f=f: lo_batch(name, f, hi, lo, gain) for f in fs] for uu, fs in plan.items()}

            def copies(name, dst, plan):
                return {uu: [lambda f=f: copy_batch(name, f, dst[:, 2 * f:2 * f + 2, :]) for f in fs] for uu, fs in plan.items()}

            def ended(s, j, r=0):
                dve.wait_ge(unit_used, s.u0 + (j + 1) * s.units + r)

            def bank(n):
                return tp[n % 2][:, :].rearrange("p (i t) -> p i t", i=2)

            def lo_batch(name, f, hi, lo, gain=None):
                n, k = BATCH[name, f]
                dve.wait_ge(tp_hi, k + 1)
                tiles = slice(2 * f, 2 * f + 2)
                if gain is None:
                    m = dve.tensor_tensor(lo[:, tiles, :], bank(n), hi[:, tiles, :].bitcast(F32), ALU.subtract)
                else:
                    for i in range(2):
                        g = gain(f, i) if callable(gain) else gain + 2 * f + i
                        m = dve.scalar_tensor_tensor(out=lo[:, 2 * f + i, :], in0=bank(n)[:, i, :], scalar=gcol[:, g:g + 1],
                                                     in1=hi[:, 2 * f + i, :].bitcast(F32), op0=ALU.mult, op1=ALU.subtract)
                m.then_inc(tp_done, 1)

            def copy_batch(name, f, dst, r=0):
                n = BATCH[name, f][0]
                dve.wait_ge(tp_full, n + 1 + r)
                dve.tensor_copy(dst, bank(n)).then_inc(tp_done, 1)

            def scaled(dst, src, norm, t):
                return dve.tensor_scalar(dst, src, rs[:, RS[norm], t:t + 1], None, ALU.mult)

            def sum_squares(norm, squares_done, quarters=4):
                dve.wait_ge(sem("squares"), squares_done)
                dve.tensor_reduce(ssum[:, 0:TT], ssq[:, :, 0:quarters], AX, ALU.add).then_inc(sem(f"{norm}_ssum"), 1)

            def inverse_root(norm):
                dve.wait_ge(sem(f"{norm}_root"), 1)
                dve.reciprocal(rs[:, RS[norm.rstrip("01") if norm.startswith("post") else norm], 0:TT], root[:, 0:TT]).then_inc(sem(f"{norm}_rs"), 1)

            sq = [0]

            def norm_of(norm, n=8, quarters=4):
                sq[0] += n
                sum_squares(norm, sq[0], quarters)
                inverse_root(norm)

            dve.memset(eps[:, :], EPS).then_inc(sem("eps_set"), 1)
            n = BATCH["gcol", 0][0]
            dve.wait_ge(tp_full, n + 1)
            dve.tensor_copy(gcol[:, 0:98], tp[n % 2][:, 0:98]).then_inc(tp_done, 1)
            dve.wait_ge(tp_done, 1)
            for f in range(3):
                lo_batch("x0", f, ahi, alo, GC["pre0"])
                split_to(f + 1)
            s = S["qk"]
            for uu in range(1, s.units):
                if uu < 6:
                    lo_batch("x0", uu + 2, ahi, alo, GC["pre0"])
                else:
                    n, k = BATCH["p", uu - 6]
                    dve.wait_ge(tp_hi, k + 1)
                    dve.tensor_tensor(plo[:, uu - 6], bank(n), phi[:, uu - 6].bitcast(F32), ALU.subtract).then_inc(tp_done, 1)
                split_to(s.u0 + uu + 3)
            norm_of("pre0")
            dve.wait_ge(sem("pre0_rs"), 1)

            s = S["qk"]

            def qk_chunk(q, i=None):
                r = 0 if i is None else i * (2 * s.units)
                rb = 0 if i is None else i * 4
                def turned():
                    for f in (2 * q - 2, 2 * q - 1):
                        at = 2 * f if i is None else 2 * f + i * 8
                        copy_batch("qk", f, qkT[:, bass.ds(at, 2), :], rb)
                along(s, q, {4: [turned]} if q else {}, r)
                ended(s, q, r)
                scaled(stg[:, q % 2, 1, :], acc[q % 2][1][:, :], "pre0", 1).then_inc(evac_dve, 1)

            qk_chunk(0)
            qk_chunk(1)
            with dve.Fori(0, 3) as i:
                first = ptr[0]
                for q in (2, 3):
                    qk_chunk(q, i)
            ptr[0] = first + 3 * 2 * s.units

            def diagonal(a, p):
                return a[:, p, :].rearrange("p (b q) -> p b q", b=3)[:, 0:3:2, :]

            def blocks(name):
                return const_of(name)[:, None, :].to_broadcast((P, 2, P))

            def softplus(h, r=0):
                p = h % 2
                dve.wait_ge(sem("attA_t"), 3 * (h + 1) + 3 * r)
                dve.scalar_tensor_tensor(out=tA[:, p, :], in0=zA[:, p, :], scalar=0.0, in1=tA[:, p, :], op0=ALU.max,
                                         op1=ALU.add).then_inc(sem("attA_m"), 1)
                dve.wait_ge(sem("attA_m"), h + 1 + r)
                dve.tensor_tensor(diagonal(tA, p), diagonal(tA, p), blocks("strict"), ALU.mult).then_inc(sem("attA_sp"), 1)
                dve.tensor_tensor(diagonal(zA, p), diagonal(zA, p), blocks("strict_neg"), ALU.add).then_inc(sem("attA_n"), 1)

            def less_sums(h, r=0):
                p = h % 2
                dve.wait_ge(sem("attA_sums"), h + 1 + r)
                dve.wait_ge(sem("attA_n"), h + 1 + r)
                dve.tensor_tensor(zA[:, p, :], zA[:, p, :], xb[1][:, 0:3 * P], ALU.subtract).then_inc(sem("attA_d"), 1)

            def head_out(h, r=0):
                dve.wait_ge(sem("attA_out"), h + 1 + r)
                at = h * HD if isinstance(r, int) else r * HD + h * HD
                dve.tensor_copy(nat[:, :, bass.ds(at, HD)], tp[h % 2][:, 0:SEQ].rearrange("p (t d) -> p t d", t=TT)).then_inc(sem("attA_o"), 1)

            def attention_of(n):
                def part(m):
                    h = m // 3
                    if m % 3 == 0 and 1 <= h <= HEADS:
                        less_sums(h - 1)
                    if m % 3 == 1 and h < HEADS:
                        softplus(h)
                    if m % 3 == 2 and 1 <= h <= HEADS:
                        head_out(h - 1)
                return {uu: [lambda m=8 * n + uu: part(m)] for uu in range(8)}

            s = S["v"]
            for j in range(4):
                if j == 1:
                    dve.wait_ge(sem("tab_in"), 16)
                along(s, j, attention_of(j - 1) if j else copies("qk", qkT, {4: [14, 15]}))
                ended(s, j)
                scaled(vA[:, 1, j * CH:(j + 1) * CH], acc[(s.c0 + j) % 2][1][:, :], "pre0", 1).then_inc(evac_dve, 1)

            def gated(s, j, outputs_done, n):
                c, p = s.c0 + j, (s.c0 + j) % 2
                dve.wait_ge(evac_act, c + 1)
                dve.wait_ge(outputs_done, n)
                cols = slice(j * CH, (j + 1) * CH)
                dve.tensor_tensor(nat[:, :, cols], nat[:, :, cols], stg[:, p, :, :], ALU.mult).then_inc(evac_dve, 1)

            s = S["g"]
            for j in range(4):
                along(s, j, join(attention_of(3 + j), los("ogA", bhi, blo, None, OG_EARLY) if j == 3 else {}))
                gated(s, j, sem("attA_o"), 4 * (j + 1))

            def post(layer, y, x1, x2, gain, norms):
                s = S[f"out_{'ab'[layer]}"]
                for j in range(4):
                    p = (s.c0 + j) % 2
                    along(s, j, los(y, bhi, blo, None, OG_LATE if layer == 0 else SPREAD) if j == 0 else {})
                    ended(s, j)
                    dve.tensor_copy(nat[:, 1, j * CH:(j + 1) * CH], acc[p][1][:, :]).then_inc(evac_dve, 1)
                norm_of(f"post{layer}")
                dve.wait_ge(sem(f"post{layer}_rs"), 1)
                dve.wait_ge(sem(f"post_in{layer}"), 16)
                s = S[f"ple{layer}"]
                for j in range(4):
                    p = (s.c0 + j) % 2
                    split_to(s.u0 + j + 4)
                    ended(s, j)
                    dve.tensor_copy(pp[:, 1, j * CH:(j + 1) * CH], acc[p][1][:, :]).then_inc(evac_dve, 1)
                    for t in range(TT):
                        yq = nat[:, t, j * CH:(j + 1) * CH]
                        dve.scalar_tensor_tensor(out=yq, in0=yq, scalar=rs[:, RS["post"], t:t + 1], in1=gains[:, j * CH:(j + 1) * CH],
                                                 op0=ALU.mult, op1=ALU.mult).then_inc(sem(f"post{layer}_y"), 1)
                    for t in range(TT):
                        xq = x[:, t, j * CH:(j + 1) * CH]
                        dve.wait_ge(sem(f"post{layer}_y"), TT * j + t + 1)
                        m = dve.tensor_tensor(xq, xq, nat[:, t, j * CH:(j + 1) * CH], ALU.add)
                    m.then_inc(x_done, 1)
                for f in range(3):
                    lo_batch(x1, f, ahi, alo)
                s = S[f"gate{layer}"]
                for j in range(4):
                    c, p = s.c0 + j, (s.c0 + j) % 2
                    along(s, j, los(x2, bhi, blo, gain, ALONG[j]) if j else los(x1, ahi, alo, None, SPREAD))
                    dve.wait_ge(evac_act, c + 1)
                    cols = slice(j * CH, (j + 1) * CH)
                    dve.tensor_tensor(pp[:, :, cols], pp[:, :, cols], stg[:, p, :, :], ALU.mult).then_inc(evac_dve, 1)
                    dve.wait_ge(evac_dve, c + 1)
                    dve.tensor_tensor(x[:, :, cols], x[:, :, cols], pp[:, :, cols], ALU.add).then_inc(x_done, 1)

            post(0, "ogA", "x1", "x2a", GC["kv"], "pre1")

            def latent(s, norm):
                p = s.c0 % 2
                ended(s, 0)
                scaled(stg[:, p, 1, :], acc[p][1][:, :], "pre1", 1).then_inc(evac_dve, 1)
                norm_of(norm, 2, 1)

            s = S["ckv"]
            along(s, 0, join(los("x2b", ahi, alo, GC["pre1"], {0: [0, 1], 1: [2, 3]}), los("x2a", bhi, blo, GC["kv"], LAST), {4: [lambda: norm_of("pre1")]},
                             los("x2b", ahi, alo, GC["pre1"], {5: [4], 6: [5]})))
            dve.wait_ge(sem("pre1_rs"), 1)
            latent(s, "kvl")
            s = S["krope"]
            along(s, 0)
            ended(s, 0)
            scaled(kraw[:, 1, 0, :], acc[s.c0 % 2][1][:, 0:ROPE], "pre1", 1)
            scaled(kraw[:, 1, 1, :], acc[s.c0 % 2][1][:, 0:ROPE], "pre1", 1).then_inc(evac_dve, 1)
            s = S["cq"]
            n = BATCH["kr", 0][0]

            def k_rope_out():
                dve.wait_ge(tp_full, n + 1)
                dve.tensor_copy(krT[:, :], tp[n % 2][:, 0:SEQ]).then_inc(tp_done, 1)
            along(s, 0, join(los("x2b", ahi, alo, GC["pre1"], {0: [6], 1: [7]}), los("ckv", kvhi, kvlo, GC["kvl"], {4: [0], 5: [1]}), {7: [k_rope_out]}))
            latent(s, "ql")
            s = S["uk"]
            for j in range(4):
                p = (s.c0 + j) % 2
                along(s, j)
                ended(s, j)
                scaled(stg[:, p, 1, :], acc[p][1][:, :], "kvl", 1).then_inc(evac_dve, 1)
                if j:
                    for f in (2 * j - 2, 2 * j - 1):
                        copy_batch("uk", f, knT[:, 2 * f:2 * f + 2, :])
                if j == 0:
                    for f in range(2):
                        lo_batch("cq", f, cqhi, cqlo, GC["ql"])
            s = S["uv"]
            for j in range(4):
                p = (s.c0 + j) % 2
                along(s, j)
                ended(s, j)
                scaled(vB[:, 1, j * CH:(j + 1) * CH], acc[p][1][:, :], "kvl", 1).then_inc(evac_dve, 1)
                if j == 0:
                    for f in (6, 7):
                        copy_batch("uk", f, knT[:, 2 * f:2 * f + 2, :])

            s = S["uq"]

            def q_chunk(j):
                split_to(s.u0 + (j + 1) * 2 + 3)
                ended(s, j)
                if j >= 2:
                    dve.wait_ge(sem("q_roped"), j - 1)
                scaled(stg[:, j % 2, 1, 0:2 * QHEAD], acc[0][1][:, 0:2 * QHEAD], "ql", 1).then_inc(evac_dve, 1)
                if j >= 2:
                    dve.wait_ge(sem("attB_s"), 2 * (j - 1))
                copy_batch("uq", 2 * j, qn[:, j % 2])
                n = BATCH["uq", 2 * j + 1][0]
                dve.wait_ge(tp_full, n + 1)
                dve.tensor_copy(qr[:, j % 2, :], tp[n % 2][:, 0:SEQ]).then_inc(tp_done, 1)

            q_chunk(0)
            for c in range(8):
                for i in range(2):
                    h = 2 * c + i
                    dve.wait_ge(sem("attB_s"), 2 * c + i + 1)
                    if h >= 2:
                        dve.wait_ge(sem("attB_t"), h - 1)
                    dve.scalar_tensor_tensor(out=sB[:, i, :], in0=xb[i][:, 0:3 * P], scalar=QHEAD ** -0.5, in1=const_of("chunk_neg"),
                                             op0=ALU.mult, op1=ALU.add).then_inc(sem("attB_m"), 1)
                    dve.wait_ge(sem("attB_m"), h + 1)
                    dve.tensor_reduce(mx[:, i, 0:1], sB[:, i, 0:P], AX, ALU.max, negate=True)
                    dve.tensor_reduce(mx[:, i, 1:2], sB[:, i, P:3 * P], AX, ALU.max, negate=True).then_inc(sem("attB_mx"), 1)
                if c < 7:
                    q_chunk(c + 1)
                dve.wait_ge(sem("attB_out"), c + 1)
                dve.reciprocal(rden[:, c % 2, :], den[:, c % 2, :]).then_inc(sem("attB_r"), 1)
                dve.wait_ge(sem("attB_r"), c + 1)
                dve.tensor_tensor(nat[:, :, c * 2 * HD:(c + 1) * 2 * HD].rearrange("p t (i d) -> p i t d", i=2),
                                  acc[1][0][:, :].rearrange("p (i t d) -> p i t d", i=2, t=TT),
                                  rden[:, c % 2, :].rearrange("p (i t) -> p i t", i=2)[:, :, :, None].to_broadcast((P, 2, TT, HD)),
                                  ALU.mult).then_inc(sem("attB_o"), 1)
            s = S["gb"]
            for j in range(4):
                along(s, j)
                gated(s, j, sem("attB_o"), HEADS // 2)
            for f in range(3):
                lo_batch("ogB", f, bhi, blo)
            post(1, "ogB", "x3", "x4", GC["norm1"], "norm1")
            for f in (6, 7):
                lo_batch("x4", f, bhi, blo, GC["norm1"])
            norm_of("norm1")

            sq[0] += 4
            dve.wait_ge(sem("squares"), sq[0])
            dve.tensor_reduce(ssum[0:META, 0:1], ssq[0:META, 0, :], AX, ALU.add).then_inc(sem("metan_ssum"), 1)
            dve.wait_ge(sem("metan_root"), 1)
            rsM = rs[0:META, 7, 0:1]
            dve.reciprocal(rsM, root[0:META, 0:1]).then_inc(sem("metan_rs"), 1)
            n, k = BATCH["meta", 0]
            dve.wait_ge(tp_full, n + 1)
            scaledM = stg[:, 1, 0, 0:KT * META].rearrange("p (k m) -> p k m", m=META)
            dve.tensor_tensor(scaledM, tp[n % 2][:, 0:KT * META].rearrange("p (k m) -> p k m", m=META),
                              gcol[:, GC["norm1"]:GC["norm1"] + KT][:, :, None].to_broadcast((P, KT, META)), ALU.mult).then_inc(sem("meta_scaled"), 1)
            dve.wait_ge(tp_hi, k + 1)
            dve.tensor_tensor(metaT[:, :, 32:32 + META], scaledM, metaT[:, :, 0:META].bitcast(F32), ALU.subtract).then_inc(tp_done, 1)
            dve.wait_ge(sem("metan_rs"), 1)
            dve.wait_ge(sem("norm1_rs"), 1)
            metas = [0]

            def plain(name, j, dst, meta=None):
                s = S[name]
                c = s.c0 + j
                split_to(s.u0 + (j + 1) * s.units + 3)
                ended(s, j)
                m = scaled(dst, acc[c % 2][1][:, 0:s.cols], "norm1", 1)
                if meta is not None:
                    k = metas[0]
                    metas[0] += 1
                    tmp = msc[0:META, 0:s.cols]
                    if k:
                        dve.wait_ge(evac_dve, c)
                    dve.tensor_copy(tmp, xb[c % 2][32:32 + META, 0:s.cols]).then_inc(sem("meta_step"), 1)
                    dve.wait_ge(sem("meta_step"), 2 * k + 1)
                    dve.tensor_tensor(tmp, xb[c % 2][0:META, 0:s.cols], tmp, ALU.add).then_inc(sem("meta_step"), 1)
                    dve.wait_ge(sem("meta_step"), 2 * k + 2)
                    m = dve.tensor_scalar(meta, tmp, rsM, None, ALU.mult)
                m.then_inc(evac_dve, 1)

            dve.wait_ge(sem("glr_zero"), 1)
            plain("glr", 0, glr[:, 1, 0:GRANK], glrM[0:META, 0:GRANK])
            plain("k2", 0, kend[:, 1, :], kendM[0:META, :])
            n = BATCH["glr", 0][0]
            dve.wait_ge(tp_full, n + 1)
            dve.tensor_copy(glrT[:, :], tp[n % 2][:, 0:SEQ + META]).then_inc(tp_done, 1)
            plain("q2", 0, stg[:, 0, 1, :])
            for t in range(TT + 1):
                n = P if t < TT else META
                src = (tp[0], tp[1], xb[1])[t][0:n, :]
                soft = stg[:, 1, t, :] if t < TT else msc[0:META, :]
                dst = logg[:, t, :] if t < TT else loggM[0:META, :]
                dve.wait_ge(sem("lg"), 3 * t + 3)
                dve.scalar_tensor_tensor(out=dst, in0=src, scalar=0.0, in1=soft, op0=ALU.min, op1=ALU.subtract).then_inc(sem("logg"), 1)
            plain("v2", 0, vC[:, 1, 0:CH], vM[0:META, 0:CH])
            dve.wait_ge(sem("eG"), 4)
            dve.wait_ge(evac_act, S["q2"].c0 + 1)
            dve.tensor_tensor(nat[:, :, 0:CH], nat[:, :, 0:CH], kend[:, :, :], ALU.mult).then_inc(sem("kinv"), 1)
            dve.scalar_tensor_tensor(out=stg[:, 0, :, :], in0=stg[:, 0, :, :], scalar=DK ** -0.5, in1=stg[:, 1, :, :],
                                     op0=ALU.mult, op1=ALU.mult).then_inc(sem("qdec"), 1)
            dve.wait_ge(sem("eG"), 7)
            dve.tensor_tensor(kend[:, :, :], kend[:, :, :], nat[:, :, CH:2 * CH], ALU.mult).then_inc(sem("kend"), 1)
            dve.tensor_tensor(kendM[0:META, :], kendM[0:META, :], oneM[0:META, :], ALU.mult).then_inc(sem("kend"), 1)
            plain("v2", 1, vC[:, 1, CH:2 * CH], vM[0:META, CH:2 * CH])
            for f in range(2):
                copy_batch("kinv", f, kTc[:, 2 * f:2 * f + 2, :])
            dve.wait_ge(sem("q_zero"), 1)
            for f in range(2):
                n = BATCH["qdec", f][0]
                dve.wait_ge(tp_full, n + 1)
                src = tp[n % 2][:, :].rearrange("p (i t q) -> p i t q", i=2, t=TT)
                dve.tensor_copy(qA[:, 2 * f:2 * f + 2, :, 0:64], src[:, :, :, 0:64])
                dve.tensor_copy(qB[:, 2 * f:2 * f + 2, :, 64:P], src[:, :, :, 64:P]).then_inc(tp_done, 1)
            for j in range(2):
                plain("pu", j, nat[:, 1, (2 + j) * CH:(3 + j) * CH], puM[0:META, j * CH:(j + 1) * CH])

            dve.wait_ge(sem("decay"), 1)
            for h in range(GLA_H):
                dve.wait_ge(sem("gla_scores"), h + 1)
                if h:
                    dve.wait_ge(sem("gla_out"), h)
                dve.tensor_scalar(sc[:, :, :], tp[0][:, 0:SEQ].rearrange("p (t c) -> p t c", t=TT), 3e38, -3e38, ALU.min, ALU.max).then_inc(sem("gla_clip"), 1)
                dve.wait_ge(sem("gla_clip"), h + 1)
                dve.tensor_tensor(sc[:, :, :], sc[:, :, :], const_of("gla_causal")[:, None, :].to_broadcast((P, TT, P)), ALU.mult).then_inc(sem("gla_sc"), 1)
                dve.wait_ge(sem("gla_ds"), h + 1)
                st = state[:, h % 2]
                dve.tensor_copy(st[:, 0, :], xb[1][:, DV:2 * DV]).then_inc(sem("gla_step"), 1)
                for n, (src, half) in enumerate(((xb[0], 0), (xb[1], 0), (xb[0], 1))):
                    dve.wait_ge(sem("gla_step"), 3 * h + n + 1)
                    m = dve.scalar_tensor_tensor(out=st[:, n + 1, :], in0=st[:, n, :], scalar=decay[:, h, n:n + 1],
                                                 in1=src[:, half * DV:(half + 1) * DV], op0=ALU.mult, op1=ALU.add)
                    m.then_inc(sem("gla_step") if n < 2 else sem("gla_state"), 1)
                dve.wait_ge(sem("gla_out"), h + 1)
                dve.tensor_copy(nat[:, :, h * DV:(h + 1) * DV], tp[1][:, :].rearrange("p (t d) -> p t d", t=TT)).then_inc(sem("gla_o"), 1)
            sq[0] += 2 * GLA_H
            dve.wait_ge(sem("gla_root"), 1)
            dve.reciprocal(rs[:, 6, :], root[:, :]).then_inc(sem("gla_rs"), 1)
            dve.wait_ge(sem("gla_rs"), 1)
            s = S["r2"]
            for j in range(2):
                c, p = s.c0 + j, (s.c0 + j) % 2
                if j == 1:
                    split_to(s.u0 + s.units + 4)
                    for f in range(4):
                        lo_batch("pool", f, yhi, ylo)
                split_to(s.u0 + (j + 1) * s.units + 3)
                dve.wait_ge(evac_act, c + 1)
                for t in range(TT):
                    for i in range(2):
                        h = 2 * j + i
                        o = nat[:, t, h * DV:(h + 1) * DV]
                        dve.wait_ge(sem("squares"), sq[0])
                        m = dve.scalar_tensor_tensor(out=o, in0=o, scalar=rs[:, 6, t * GLA_H + h:t * GLA_H + h + 1],
                                                     in1=stg[:, p, t, i * DV:(i + 1) * DV], op0=ALU.mult, op1=ALU.mult)
                m.then_inc(evac_dve, 1)
            s = S["pool"]
            for j in range(2):
                c = s.c0 + j
                split_to(s.u0 + j + 1 + 3)
                ended(s, j)
                dve.tensor_copy(nat[:, 1, (2 + j) * CH:(3 + j) * CH], acc[c % 2][1][:, :]).then_inc(evac_dve, 1)
            for f in range(8):
                lo_batch("mixed", f, ahi, alo, lambda f, i: GC["gla"] + i if f < 4 else GC["pool"] + 2 * (f - 4) + i)

            def added(s, j):
                c, p = s.c0 + j, (s.c0 + j) % 2
                split_to(min(s.u0 + (j + 1) * s.units + 3, units))
                dve.wait_ge(evac_act, c + 1)
                x0, x1 = (x[:, t, j * CH:(j + 1) * CH] for t in range(TT))
                dve.tensor_tensor(x0, x0, stg[:, p, 0, :], ALU.add)
                dve.tensor_tensor(x1, x1, acc[p][1][:, :], ALU.add).then_inc(evac_dve, 1)

            for j in range(4):
                along(S["out2"], j, los("x5", bhi, blo, GC["norm2"], ALONG[j]) if j else {})
                added(S["out2"], j)
            for q in range(DFF // D):
                s = S[f"up{q}"]
                for j in range(4):
                    p = (s.c0 + j) % 2
                    first_x = q == 0 and j == 0
                    along(s, j, los(f"mlp{q}", ahi, alo, None, ALONG[j]) if j else
                          join(los("x5", bhi, blo, GC["norm2"], LAST), {4: [lambda: norm_of("norm2")]}) if first_x else {})
                    if first_x:
                        dve.wait_ge(sem("norm2_rs"), 1)
                    ended(s, j)
                    n = 4 * q + j
                    dve.tensor_scalar(stg[:, p, 1, :], acc[p][1][:, :], rs[:, RS["norm2"], 1:2], 0.0, ALU.mult, ALU.max).then_inc(sem("relu_dve"), 1)
                    dve.wait_ge(sem("relu_dve"), n + 1)
                    dve.tensor_tensor(stg[:, p, 1, :], stg[:, p, 1, :], stg[:, p, 1, :], ALU.mult).then_inc(evac_dve, 1)
                for j in range(4):
                    along(S[f"down{q}"], j, los(f"mlp{q}", ahi, alo, None, LAST) if j == 0 else {})
                    added(S[f"down{q}"], j)
            norm_of("final")
            dve.wait_ge(sem("final_rs"), 1)
            dve.wait_ge(sem("final_in"), 16)
            for j in range(NCH):
                for t in range(TT):
                    dve.scalar_tensor_tensor(out=nat[:, t, j * CH:(j + 1) * CH], in0=x[:, t, j * CH:(j + 1) * CH],
                                             scalar=rs[:, RS["final"], t:t + 1], in1=gains[:, j * CH:(j + 1) * CH],
                                             op0=ALU.mult, op1=ALU.mult).then_inc(sem("final_y"), 1)

        @block.gpsimd
        def _(pool):
            step = [0]
            cos = const_of("cos").rearrange("p (t i c) -> p t i c", t=TT, i=2)
            sin = const_of("sin").rearrange("p (t i c) -> p t i c", t=TT, i=2)
            dst = roped[:, :, :].rearrange("p t (i c) -> p t i c", i=2)
            half = ROPE // 2

            def op(out_, a, b_, f):
                pool.tensor_tensor(out_, a, b_, f).then_inc(sem("rope_step"), 1)
                step[0] += 1
                pool.wait_ge(sem("rope_step"), step[0])

            def rotate(a, b_):
                op(dst[:, :, :, 0:half], a, cos, ALU.mult)
                op(turn[:, :, :, :], b_, sin, ALU.mult)
                op(dst[:, :, :, 0:half], dst[:, :, :, 0:half], turn[:, :, :, :], ALU.subtract)
                op(dst[:, :, :, half:ROPE], a, sin, ALU.mult)
                op(turn[:, :, :, :], b_, cos, ALU.mult)
                return pool.tensor_tensor(dst[:, :, :, half:ROPE], dst[:, :, :, half:ROPE], turn[:, :, :, :], ALU.add)

            pool.wait_ge(sem("tab_in"), 16)
            s = S["krope"]
            pool.wait_ge(evac_act, s.c0 + 1)
            pool.wait_ge(evac_dve, s.c0 + 1)
            rotate(kraw[:, :, :, 0:half], kraw[:, :, :, half:ROPE]).then_inc(sem("k_roped"), 1)
            s = S["uq"]
            for j in range(s.chunks):
                pool.wait_ge(evac_act, s.c0 + j + 1)
                pool.wait_ge(evac_dve, s.c0 + j + 1)
                pool.wait_ge(sem("q_roped") if j else sem("k_roped"), max(j, 1))
                pool.wait_ge(tp_full, BATCH["uq", 2 * j][0] if j else BATCH["kr", 0][0] + 1)
                q = stg[:, j % 2, :, 0:2 * QHEAD].rearrange("p t (i c) -> p t i c", i=2)
                rotate(q[:, :, :, HD:HD + half], q[:, :, :, HD + half:QHEAD]).then_inc(sem("q_roped"), 1)
            pool.wait_ge(x_done, 16)
            pool.memset(metaT[:, :, :].bitcast(F32), 0.0).then_inc(sem("meta_zero"), 1)
            pool.memset(glr[:, :, :], 0.0)
            pool.memset(glrM[:, :], 0.0).then_inc(sem("glr_zero"), 1)
            pool.memset(qA[:, :, :, :], 0.0)
            pool.memset(qB[:, :, :, :], 0.0).then_inc(sem("q_zero"), 1)


_INS = ["x", "p", "norm_pre", "norm_post", "w_in_a", "w_out_a", "w_in_b", "q_latent_norm", "w_uq", "w_out_b", "kv_norm",
        "w_dkv", "kv_latent_norm", "w_uk", "w_uv", "w_ple_proj", "w_ple_gate", "meta_tokens_2", "norm1_w_2", "w_in_2",
        "gate_w2_2", "gate_b_2", "gla_norm_w_2", "pool_w_2", "pool_scale_2", "w_out_2", "norm2_w_2", "mlp_w1_2",
        "mlp_w2_2", "final_norm_w_2"]


def kernel(**inputs):
    import numpy as _np
    import concourse.bacc as _bacc
    from concourse import mybir as _mybir
    from concourse.bass_utils import run_bass_kernel_spmd as _run

    nc = _bacc.Bacc("TRN2", target_bir_lowering=False, num_devices=1)
    arrays, w = {}, {}
    for name in _INS:
        a = _np.ascontiguousarray(inputs[name])
        arrays[f"in_{name}"] = a
        w[name] = nc.dram_tensor(f"in_{name}", a.shape, _mybir.dt.from_np(a.dtype), kind="ExternalInput").ap()
    table, _ = constants()
    arrays["tables"] = table
    const = nc.dram_tensor("tables", table.shape, F32, kind="ExternalInput").ap()
    out = nc.dram_tensor("out_0", (1, SEQ, D), F32, kind="ExternalOutput").ap()
    build(nc, w, const, out)
    r = _run(nc, [arrays], core_ids=[0])
    return r.results[0]["out_0"]
```

```python
from contextlib import ExitStack

import numpy as np
import concourse.bass as bass
from concourse import mybir

F32 = mybir.dt.float32
F32R = mybir.dt.float32r
ALU = mybir.AluOpType
ACT = mybir.ActivationFunctionType
AX = mybir.AxisListType.X

P = 128
SEQ = 256
TT = SEQ // P
D = 2048
KT = D // P
CH = 512
NCH = D // CH
QT = CH // P
EPS = 1e-6
NEG = -1e30

HEADS = 16
HD = 128
ROPE = 64
LORA = 512
LK = LORA // P
QHEAD = HD + ROPE
CHUNK = 64

META = 16
GLA_H = 4
DK = 128
DV = 256
GKW = GLA_H * DK
GRANK = 16
TAU = 16.0
WINDOWS = (2, 4, 8, 16)
PGC = 256
DFF = 4 * D

LAST = {3: [6], 4: [7]}
SPREAD = {1: [3], 2: [4], 3: [5], 4: [6], 5: [7]}
OG_EARLY, OG_LATE = {5: [0], 6: [1], 7: [2]}, {0: [3], 1: [4], 2: [5], 3: [6], 4: [7]}
MIXED_LATE = {1: [4], 2: [5], 3: [6], 4: [7]}
ALONG = {1: {4: [0], 5: [1]}, 2: {4: [2], 5: [3]}, 3: {4: [4], 5: [5]}}

UNIT = 1024
RING = 4


class Stage:

    def __init__(self, name, weight, chunks, units, kt, cols):
        self.name, self.weight, self.chunks, self.units, self.kt, self.cols = name, weight, chunks, units, kt, cols
        self.u0 = self.c0 = 0


def plan():
    deep = KT // 2
    st = [
        Stage("qk", "w_in_a", 8, deep, 2, CH), Stage("v", "w_in_a", 4, deep, 2, CH),
        Stage("g", "w_in_a", 4, deep, 2, CH), Stage("out_a", "w_out_a", 4, deep, 2, CH),
        Stage("ple0", "w_ple_proj", 4, 1, 2, CH), Stage("gate0", "w_ple_gate", 4, deep, 2, CH),
        Stage("ckv", "w_dkv", 1, deep, 2, CH), Stage("krope", "w_dkv", 1, 1, KT, ROPE),
        Stage("cq", "w_in_b", 1, deep, 2, CH), Stage("uk", "w_uk", 4, 2, 2, CH), Stage("uv", "w_uv", 4, 2, 2, CH),
        Stage("uq", "w_uq", 1, 2, 2, 2 * QHEAD), Stage("attb", None, 11, 46, 2, CH),
        Stage("out_b", "w_out_b", 4, deep, 2, CH), Stage("ple1", "w_ple_proj", 4, 1, 2, CH),
        Stage("gate1", "w_ple_gate", 4, deep, 2, CH),
        Stage("k2", "w_in_2", 1, deep, 2, CH), Stage("glr", "w_in_2", 1, 1, KT, GRANK),
        Stage("pu0", "w_in_2", 1, deep, 2, CH), Stage("q2", "w_in_2", 1, deep, 2, CH),
        Stage("pu1", "w_in_2", 1, deep, 2, CH), Stage("v2", "w_in_2", 2, deep, 2, CH), Stage("r2", "w_in_2", 2, deep, 2, CH),
        Stage("pool", "pool_w_2", 2, 1, 4, PGC), Stage("out2", "w_out_2", 4, deep, 2, CH),
    ]
    for b in range(DFF // D):
        st += [Stage(f"up{b}", "mlp_w1_2", 4, deep, 2, CH), Stage(f"down{b}", "mlp_w2_2", 4, deep, 2, CH)]
    u = c = 0
    for s in st:
        s.u0, s.c0 = u, c
        u += s.units * (1 if s.name == "attb" else s.chunks)
        c += s.chunks
    return {s.name: s for s in st}, u


def join(*hooks):
    return {u: [f for h in hooks for f in h.get(u, [])] for u in sorted({u for h in hooks for u in h})}


SLOTS = HEADS // 2


def slot_units(c):
    gate = [(False, (4 * c + i) % 8) for i in range(4)]
    return gate[:1] + [(True, 0), (True, 1)] * (c + 1 < SLOTS) + gate[1:]


def constants():
    s, t = np.arange(P)[:, None], np.arange(P)[None, :]
    t2 = np.arange(SEQ)[None, :]
    inv = (1.0 / (np.float32(10000.0) ** (np.arange(0, ROPE, 2, dtype=np.float32) / np.float32(ROPE)))).astype(np.float32)
    ang = np.arange(SEQ, dtype=np.float32)[:, None] * inv[None, :]
    two = lambda a: np.concatenate([np.repeat(a[i * P:(i + 1) * P, None, :], 2, 1).reshape(P, ROPE) for i in range(TT)], 1)
    same = s // CHUNK == t // CHUNK
    hole = NEG * ((s < CHUNK) & (t >= CHUNK))
    meta_s = s - META
    parts = {
        "ident": s == t,
        "suffix": s >= t,
        "ones": np.ones((P, P)),
        "strict": s < t,
        "strict_neg": NEG * (s >= t),
        "chunk_neg": np.concatenate([hole, np.zeros((P, P)), hole], 1),
        "cos": two(np.cos(ang)), "sin": two(np.sin(ang)),
        "gla_causal": same & (s <= t),
        "gla_after": same & (s > t),
        "gla_half": np.concatenate([s // CHUNK == 0, s // CHUNK == 1], 1),
        "band": np.concatenate([((t2 >= s) & (t2 - s < w)) / w - (t2 == s) * 1.0 for w in WINDOWS], 1),
        "band_meta": np.concatenate([((s < META) & (t - meta_s < w)) / w for w in WINDOWS], 1),
    }
    where, at = {}, 0
    for name, a in parts.items():
        where[name] = (at, a.shape[1])
        at += a.shape[1]
    return np.ascontiguousarray(np.concatenate([np.asarray(a, np.float32) for a in parts.values()], 1), np.float32), where


def build(nc, w, const, out):
    S, units = plan()
    table, where = constants()
    ctx = ExitStack()
    with ctx:
        place = [(nc.sbuf_base + 63) // 64 * 64]

        def region(nbytes):
            at = place[0]
            place[0] = at + (nbytes + 63) // 64 * 64
            assert place[0] <= nc.sbuf_usable_end, place[0]
            return at

        def sb(name, shape, dt, at):
            return nc.alloc_sbuf_tensor_at(name, shape, dt, offset=at)

        KB = 1024
        raw = sb("raw", [P, RING, UNIT], F32, region(16 * KB))
        whi = sb("whi", [P, RING, UNIT], F32R, region(16 * KB))
        wlo = sb("wlo", [P, RING, UNIT], F32R, region(16 * KB))
        x = sb("x", [P, TT, D], F32, region(16 * KB))
        nat = sb("nat", [P, TT, D], F32, region(16 * KB))
        r0, r1, r2 = region(32 * KB), region(32 * KB), region(16 * KB)
        stg_at = region(8 * KB)
        r3 = region(8 * KB)
        r4 = region(9 * KB)
        ahi = sb("ahi", [P, KT, SEQ], F32R, r0)
        alo = sb("alo", [P, KT, SEQ], F32R, r0 + 16 * KB)
        bhi = sb("bhi", [P, KT, SEQ], F32R, r1)
        blo = sb("blo", [P, KT, SEQ], F32R, r1 + 16 * KB)
        stg = sb("stg", [P, 2, TT, CH], F32, stg_at)
        gains = sb("gains", [P, D], F32, r3)
        tab = sb("tab", [P, table.shape[1]], F32, region(table.shape[1] * 4))
        p_at = region(8 * KB)
        phi = sb("phi", [P, 2, 2, SEQ], F32R, p_at)
        plo = sb("plo", [P, 2, 2, SEQ], F32R, p_at + 4 * KB)
        gcol = sb("gcol", [P, P], F32, region(512))
        st_at = region(1024)
        ssq = sb("ssq", [P, TT, 4], F32, st_at)
        ssum = sb("ssum", [P, 8], F32, st_at + 64)
        root = sb("root", [P, 8], F32, st_at + 128)
        rs = sb("rs", [P, 8, 8], F32, st_at + 192)
        mx = sb("mx", [P, 2, 4], F32, st_at + 512)
        den = sb("den", [P, 2, 4], F32, st_at + 576)
        rden = sb("rden", [P, 2, 4], F32, st_at + 640)
        eps = sb("eps", [P, 1], F32, st_at + 704)
        psrc = sb("psrc", [P, 2, TT, 2 * P], F32, r2)
        qkT = sb("qkT", [P, 2 * HEADS, SEQ], F32, r1)
        vA = sb("vA", [P, TT, D], F32, r2)
        zA = sb("zA", [P, 2, 2, 3 * P], F32, r3)
        tA = sb("tA", [P, 2, 3 * P], F32, r4)
        pp = sb("pp", [P, TT, D], F32, r2)
        knT = sb("knT", [P, HEADS, SEQ], F32, r1)
        vB = sb("vB", [P, TT, D], F32, r1 + 16 * KB)
        kvhi = sb("kvhi", [P, LK, SEQ], F32R, r2)
        kvlo = sb("kvlo", [P, LK, SEQ], F32R, r2 + 4 * KB)
        cqhi = sb("cqhi", [P, LK, SEQ], F32R, r2 + 8 * KB)
        cqlo = sb("cqlo", [P, LK, SEQ], F32R, r2 + 12 * KB)
        sB = sb("sB", [P, 2, 3 * P], F32, r3)
        pB = sb("pB", [P, 2, 3 * P], F32, r3 + 3 * KB)
        qn = sb("qn", [P, 2, 2, SEQ], F32, r4)
        qr = sb("qr", [P, 2, SEQ], F32, r4 + 4 * KB)
        krT = sb("krT", [P, SEQ], F32, r4 + 6 * KB)
        roped = sb("roped", [P, TT, 2 * ROPE], F32, r4 + 7 * KB)
        turn = sb("turn", [P, TT, 2, ROPE // 2], F32, r4 + 8 * KB)
        kraw = sb("kraw", [P, TT, 2, ROPE], F32, r4)
        vC = sb("vC", [P, TT, GLA_H * DV], F32, r0)
        vM = sb("vM", [P, GLA_H * DV], F32, r0 + 8 * KB)
        kend = sb("kend", [P, TT, GKW], F32, r0 + 12 * KB)
        kendM = sb("kendM", [P, GKW], F32, r0 + 16 * KB)
        kTc = sb("kTc", [P, GLA_H, SEQ], F32, r0 + 18 * KB)
        qA = sb("qA", [P, GLA_H, TT, P], F32, r0 + 22 * KB)
        qB = sb("qB", [P, GLA_H, TT, P], F32, r0 + 26 * KB)
        oneM = sb("oneM", [P, CH], F32, r0 + 30 * KB)
        metaT = sb("metaT", [P, KT, P], F32R, r4)
        logg = sb("logg", [P, TT, GKW], F32, r2 + 8 * KB)
        loggM = sb("loggM", [P, GKW], F32, r2 + 12 * KB)
        msc = sb("msc", [P, GKW], F32, r2 + 14 * KB)
        yhi = sb("yhi", [P, 8, SEQ], F32R, r2)
        ylo = sb("ylo", [P, 8, SEQ], F32R, r2 + 8 * KB)
        puM = sb("puM", [P, 2 * CH], F32, p_at)
        metax = sb("metax", [P, D], F32, r3)
        state = sb("state", [P, 2, 4, DV], F32, r3)
        glr = sb("glr", [P, TT, P], F32, r2)
        glrM = sb("glrM", [P, P], F32, r2 + 1 * KB)
        glrT = sb("glrT", [P, SEQ + META], F32, r2 + 1536)
        gw2 = sb("gw2", [P, GKW], F32, r2 + 3 * KB)
        brow = sb("brow", [P, GKW], F32, r2 + 5 * KB)
        decay = sb("decay", [P, GLA_H, 4], F32, r2 + 7 * KB)
        sc = sb("sc", [P, TT, P], F32, r4 + 8 * KB)
        scaledM = sb("scaledM", [P, KT, META], F32, r4 + 8 * KB)
        ssqM = sb("ssqM", [P, 4], F32, st_at + 768)
        ssumM = sb("ssumM", [P, 1], F32, st_at + 800)
        rootM = sb("rootM", [P, 1], F32, st_at + 832)

        acc = [[ctx.enter_context(nc.psum_tensor(f"acc{p}{t}", [P, CH], F32)) for t in range(TT)] for p in range(2)]
        tp = [ctx.enter_context(nc.psum_tensor(f"tp{p}", [P, CH], F32)) for p in range(2)]
        xb = [ctx.enter_context(nc.psum_tensor(f"xb{p}", [P, CH], F32)) for p in range(2)]

        def const_of(name, rows=P):
            a, n = where[name]
            return tab[0:rows, a:a + n]

        ident = const_of("ident")
        GC = {"pre0": 0, "pre1": 16, "kv": 32, "norm1": 48, "norm2": 64, "kvl": 80, "ql": 84, "gla": 88, "pool": 90}
        RS = {"pre0": 0, "post": 1, "pre1": 2, "kvl": 3, "ql": 4, "norm1": 5, "norm2": 0, "final": 1}

        sems = {}

        def sem(name):
            if name not in sems:
                sems[name] = ctx.enter_context(nc.semaphore(name))
            return sems[name]

        raw_full = [sem(f"raw_full{i}") for i in range(RING)]
        hi_done, lo_done = sem("hi_done"), sem("lo_done")
        unit_used = sem("unit_used")
        evac_act, evac_dve = sem("evac_act"), sem("evac_dve")
        tp_full, tp_hi, tp_done = sem("tp_full"), sem("tp_hi"), sem("tp_done")
        x_done = sem("x_done")

        order = [("gcol", 1), ("x0", 8), ("p", 2), ("qk", 16), ("ogA", 8), ("x1", 8), ("x2a", [0, 1, 2, 3, 4, 5]),
                 ("x2b", [0, 1, 2, 3]), ("x2a", [6, 7]), ("x2b", [4, 5, 6, 7]), ("ckv", 2), ("kr", 1),
                 ("cq", 2), ("uk", 8), ("uq", 16), ("ogB", 8), ("x3", 8), ("x4", [0, 1, 2, 3, 4, 5]), ("meta", 1),
                 ("x4", [6, 7]), ("glr", 1), ("kinv", 2),
                 ("qdec", 2), ("pool", 4), ("mixed", 8), ("x5", 8)] + [(f"mlp{q}", 8) for q in range(DFF // D)]
        whole = ("gcol", "qk", "kr", "uk", "uq", "glr", "kinv", "qdec")
        BATCH, n_all, n_split = {}, 0, 0
        for name, fs in order:
            for f in range(fs) if isinstance(fs, int) else fs:
                BATCH[name, f] = (n_all, n_split)
                n_all += 1
                n_split += 0 if name in whole else 1

        def shape_of(u):
            s = max((s for s in S.values() if s.u0 <= u), key=lambda s: s.u0)
            if s.name == "attb":
                c, k = (u - s.u0) // 6, (u - s.u0) % 6
                return s.kt, 2 * QHEAD if slot_units(c)[k][0] else CH
            return s.kt, s.cols

        def q_chunk_at(j):
            return S["attb"].c0 + (j - 1) + (j - 1) // 2 if j else S["uq"].c0

        def gate_chunk_at(j):
            return S["attb"].c0 + min(2 * j + 2, SLOTS - 1) + j

        def unit_source(s, j, uu):
            if s.name == "pool":
                return w["pool_w_2"][0, 2 * j:2 * j + 2].rearrange("g (k p) n -> p (g k) n", p=P)
            base = {"v": 2 * D, "g": 3 * D, "krope": LORA, "q2": 0, "k2": GKW, "v2": 2 * GKW,
                    "r2": 2 * GKW + GLA_H * DV, "glr": 2 * GKW + 2 * GLA_H * DV,
                    "pu0": 2 * GKW + 2 * GLA_H * DV + GRANK, "pu1": 2 * GKW + 2 * GLA_H * DV + GRANK + CH}.get(s.name, 0)
            t = w[s.weight]
            if len(t.shape) == 3:
                t = t[1 if s.name in ("ple1", "gate1") else 0]
            row = uu * s.kt * P
            if s.name.startswith("down"):
                row = row + int(s.name[4:]) * D
            if s.name.startswith("up"):
                base = int(s.name[2:]) * D
            col = base + j * s.cols
            return t[row:row + s.kt * P, bass.ds(col, s.cols)].rearrange("(k p) n -> p k n", p=P)

        def x_rows(ap):
            return ap.rearrange("(t p) d -> p t d", p=P)

        block = ctx.enter_context(nc.Block())

        @block.sync
        def _(sp):
            def load(s, j, uu, r=0):
                u = s.u0 + j * s.units + uu if isinstance(j, int) else s.u0 + uu
                if u >= RING or not isinstance(r, int):
                    sp.wait_ge(lo_done, u - RING + 1 + r)
                dst = raw[:, u % RING, 0:s.kt * s.cols].rearrange("p (k n) -> p k n", k=s.kt)
                sp.dma_start(dst, unit_source(s, j, uu)).then_inc(raw_full[u % RING], 16)

            def stage(name, lo=0, hi=None):
                s = S[name]
                for j in range(lo, s.chunks if hi is None else hi):
                    for uu in range(s.units):
                        load(s, j, uu)

            sp.dma_start(tab[:, 0:P], const[:, 0:P]).then_inc(sem("ident_in"), 16)
            rows = [("norm_pre", 0, "pre0", 16), ("norm_pre", 1, "pre1", 16), ("kv_norm", None, "kv", 16),
                    ("norm1_w_2", 0, "norm1", 16), ("norm2_w_2", 0, "norm2", 16), ("kv_latent_norm", None, "kvl", 4),
                    ("q_latent_norm", 0, "ql", 4), ("gla_norm_w_2", 0, "gla", 2), ("pool_scale_2", 0, "pool", 8)]
            for name, i, key, n in rows:
                src = w[name] if i is None else w[name][i]
                sp.dma_start(gains[GC[key]:GC[key] + n, 0:P], src.rearrange("(a b) -> a b", b=P)).then_inc(sem("gain_rows_in"), 16)
            s = S["qk"]
            for uu in range(s.units):
                if uu < NCH:
                    c = slice(uu * CH, (uu + 1) * CH)
                    sp.dma_start(x[:, :, c], x_rows(w["x"][0])[:, :, c]).then_inc(sem(f"x_in{uu}"), 16)
                if uu == NCH:
                    for l in range(2):
                        sp.dma_start(psrc[:, l], x_rows(w["p"][l, 0])).then_inc(sem(f"p_in{l}"), 16)
                load(s, 0, uu)
            sp.dma_start(tab[:, P:], const[:, P:]).then_inc(sem("tab_in"), 16)
            s = S["qk"]
            with sp.Fori(1, s.chunks) as j:
                for uu in range(s.units):
                    load(s, j, uu, r=j * s.units)
            stage("v")
            stage("g")
            stage("out_a", 0, 1)
            sp.wait_ge(sem("attA_o"), HEADS // 2)
            sp.dma_start(gains[:, :], w["norm_post"][0:1, :].to_broadcast((P, D))).then_inc(sem("post_in0"), 16)
            stage("out_a", 1)
            for name in ("ple0", "gate0", "ckv", "krope", "cq", "uk", "uv", "uq"):
                stage(name)
            u = S["attb"].u0
            for c in range(SLOTS):
                for query, uu in slot_units(c):
                    sp.wait_ge(lo_done, u - RING + 1)
                    if query:
                        src = w["w_uq"][0, uu * 2 * P:(uu + 1) * 2 * P, (c + 1) * 2 * QHEAD:(c + 2) * 2 * QHEAD]
                    else:
                        src = w["w_in_b"][0, uu * 2 * P:(uu + 1) * 2 * P, LORA + c // 2 * CH:LORA + (c // 2 + 1) * CH]
                    cols = 2 * QHEAD if query else CH
                    sp.dma_start(raw[:, u % RING, 0:2 * cols].rearrange("p (k n) -> p k n", k=2),
                                 src.rearrange("(k p) n -> p k n", p=P)).then_inc(raw_full[u % RING], 16)
                    u += 1
            stage("out_b", 0, 1)
            sp.wait_ge(sem("attB_o"), HEADS // 2)
            sp.dma_start(gains[:, :], w["norm_post"][1:2, :].to_broadcast((P, D))).then_inc(sem("post_in1"), 16)
            stage("out_b", 1)
            stage("ple1")
            stage("gate1", 0, 1)
            sp.wait_ge(sem("post1_y"), 8)
            sp.dma_start(metax[0:META, :], w["meta_tokens_2"]).then_inc(sem("meta_in"), 16)
            stage("gate1", 1)
            stage("k2")
            sp.wait_ge(x_done, 16)
            sp.dma_start(gw2[0:GRANK, :], w["gate_w2_2"][0]).then_inc(sem("gate_in"), 16)
            sp.dma_start(brow[0:1, :], w["gate_b_2"]).then_inc(sem("gate_in2"), 16)
            for name in ("glr", "pu0", "q2", "pu1", "v2", "r2", "pool"):
                stage(name)
            sp.wait_ge(sem("gla_rs"), 1)
            sp.dma_start(gains[:, :], w["final_norm_w_2"].rearrange("(a b) -> a b", a=1).to_broadcast((P, D))).then_inc(sem("final_in"), 16)
            stage("out2")
            for b in range(DFF // D):
                stage(f"up{b}")
                stage(f"down{b}")
            for j in range(NCH):
                sp.wait_ge(sem("final_y"), TT * (j + 1))
                c = slice(j * CH, (j + 1) * CH)
                sp.dma_start(x_rows(out[0])[:, :, c], nat[:, :, c]).then_inc(sem("stored"), 16)
            sp.wait_ge(sem("stored"), 16 * NCH)

        @block.tensor
        def _(pe):
            b = [0]

            def product(s, j, hi, lo, r=0, rc=0, hooks={}, need=None, banks=None, meta=False, behind=1, before=None, free=None):
                u, c = s.u0 + j * s.units, s.c0 + j
                bank = banks or acc[c % 2]
                if free:
                    free()
                elif c >= 2:
                    pe.wait_ge(evac_act, c - behind + rc)
                    pe.wait_ge(evac_dve, c - behind + rc)
                if before:
                    before()
                for uu in range(s.units):
                    for hook in hooks.get(uu, []):
                        hook()
                    if need:
                        pe.wait_ge(tp_done, BATCH[need, uu][0] + 1)
                    unit(u + uu, bank, hi, lo, uu * s.kt, s.kt, s.cols, uu == 0, uu == s.units - 1, r, xb[c % 2] if meta else None)

            def unit(u, bank, hi, lo, kt0, n, cols, first, last, r=0, meta_bank=None):
                pe.wait_ge(lo_done, u + 1 + r)
                slot = u % RING
                for k in range(n):
                    kt, wc = kt0 + k, slice(k * cols, (k + 1) * cols)
                    start, stop = first and k == 0, last and k == n - 1
                    for t in range(TT):
                        tok = slice(t * P, (t + 1) * P)
                        o = bank[t][:, 0:cols]
                        pe.matmul(o, hi[:, kt, tok], whi[:, slot, wc], start=start, stop=False)
                        pe.matmul(o, hi[:, kt, tok], wlo[:, slot, wc], start=False, stop=False)
                        mm = pe.matmul(o, lo[:, kt, tok], whi[:, slot, wc], start=False, stop=stop)
                    if meta_bank is not None:
                        o = meta_bank[:, 0:cols]
                        pe.matmul(o, metaT[:, kt, :], whi[:, slot, wc], start=start, stop=False)
                        mm = pe.matmul(o, metaT[:, kt, :], wlo[:, slot, wc], start=False, stop=stop)
                mm.then_inc(unit_used, 1)

            def batch(parts, r=0):
                n = b[0]
                b[0] += 1
                if n >= 2:
                    pe.wait_ge(tp_done, n - 1 + r)
                for src, k, o in parts:
                    mm = pe.transpose(tp[n % 2][:, o:o + k], src, ident[0:k, 0:k])
                mm.then_inc(tp_full, 1)

            def pair(src, f):
                batch([(src[:, t, (2 * f + i) * P:(2 * f + i + 1) * P], P, i * SEQ + t * P) for i in range(2) for t in range(TT)])

            def staged(par, r=0, b_r=0):
                for f in range(2):
                    batch([(stg[:, par, t, (2 * f + i) * P:(2 * f + i + 1) * P], P, i * SEQ + t * P)
                           for i in range(2) for t in range(TT)], r=b_r)

            def ready(name, f):
                j = f // 2
                if name == "x0":
                    pe.wait_ge(sem(f"x_in{j}"), 16)
                elif name in X_DONE:
                    pe.wait_ge(x_done, X_DONE[name] + j + 1)
                elif name == "mixed":
                    evacuated(S["r2"].c0 + j if f < 4 else S["pool"].c0 + j - 2)
                elif name == "x5":
                    pe.wait_ge(evac_dve, S["out2"].c0 + j + 1)
                else:
                    evacuated(S["g"].c0 + j if name == "ogA" else gate_chunk_at(j))

            def turn(name, f):
                ready(name, f)
                assert BATCH[name, f][0] == b[0], (name, f)
                pair(x if name.startswith("x") else nat, f)

            def turns(name, plan):
                return {uu: [lambda f=f: turn(name, f) for f in fs] for uu, fs in plan.items()}

            def turn_part(name, f, c):
                evacuated(c)
                assert BATCH[name, f][0] == b[0], (name, f)
                batch([(stg[:, c % 2, t, (2 * (f % 2) + i) * P:(2 * (f % 2) + i + 1) * P], P, i * SEQ + t * P)
                       for i in range(2) for t in range(TT)])

            def turns_staged(name, plan, c):
                return {uu: [lambda f=f: turn_part(name, f, c) for f in fs] for uu, fs in plan.items()}
            X_DONE = {"x1": 0, "x2a": 4, "x2b": 4, "x3": 8, "x4": 12}

            def evacuated(c, r=0):
                pe.wait_ge(evac_act, c + 1 + r)
                pe.wait_ge(evac_dve, c + 1 + r)

            pe.wait_ge(sem("ident_in"), 16)
            pe.wait_ge(sem("gain_rows_in"), 9 * 16)
            batch([(gains[0:98, 0:P], 98, 0)])
            for f in range(3):
                turn("x0", f)

            def turn_p(l):
                pe.wait_ge(sem(f"p_in{l}"), 16)
                batch([(psrc[:, l, t, k * P:(k + 1) * P], P, k * SEQ + t * P) for k in range(2) for t in range(TT)])
            s = S["qk"]
            product(s, 0, ahi, alo, need="x0", hooks=join(turns("x0", SPREAD), {6 + l: [lambda l=l: turn_p(l)] for l in range(2)}))
            with pe.Fori(0, 3) as i:
                b_start = b[0]
                for q in (1, 2):
                    rc, r = i * 2, i * (2 * s.units)

                    def turn_last(q=q, rc=rc):
                        evacuated(s.c0 + q - 1, rc)
                        staged((s.c0 + q - 1) % 2, b_r=i * 4)
                    product(s, q, ahi, alo, r=r, rc=rc, hooks={4: [turn_last]})
            b[0] = b_start + 4 * 3
            product(s, 7, ahi, alo, hooks=turns_staged("qk", {4: [12, 13]}, 6))
            product(S["v"], 0, ahi, alo, hooks=turns_staged("qk", {4: [14, 15]}, 7))

            def logits(c):
                if c == 0:
                    pe.wait_ge(sem("tab_in"), 16)
                    pe.wait_ge(tp_done, b[0])
                else:
                    pe.wait_ge(sem("attA_z"), c)
                for i in range(2):
                    h, z = 2 * c + i, xb[i]
                    pe.matmul(z[:, 0:SEQ], qkT[:, HEADS + h, 0:P], qkT[:, h, :], start=True, stop=True)
                    mm = pe.matmul(z[:, SEQ:SEQ + P], qkT[:, HEADS + h, P:SEQ], qkT[:, h, P:SEQ], start=True, stop=True)
                mm.then_inc(sem("attA_logits"), 1)

            def later_sums(c):
                pe.wait_ge(sem("attA_sp"), c + 1)
                if c:
                    pe.wait_ge(sem("attA_o"), c)
                for i in range(2):
                    pe.matmul(tp[i][:, 0:3 * P], const_of("suffix"), tA[:, i, :], start=True, stop=False)
                    mm = pe.matmul(tp[i][:, P:2 * P], const_of("ones"), tA[:, i, 2 * P:3 * P], start=False, stop=True)
                mm.then_inc(sem("attA_sums"), 1)

            def values(c):
                pe.wait_ge(sem("attA_w"), c + 1)
                if c % 2 == 0:
                    pe.wait_ge(evac_act, S["v"].c0 + c // 2 + 1)
                    pe.wait_ge(evac_dve, S["v"].c0 + c // 2 + 1)
                for i in range(2):
                    h, o, w_ = 2 * c + i, tp[0][:, i * SEQ:(i + 1) * SEQ], zA[:, c % 2, i, :]
                    v = slice(h * HD, (h + 1) * HD)
                    pe.matmul(o[:, 0:P], w_[:, 0:P], vA[:, 0, v], start=True, stop=True)
                    pe.matmul(o[:, P:2 * P], w_[:, P:2 * P], vA[:, 0, v], start=True, stop=False)
                    mm = pe.matmul(o[:, P:2 * P], w_[:, 2 * P:3 * P], vA[:, 1, v], start=False, stop=True)
                mm.then_inc(sem("attA_out"), 1)

            def attention_part(m):
                c, r = m // 6, m % 6
                if r == 0 and c < HEADS // 2:
                    logits(c)
                if r == 0 and 1 <= c <= HEADS // 2:
                    later_sums(c - 1)
                if r == 3 and 1 <= c <= HEADS // 2:
                    values(c - 1)

            def attention_of(n):
                return {uu: [lambda m=8 * n + uu: attention_part(m)] for uu in range(8)}
            for j in range(1, 4):
                product(S["v"], j, ahi, alo, hooks=attention_of(j - 1))

            for j in range(4):
                hooks = attention_of(3 + j)
                if j == 3:
                    hooks = join(hooks, {5: [lambda: pe.wait_ge(sem("attA_o"), HEADS // 2)]}, turns("ogA", OG_EARLY))
                product(S["g"], j, ahi, alo, hooks=hooks)

            def turn_meta():
                pe.wait_ge(sem("meta_in"), 16)
                batch([(metax[0:META, k * P:(k + 1) * P], META, k * META) for k in range(KT)])

            def post(layer, y, x1, x2):
                ab = "ab"[layer]
                def gates_out():
                    pe.wait_ge(evac_act, gate_chunk_at(3) + 1)
                for j in range(4):
                    product(S[f"out_{ab}"], j, bhi, blo, need=y if j == 0 else None, free=gates_out if layer and j == 0 else None, hooks=turns(y, OG_LATE if layer == 0 else SPREAD) if j == 0 else {})
                for j in range(4):
                    product(S[f"ple{layer}"], j, phi[:, layer], plo[:, layer])
                for f in range(3):
                    turn(x1, f)
                for j in range(4):
                    hooks = turns(x2, ALONG[j]) if j else turns(x1, SPREAD)
                    if layer and j == 3:
                        hooks = join(hooks, {6: [turn_meta]})
                    product(S[f"gate{layer}"], j, ahi, alo, need=x1 if j == 0 else None, hooks=hooks)

            post(0, "ogA", "x1", "x2a")

            product(S["ckv"], 0, bhi, blo, need="x2a", hooks=join(turns("x2b", {0: [0, 1], 1: [2, 3]}), turns("x2a", LAST), turns("x2b", {5: [4], 6: [5]})))
            product(S["krope"], 0, bhi, blo)
            c = S["ckv"].c0

            def turn_k_rope():
                pe.wait_ge(sem("k_roped"), 1)
                batch([(roped[:, t, :], P, t * P) for t in range(TT)])
            product(S["cq"], 0, ahi, alo, need="x2b", hooks=join(turns("x2b", {0: [6], 1: [7]}), turns_staged("ckv", {4: [0], 5: [1]}, c), {7: [turn_k_rope]}))
            pe.wait_ge(tp_done, b[0])
            s = S["uk"]
            for j in range(4):
                product(s, j, kvhi, kvlo)
                if j:
                    for f in (2 * j - 2, 2 * j - 1):
                        turn_part("uk", f, s.c0 + j - 1)
                if j == 0:
                    for f in range(2):
                        turn_part("cq", f, S["cq"].c0)
            s = S["uv"]
            for j in range(4):
                product(s, j, kvhi, kvlo)
                if j == 0:
                    for f in (6, 7):
                        turn_part("uk", f, s.c0 - 1)

            def turn_queries(j):
                evacuated(q_chunk_at(j))
                batch([(stg[:, j % 2, t, i * QHEAD:i * QHEAD + HD], P, i * SEQ + t * P) for i in range(2) for t in range(TT)])

            def turn_roped(j):
                pe.wait_ge(sem("q_roped"), j + 1)
                batch([(roped[:, t, :], P, t * P) for t in range(TT)])

            def scores(c):
                pe.wait_ge(tp_done, b[0])
                if c:
                    pe.wait_ge(sem("attB_m"), 2 * c)
                for i in range(2):
                    rows, h = slice(i * ROPE, (i + 1) * ROPE), 2 * c + i
                    for o, qt, n in ((0, 0, P), (P, 1, SEQ)):
                        q = slice(qt * P, (qt + 1) * P)
                        pe.matmul(xb[i][:, o:o + n], qn[:, c % 2, i, q], knT[:, h, 0:n], start=True, stop=False)
                        mm = pe.matmul(xb[i][:, o:o + n], qr[rows, c % 2, q], krT[rows, 0:n], start=False, stop=True)
                    mm.then_inc(sem("attB_s"), 1)

            def turned(c):
                for i in range(2):
                    pe.wait_ge(sem("attB_p"), 2 * c + i + 1)
                    for k in range(3):
                        mm = pe.transpose(acc[0][i][:, k * P:(k + 1) * P], sB[:, i, k * P:(k + 1) * P], ident)
                    mm.then_inc(sem("attB_t"), 1)

            def outputs(c):
                pe.wait_ge(sem("attB_pt"), 2 * c + 2)
                for i in range(2):
                    o, cols = acc[0][0][:, i * SEQ:(i + 1) * SEQ], slice((2 * c + i) * HD, (2 * c + i + 1) * HD)
                    pe.matmul(o[:, 0:P], pB[:, i, 0:P], vB[:, 0, cols], start=True, stop=True)
                    pe.matmul(o[:, P:SEQ], pB[:, i, P:2 * P], vB[:, 0, cols], start=True, stop=False)
                    mm = pe.matmul(o[:, P:SEQ], pB[:, i, 2 * P:3 * P], vB[:, 1, cols], start=False, stop=True)
                mm.then_inc(sem("attB_out"), 1)

            evacuated(S["uv"].c0 + 3)
            pe.wait_ge(tp_done, b[0])
            product(S["uq"], 0, cqhi, cqlo, banks=acc[0], behind=0)
            turn_queries(0)
            turn_roped(0)
            u = S["attb"].u0
            for c in range(SLOTS):
                more = c + 1 < SLOTS
                for k, (query, uu) in enumerate(slot_units(c)):
                    if k == 0:
                        scores(c)
                        if c and c % 2 == 0:
                            pe.wait_ge(evac_act, gate_chunk_at(c // 2 - 1) + 1)
                    if query and uu == 0 and c:
                        pe.wait_ge(sem("attB_o"), c)
                    if more and k == 4:
                        turn_queries(c + 1)
                    if more and k == 5:
                        turn_roped(c + 1)
                    if uu % 4 == 3:
                        if not more:
                            pe.wait_ge(sem("attB_o"), c)
                        turned(c)
                    bank, hi, lo = (acc[0], cqhi, cqlo) if query else (acc[1], ahi, alo)
                    unit(u, bank, hi, lo, 2 * uu, 2, 2 * QHEAD if query else CH, uu == 0, uu == (1 if query else 7))
                    u += 1
                outputs(c)
            for f in range(3):
                turn("ogB", f)
            post(1, "ogB", "x3", "x4")

            pe.wait_ge(tp_done, BATCH["meta", 0][0] + 1)
            product(S["k2"], 0, bhi, blo, need="x4", hooks=turns("x4", LAST), meta=True)
            product(S["glr"], 0, bhi, blo, meta=True, before=lambda: pe.wait_ge(sem("norm1_rs"), 1))
            other = xb[(S["pu0"].c0 + 1) % 2]

            def turn_latents():
                evacuated(S["glr"].c0)
                batch([(glr[:, t, :], P, t * P) for t in range(TT)] + [(glrM[0:META, :], META, SEQ)])

            def gate_logits():
                pe.wait_ge(tp_done, b[0])
                pe.wait_ge(sem("gate_in"), 16)
                pe.wait_ge(sem("gate_in2"), 16)
                for t in range(TT + 1):
                    n = P if t < TT else META
                    o = (tp[0], tp[1], other)[t]
                    pe.matmul(o[0:n, :], glrT[0:GRANK, t * P:t * P + n], gw2[0:GRANK, :], start=True, stop=False)
                    pe.matmul(o[0:n, :], const_of("ones")[0:1, 0:n], brow[0:1, :], start=False, stop=True).then_inc(sem("graw"), 1)
            product(S["pu0"], 0, bhi, blo, hooks={4: [turn_latents], 6: [gate_logits]}, meta=True)

            def sums_from_start():
                pe.wait_ge(sem("logg"), 3)
                for t in range(TT):
                    pe.matmul(tp[t][:, :], const_of("gla_causal"), logg[:, t, :], start=True, stop=True).then_inc(sem("G"), 1)

            def sums_to_end():
                for t in range(TT):
                    pe.wait_ge(sem("eG"), 2 * (t + 1))
                    pe.matmul(tp[t][:, :], const_of("gla_after"), logg[:, t, :], start=True, stop=True).then_inc(sem("G"), 1)
                evacuated(S["pu0"].c0)
                pe.matmul(xb[0][0:META, :], const_of("gla_after")[0:META, 0:META], loggM[0:META, :], start=True, stop=True).then_inc(sem("G"), 1)

            def sums_over_chunk():
                for h in range(GLA_H):
                    for t in range(TT):
                        mm = pe.matmul(xb[1][:, (h * TT + t) * 2:(h * TT + t) * 2 + 2], logg[:, t, h * DK:(h + 1) * DK],
                                       const_of("gla_half"), start=True, stop=True)
                mm.then_inc(sem("G"), 1)
            product(S["q2"], 0, bhi, blo, hooks={2: [sums_from_start], 5: [sums_to_end], 6: [sums_over_chunk]})

            def turn_keys(f):
                pe.wait_ge(sem("kinv"), 1)
                pair(nat, f)

            def turn_decayed_queries(f):
                pe.wait_ge(sem("qdec"), 1)
                batch([(stg[:, 0, t, (2 * f + i) * P:(2 * f + i + 1) * P], P, i * SEQ + t * P) for i in range(2) for t in range(TT)])

            def banks_out():
                pe.wait_ge(sem("eG"), 7)
                pe.wait_ge(sem("decay"), 1)
            product(S["pu1"], 0, bhi, blo, hooks={3: [lambda: turn_keys(0)], 4: [lambda: turn_keys(1)], 5: [lambda: turn_decayed_queries(0)],
                                                  6: [lambda: turn_decayed_queries(1)]}, meta=True, before=banks_out)
            for j in range(2):
                product(S["v2"], j, bhi, blo, meta=True)

            def head_in(h):
                dk, dv = slice(h * DK, (h + 1) * DK), slice(h * DV, (h + 1) * DV)
                if h == 0:
                    evacuated(S["v2"].c0 + 1)
                    pe.wait_ge(tp_done, b[0])
                    pe.wait_ge(sem("kend"), 2)
                else:
                    pe.wait_ge(sem("gla_clip"), h)
                    pe.wait_ge(sem("gla_state"), h)
                for t in range(TT):
                    k_ = kTc[:, h, t * P:(t + 1) * P]
                    pe.matmul(tp[0][:, t * P:t * P + 64], k_, qA[:, h, t, 0:64], start=True, stop=True)
                    mm = pe.matmul(tp[0][:, t * P + 64:t * P + P], k_, qB[:, h, t, 64:P], start=True, stop=True)
                mm.then_inc(sem("gla_scores"), 1)
                pe.matmul(xb[0][:, 0:DV], kend[0:64, 0, dk], vC[0:64, 0, dv], start=True, stop=True)
                pe.matmul(xb[0][:, DV:2 * DV], kend[0:64, 1, dk], vC[0:64, 1, dv], start=True, stop=True)
                pe.matmul(xb[1][:, 0:DV], kend[64:P, 0, dk], vC[64:P, 0, dv], start=True, stop=True)
                pe.matmul(xb[1][:, DV:2 * DV], kendM[0:META, dk], vM[0:META, dv], start=True, stop=True).then_inc(sem("gla_ds"), 1)

            def head_out(h):
                pe.wait_ge(sem("gla_sc"), h + 1)
                pe.wait_ge(sem("gla_state"), h + 1)
                if h:
                    pe.wait_ge(sem("gla_o"), h)
                for t in range(TT):
                    o = tp[1][:, t * DV:(t + 1) * DV]
                    pe.matmul(o, sc[:, t, :], vC[:, t, h * DV:(h + 1) * DV], start=True, stop=False)
                    pe.matmul(o, qA[:, h, t, :], state[:, h % 2, 2 * t, :], start=False, stop=False)
                    mm = pe.matmul(o, qB[:, h, t, :], state[:, h % 2, 2 * t + 1, :], start=False, stop=True)
                mm.then_inc(sem("gla_out"), 1)
            product(S["r2"], 0, bhi, blo, hooks={0: [lambda: head_in(0)], 2: [lambda: head_out(0), lambda: head_in(1)],
                                                 4: [lambda: head_out(1), lambda: head_in(2)], 6: [lambda: head_out(2), lambda: head_in(3)]})

            def pooled(f):
                n = b[0]
                b[0] += 1
                if f == 0:
                    pe.wait_ge(sem("gla_o"), GLA_H)
                if f >= 2:
                    pe.wait_ge(tp_done, n - 1)
                band, bm = const_of("band"), const_of("band_meta")
                for i in range(2):
                    ct = 2 * f + i
                    g, cs = ct // 2, slice(NCH // 2 * CH + ct * P, NCH // 2 * CH + (ct + 1) * P)
                    o = tp[n % 2][:, i * SEQ:(i + 1) * SEQ]
                    pe.matmul(o, nat[:, 0, cs], band[:, g * SEQ:(g + 1) * SEQ], start=True, stop=False)
                    pe.matmul(o[:, P:SEQ], nat[:, 1, cs], band[:, g * SEQ:g * SEQ + P], start=False, stop=False)
                    mm = pe.matmul(o[:, 0:P], puM[0:META, ct * P:(ct + 1) * P], bm[0:META, g * P:(g + 1) * P], start=False, stop=True)
                mm.then_inc(tp_full, 1)
            product(S["r2"], 1, bhi, blo, hooks=join({0: [lambda: head_out(3)]}, {2 + f: [lambda f=f: pooled(f)] for f in range(4)},
                                                     turns("mixed", {6: [0], 7: [1]})))
            pe.wait_ge(tp_done, BATCH["pool", 3][0] + 1)
            s = S["pool"]
            for j in range(2):
                u, c = s.u0 + j, s.c0 + j
                pe.wait_ge(evac_act, c - 1)
                pe.wait_ge(evac_dve, c - 1)
                pe.wait_ge(lo_done, u + 1)
                for g in range(2):
                    for t in range(TT):
                        for k in range(2):
                            ct, tok = 4 * j + 2 * g + k, slice(t * P, (t + 1) * P)
                            o = acc[c % 2][t][:, g * PGC:(g + 1) * PGC]
                            cols = slice((2 * g + k) * PGC, (2 * g + k + 1) * PGC)
                            pe.matmul(o, yhi[:, ct, tok], whi[:, u % RING, cols], start=(k == 0), stop=False)
                            pe.matmul(o, yhi[:, ct, tok], wlo[:, u % RING, cols], start=False, stop=False)
                            mm = pe.matmul(o, ylo[:, ct, tok], whi[:, u % RING, cols], start=False, stop=(k == 1))
                mm.then_inc(unit_used, 1)
            for f in (2, 3):
                turn("mixed", f)
            for j in range(4):
                product(S["out2"], j, ahi, alo, need=None if j else "mixed", hooks=turns("x5", ALONG[j]) if j else turns("mixed", MIXED_LATE))

            for q in range(DFF // D):
                s = S[f"up{q}"]
                for j in range(4):
                    first_x = q == 0 and j == 0
                    product(s, j, bhi, blo, need="x5" if first_x else None,
                            hooks=turns_staged(f"mlp{q}", ALONG[j], s.c0 + j - 1) if j else turns("x5", LAST) if first_x else {})
                for j in range(4):
                    product(S[f"down{q}"], j, ahi, alo, need=f"mlp{q}" if j == 0 else None,
                            hooks=turns_staged(f"mlp{q}", LAST, s.c0 + 3) if j == 0 else {})

        @block.scalar
        def _(act):
            ptr = [0]

            def split_to(target, r=0):
                for u in range(ptr[0], target):
                    kt, cols = shape_of(u)
                    act.wait_ge(raw_full[u % RING], 16 * (u // RING + 1) + r * 16 // RING if isinstance(r, int) else 16 * (u // RING + 1) + r * (16 // RING))
                    if u >= RING:
                        act.wait_ge(unit_used, u - RING + 1 + r)
                    n = kt * cols
                    act.activation(whi[:, u % RING, 0:n], raw[:, u % RING, 0:n], ACT.Copy).then_inc(hi_done, 1)
                ptr[0] = max(ptr[0], target)

            def along(s, j, hooks={}, r=0):
                for uu in range(s.units):
                    split_to(min(s.u0 + j * s.units + uu + 4, units), r)
                    for hook in hooks.get(uu, []):
                        hook()

            def his(name, dst, gain, plan):
                return {uu: [lambda f=f: hi_batch(name, f, dst, gain) for f in fs] for uu, fs in plan.items()}

            def hi_mixed(f):
                n = BATCH["mixed", f][0]
                act.wait_ge(tp_full, n + 1)
                src = tp[n % 2][:, :].rearrange("p (i t) -> p i t", i=2)
                for i in range(2):
                    g = GC["gla"] + i if f < 4 else GC["pool"] + 2 * (f - 4) + i
                    m = act.activation(ahi[:, 2 * f + i, :], src[:, i, :], ACT.Copy, scale=gcol[:, g:g + 1])
                m.then_inc(tp_hi, 1)

            def his_mixed(plan):
                return {uu: [lambda f=f: hi_mixed(f) for f in fs] for uu, fs in plan.items()}

            def ended(s, j, r=0):
                act.wait_ge(unit_used, s.u0 + (j + 1) * s.units + r)

            def hi_batch(name, f, dst, gain=None, at=None):
                n, k = BATCH[name, f][0], f if at is None else at
                act.wait_ge(tp_full, n + 1)
                src = tp[n % 2][:, :].rearrange("p (i t) -> p i t", i=2)
                if gain is None:
                    m = act.activation(dst[:, 2 * k:2 * k + 2, :], src, ACT.Copy)
                else:
                    for i in range(2):
                        m = act.activation(dst[:, 2 * k + i, :], src[:, i, :], ACT.Copy, scale=gcol[:, gain + 2 * k + i:gain + 2 * k + i + 1])
                m.then_inc(tp_hi, 1)

            def squares(norm, j, src, junk=None):
                for t in range(TT):
                    n = sq[0]
                    sq[0] += 1
                    if n >= 2:
                        act.wait_ge(sem("squares"), n if junk else n - 1)
                    act.activation((junk or xb[n % 2])[:, 0:CH], src[:, t, j * CH:(j + 1) * CH], ACT.Square,
                                   accum_out=ssq[:, t, j:j + 1]).then_inc(sem("squares"), 1)
            sq = [0]

            def sqrt_of(norm, n=TT, width=D):
                act.wait_ge(sem(f"{norm}_ssum"), 1)
                act.activation(root[:, 0:n], ssum[:, 0:n], ACT.Sqrt, scale=1.0 / width, bias=eps_col).then_inc(sem(f"{norm}_root"), 1)
            eps_col = eps[:, 0:1]

            def scaled(dst, src, norm, t):
                return act.activation(dst, src, ACT.Copy, scale=rs[:, RS[norm], t:t + 1])

            act.wait_ge(sem("eps_set"), 1)
            act.wait_ge(tp_done, 1)
            for f in range(3):
                hi_batch("x0", f, ahi, GC["pre0"])
                split_to(f + 1)
            squares("pre0", 0, x)
            s = S["qk"]
            for uu in range(1, s.units):
                if uu < 6:
                    hi_batch("x0", uu + 2, ahi, GC["pre0"])
                else:
                    n = BATCH["p", uu - 6][0]
                    act.wait_ge(tp_full, n + 1)
                    act.activation(phi[:, uu - 6], tp[n % 2][:, :].rearrange("p (i t) -> p i t", i=2), ACT.Copy).then_inc(tp_hi, 1)
                split_to(s.u0 + uu + 3)
                if uu % 2 == 0:
                    squares("pre0", uu // 2, x)
            sqrt_of("pre0")
            s = S["qk"]
            act.wait_ge(sem("pre0_rs"), 1)

            def qk_chunk(q, i=None):
                r = 0 if i is None else i * (2 * s.units)
                along(s, q, r=r)
                ended(s, q, r)
                scaled(stg[:, q % 2, 0, :], acc[q % 2][0][:, :], "pre0", 0).then_inc(evac_act, 1)

            qk_chunk(0)
            qk_chunk(1)
            with act.Fori(0, 3) as i:
                first = ptr[0]
                for q in (2, 3):
                    qk_chunk(q, i)
            ptr[0] = first + 3 * 2 * s.units

            def z_out(c):
                act.wait_ge(sem("attA_logits"), c + 1)
                if c >= 2:
                    act.wait_ge(sem("attA_out"), c - 1)
                for i in range(2):
                    m = act.activation(zA[:, c % 2, i, :], xb[i][:, 0:3 * P], ACT.Copy, scale=HD ** -0.5)
                m.then_inc(sem("attA_z"), 1)

            def softplus_exp(c):
                act.wait_ge(sem("attA_abs"), 2 * c + 2)
                act.activation(tA[:, :, :], tA[:, :, :], ACT.Exp).then_inc(sem("attA_t"), 1)

            def softplus_log(c):
                act.wait_ge(sem("attA_t"), 2 * c + 1)
                act.activation(tA[:, :, :], tA[:, :, :], ACT.Ln, bias=1.0).then_inc(sem("attA_t"), 1)

            def weights(c):
                act.wait_ge(sem("attA_d"), c + 1)
                act.activation(zA[:, c % 2], zA[:, c % 2], ACT.Exp).then_inc(sem("attA_w"), 1)

            def attention_of(n):
                def part(m):
                    c, r = m // 6, m % 6
                    if r == 0 and c < HEADS // 2:
                        z_out(c)
                    if r == 1 and 1 <= c <= HEADS // 2:
                        weights(c - 1)
                    if r == 2 and c < HEADS // 2:
                        softplus_exp(c)
                    if r == 3 and c < HEADS // 2:
                        softplus_log(c)
                return {uu: [lambda m=8 * n + uu: part(m)] for uu in range(8)}

            s = S["v"]
            for j in range(4):
                along(s, j, attention_of(j - 1) if j else {})
                ended(s, j)
                scaled(vA[:, 0, j * CH:(j + 1) * CH], acc[(s.c0 + j) % 2][0][:, :], "pre0", 0).then_inc(evac_act, 1)

            def silu_out(bank, par, norm):
                for t in range(TT):
                    m = act.activation(stg[:, par, t, :], bank[t][:, :], ACT.Silu, scale=rs[:, RS[norm], t:t + 1])
                m.then_inc(evac_act, 1)

            s = S["g"]
            for j in range(4):
                along(s, j, join(attention_of(3 + j), his("ogA", bhi, None, OG_EARLY) if j == 3 else {}))
                ended(s, j)
                if j >= 2:
                    act.wait_ge(evac_dve, s.c0 + j - 1)
                silu_out(acc[(s.c0 + j) % 2], (s.c0 + j) % 2, "pre0")

            def meta_in():
                act.wait_ge(sem("meta_in"), 16)
                for i in range(4):
                    n = sq[0]
                    sq[0] += 1
                    act.wait_ge(sem("squares"), n - 1)
                    act.activation(xb[n % 2][0:META, 0:CH], metax[0:META, i * CH:(i + 1) * CH], ACT.Square,
                                   accum_out=ssqM[0:META, i:i + 1]).then_inc(sem("squares"), 1)
                act.wait_ge(sem("meta_zero"), 1)
                act.wait_ge(sem("meta_scaled"), 1)
                act.activation(metaT[:, :, 0:META], scaledM[:, :, :], ACT.Copy).then_inc(tp_hi, 1)

            def meta_root():
                act.wait_ge(sem("metan_ssum"), 1)
                act.activation(rootM[0:META, :], ssumM[0:META, :], ACT.Sqrt, scale=1.0 / D, bias=eps[0:META, 0:1]).then_inc(sem("metan_root"), 1)

            def post(layer, y, x1, x2, gain, norms):
                s = S[f"out_{'ab'[layer]}"]
                for j in range(4):
                    p = (s.c0 + j) % 2
                    along(s, j, his(y, bhi, None, OG_LATE if layer == 0 else SPREAD) if j == 0 else {})
                    ended(s, j)
                    act.activation(nat[:, 0, j * CH:(j + 1) * CH], acc[p][0][:, :], ACT.Copy).then_inc(evac_act, 1)
                    act.wait_ge(evac_act, s.c0 + j + 1)
                    act.wait_ge(evac_dve, s.c0 + j + 1)
                    squares("post", j, nat)
                sqrt_of(f"post{layer}")
                s = S[f"ple{layer}"]
                for j in range(4):
                    p = (s.c0 + j) % 2
                    split_to(s.u0 + j + 4)
                    ended(s, j)
                    act.activation(pp[:, 0, j * CH:(j + 1) * CH], acc[p][0][:, :], ACT.Copy).then_inc(evac_act, 1)
                for f in range(3):
                    hi_batch(x1, f, ahi)
                s = S[f"gate{layer}"]
                for j in range(4):
                    c, p = s.c0 + j, (s.c0 + j) % 2

                    def last_squares(j=j):
                        act.wait_ge(x_done, 8 * layer + 4 + j)
                        squares(norms, j - 1, x)
                    hooks = join({4: [last_squares]}, his(x2, bhi, gain, ALONG[j])) if j else his(x1, ahi, None, SPREAD)
                    along(s, j, join(hooks, {6: [meta_in], 7: [meta_root]}) if layer and j == 3 else hooks)
                    ended(s, j)
                    for t in range(TT):
                        m = act.activation(stg[:, p, t, :], acc[p][t][:, :], ACT.Sigmoid)
                    m.then_inc(evac_act, 1)

            def x_norm(layer, norms, junk=None):
                act.wait_ge(x_done, 8 * layer + 8)
                squares(norms, 3, x, junk)
                sqrt_of(norms)

            post(0, "ogA", "x1", "x2a", GC["kv"], "pre1")

            def latent(s, norm):
                p = s.c0 % 2
                ended(s, 0)
                scaled(stg[:, p, 0, :], acc[p][0][:, :], "pre1", 0).then_inc(evac_act, 1)
                act.wait_ge(evac_act, s.c0 + 1)
                act.wait_ge(evac_dve, s.c0 + 1)
                squares(norm, 0, stg[:, p])
                sqrt_of(norm, width=LORA)

            s = S["ckv"]
            along(s, 0, join(his("x2b", ahi, GC["pre1"], {0: [0, 1], 1: [2, 3]}), his("x2a", bhi, GC["kv"], LAST), {4: [lambda: x_norm(0, "pre1")]},
                             his("x2b", ahi, GC["pre1"], {5: [4], 6: [5]})))
            act.wait_ge(sem("pre1_rs"), 1)
            latent(s, "kvl")
            s = S["krope"]
            along(s, 0)
            ended(s, 0)
            scaled(kraw[:, 0, 0, :], acc[s.c0 % 2][0][:, 0:ROPE], "pre1", 0)
            scaled(kraw[:, 0, 1, :], acc[s.c0 % 2][0][:, 0:ROPE], "pre1", 0).then_inc(evac_act, 1)
            s = S["cq"]
            along(s, 0, join(his("x2b", ahi, GC["pre1"], {0: [6], 1: [7]}), his("ckv", kvhi, GC["kvl"], {4: [0], 5: [1]})))
            latent(s, "ql")
            act.wait_ge(sem("kvl_rs"), 1)
            s = S["uk"]
            for j in range(4):
                p = (s.c0 + j) % 2
                along(s, j)
                ended(s, j)
                scaled(stg[:, p, 0, :], acc[p][0][:, :], "kvl", 0).then_inc(evac_act, 1)
                if j == 0:
                    for f in range(2):
                        hi_batch("cq", f, cqhi, GC["ql"])
            s = S["uv"]
            for j in range(4):
                p = (s.c0 + j) % 2
                along(s, j)
                ended(s, j)
                scaled(vB[:, 0, j * CH:(j + 1) * CH], acc[p][0][:, :], "kvl", 0).then_inc(evac_act, 1)

            act.wait_ge(sem("ql_rs"), 1)

            def queries_out(j):
                if j >= 2:
                    act.wait_ge(sem("q_roped"), j - 1)
                scaled(stg[:, j % 2, 0, 0:2 * QHEAD], acc[0][0][:, 0:2 * QHEAD], "ql", 0).then_inc(evac_act, 1)

            along(S["uq"], 0)
            ended(S["uq"], 0)
            queries_out(0)
            u = S["attb"].u0
            for c in range(SLOTS):
                for query, uu in slot_units(c):
                    if uu % 4 == 3:
                        if c:
                            act.wait_ge(sem("attB_out"), c)
                        for i in range(2):
                            act.wait_ge(sem("attB_t"), 2 * c + i + 1)
                            act.activation(pB[:, i, :], acc[0][i][:, 0:3 * P], ACT.Copy).then_inc(sem("attB_pt"), 1)
                    split_to(u + 4)
                    u += 1
                    if not query and uu % 4 == 0:
                        for i in range(2):
                            act.wait_ge(sem("attB_mx"), 2 * c + i + 1)
                            act.activation(sB[:, i, 0:P], sB[:, i, 0:P], ACT.Exp, bias=mx[:, i, 0:1], accum_out=den[:, c % 2, 2 * i:2 * i + 1])
                            act.activation(sB[:, i, P:3 * P], sB[:, i, P:3 * P], ACT.Exp, bias=mx[:, i, 1:2],
                                           accum_out=den[:, c % 2, 2 * i + 1:2 * i + 2]).then_inc(sem("attB_p"), 1)
                    if query and uu == 1:
                        act.wait_ge(unit_used, u)
                        queries_out(c + 1)
                if c == SLOTS - 1:
                    hi_batch("ogB", 0, bhi)
                if c % 2:
                    act.wait_ge(unit_used, u)
                    silu_out(acc[1], 0, "pre1")
            for f in range(1, 3):
                hi_batch("ogB", f, bhi)
            post(1, "ogB", "x3", "x4", GC["norm1"], "norm1")

            def plain(name, j, dst, hooks={}):
                s = S[name]
                along(s, j, hooks)
                ended(s, j)
                scaled(dst, acc[(s.c0 + j) % 2][0][:, 0:s.cols], "norm1", 0).then_inc(evac_act, 1)

            def k2_norm():
                x_norm(1, "norm1", xb[(S["k2"].c0 + 1) % 2])
                act.wait_ge(sem("norm1_rs"), 1)
            plain("k2", 0, kend[:, 0, :], join(his("x4", bhi, GC["norm1"], LAST), {5: [k2_norm]}))
            act.wait_ge(sem("glr_zero"), 1)
            plain("glr", 0, glr[:, 0, 0:GRANK])
            other = xb[(S["pu0"].c0 + 1) % 2]
            soft = [stg[:, 1, t, :] for t in range(TT)] + [msc[0:META, :]]

            def gate_abs():
                act.wait_ge(evac_dve, S["glr"].c0 + 1)
                for t in range(TT + 1):
                    act.wait_ge(sem("graw"), t + 1)
                    act.activation(soft[t], (tp[0], tp[1], other)[t][0:(P if t < TT else META), :], ACT.Abs).then_inc(sem("lg"), 1)

            def gate_exp():
                for t in range(TT + 1):
                    act.wait_ge(sem("lg"), t + 1)
                    act.activation(soft[t], soft[t], ACT.Exp, scale=-1.0).then_inc(sem("lg"), 1)

            def gate_log():
                for t in range(TT + 1):
                    act.wait_ge(sem("lg"), TT + 1 + t + 1)
                    act.activation(soft[t], soft[t], ACT.Ln, bias=1.0).then_inc(sem("lg"), 1)
            plain("pu0", 0, nat[:, 0, 2 * CH:3 * CH], {6: [gate_abs], 7: [gate_exp]})

            def exps_from_start():
                for t in range(TT):
                    act.wait_ge(sem("G"), t + 1)
                    act.wait_ge(sem("logg"), t + 1)
                    act.activation(stg[:, 1, t, :], tp[t][:, :], ACT.Exp, scale=1.0 / TAU).then_inc(sem("eG"), 1)
                    act.activation(nat[:, t, 0:CH], tp[t][:, :], ACT.Exp, scale=-1.0 / TAU).then_inc(sem("eG"), 1)

            def exps_to_end():
                for t in range(TT):
                    act.wait_ge(sem("G"), 3 + t)
                    act.activation(nat[:, t, CH:2 * CH], tp[t][:, :], ACT.Exp, scale=1.0 / TAU).then_inc(sem("eG"), 1)
                act.wait_ge(sem("G"), 5)
                act.activation(oneM[0:META, :], xb[0][0:META, :], ACT.Exp, scale=1.0 / TAU).then_inc(sem("eG"), 1)

            def decays():
                act.wait_ge(sem("G"), 6)
                act.activation(decay[:, :, :], xb[1][:, 0:4 * GLA_H].rearrange("p (h n) -> p h n", h=GLA_H), ACT.Exp, scale=1.0 / TAU).then_inc(sem("decay"), 1)
            plain("q2", 0, stg[:, 0, 0, :], {0: [gate_log], 2: [exps_from_start], 5: [exps_to_end], 6: [decays]})
            plain("pu1", 0, nat[:, 0, 3 * CH:4 * CH])
            for j in range(2):
                plain("v2", j, vC[:, 0, j * CH:(j + 1) * CH])

            def head_out(h):
                act.wait_ge(sem("gla_out"), h + 1)
                act.activation(nat[:, :, h * DV:(h + 1) * DV], tp[1][:, :].rearrange("p (t d) -> p t d", t=TT), ACT.Copy).then_inc(sem("gla_o"), 1)
                if h == 0:
                    act.wait_ge(evac_dve, S["v2"].c0 + 2)
                act.wait_ge(sem("gla_o"), h + 1)
                for t in range(TT):
                    n = sq[0]
                    sq[0] += 1
                    act.wait_ge(sem("squares"), n)
                    act.activation(msc[:, 0:DV], nat[:, t, h * DV:(h + 1) * DV], ACT.Square,
                                   accum_out=ssum[:, t * GLA_H + h:t * GLA_H + h + 1]).then_inc(sem("squares"), 1)

            def heads_root():
                act.wait_ge(sem("squares"), sq[0])
                act.activation(root[:, :], ssum[:, :], ACT.Sqrt, scale=1.0 / DV, bias=eps_col).then_inc(sem("gla_root"), 1)
            s = S["r2"]
            for j in range(2):
                p = (s.c0 + j) % 2
                along(s, j, join({0: [lambda: head_out(3)], 1: [heads_root]}, {2 + f: [lambda f=f: hi_batch("pool", f, yhi)] for f in range(4)}, his_mixed({6: [0], 7: [1]}))
                      if j else {2 * h + 2: [lambda h=h: head_out(h)] for h in range(3)})
                ended(s, j)
                for t in range(TT):
                    m = act.activation(stg[:, p, t, :], acc[p][t][:, :], ACT.Silu, scale=rs[:, RS["norm1"], t:t + 1])
                m.then_inc(evac_act, 1)
            s = S["pool"]
            for j in range(2):
                c = s.c0 + j
                split_to(s.u0 + j + 1 + 3)
                ended(s, j)
                act.activation(nat[:, 0, (2 + j) * CH:(3 + j) * CH], acc[c % 2][0][:, :], ACT.Copy).then_inc(evac_act, 1)
            for f in (2, 3):
                hi_mixed(f)

            def added(s, j):
                c, p = s.c0 + j, (s.c0 + j) % 2
                split_to(min(s.u0 + (j + 1) * s.units + 3, units))
                ended(s, j)
                act.activation(stg[:, p, 0, :], acc[p][0][:, :], ACT.Copy).then_inc(evac_act, 1)

            s = S["out2"]
            for j in range(4):
                def last_squares(j=j):
                    act.wait_ge(evac_dve, s.c0 + j)
                    squares("norm2", j - 1, x)
                along(s, j, join({4: [last_squares]}, his("x5", bhi, GC["norm2"], ALONG[j])) if j else his_mixed(MIXED_LATE))
                added(s, j)

            def x5_norm():
                act.wait_ge(evac_dve, S["out2"].c0 + 4)
                squares("norm2", 3, x)
                sqrt_of("norm2")
            for q in range(DFF // D):
                s = S[f"up{q}"]
                for j in range(4):
                    p = (s.c0 + j) % 2
                    first_x = q == 0 and j == 0
                    along(s, j, his(f"mlp{q}", ahi, None, ALONG[j]) if j else join(his("x5", bhi, GC["norm2"], LAST), {4: [x5_norm]}) if first_x else {})
                    if first_x:
                        act.wait_ge(sem("norm2_rs"), 1)
                    ended(s, j)
                    n = 4 * q + j
                    act.activation(stg[:, p, 0, :], acc[p][0][:, :], ACT.Relu, scale=rs[:, RS["norm2"], 0:1]).then_inc(sem("relu"), 1)
                    act.wait_ge(sem("relu"), n + 1)
                    act.activation(stg[:, p, 0, :], stg[:, p, 0, :], ACT.Square).then_inc(evac_act, 1)
                for j in range(4):
                    along(S[f"down{q}"], j, his(f"mlp{q}", ahi, None, LAST) if j == 0 else {})
                    added(S[f"down{q}"], j)
                    if q == DFF // D - 1:
                        act.wait_ge(evac_dve, S[f"down{q}"].c0 + j + 1)
                        squares("final", j, x)
            sqrt_of("final")

        @block.vector
        def _(dve):
            ptr = [0]
            def split_to(target, r=0):
                for u in range(ptr[0], target):
                    kt, cols = shape_of(u)
                    n = kt * cols
                    dve.wait_ge(hi_done, u + 1 + r)
                    dve.tensor_tensor(wlo[:, u % RING, 0:n], raw[:, u % RING, 0:n], whi[:, u % RING, 0:n].bitcast(F32),
                                      ALU.subtract).then_inc(lo_done, 1)
                ptr[0] = max(ptr[0], target)

            def along(s, j, hooks={}, r=0):
                for uu in range(s.units):
                    split_to(min(s.u0 + j * s.units + uu + 4, units), r)
                    for hook in hooks.get(uu, []):
                        hook()

            def los(name, hi, lo, gain, plan):
                return {uu: [lambda f=f: lo_batch(name, f, hi, lo, gain) for f in fs] for uu, fs in plan.items()}

            def copies(name, dst, plan):
                return {uu: [lambda f=f: copy_batch(name, f, dst[:, 2 * f:2 * f + 2, :]) for f in fs] for uu, fs in plan.items()}

            def ended(s, j, r=0):
                dve.wait_ge(unit_used, s.u0 + (j + 1) * s.units + r)

            def bank(n):
                return tp[n % 2][:, :].rearrange("p (i t) -> p i t", i=2)

            def lo_batch(name, f, hi, lo, gain=None):
                n, k = BATCH[name, f]
                dve.wait_ge(tp_hi, k + 1)
                tiles = slice(2 * f, 2 * f + 2)
                if gain is None:
                    m = dve.tensor_tensor(lo[:, tiles, :], bank(n), hi[:, tiles, :].bitcast(F32), ALU.subtract)
                else:
                    for i in range(2):
                        g = gain(f, i) if callable(gain) else gain + 2 * f + i
                        m = dve.scalar_tensor_tensor(out=lo[:, 2 * f + i, :], in0=bank(n)[:, i, :], scalar=gcol[:, g:g + 1],
                                                     in1=hi[:, 2 * f + i, :].bitcast(F32), op0=ALU.mult, op1=ALU.subtract)
                m.then_inc(tp_done, 1)

            def copy_batch(name, f, dst, r=0):
                n = BATCH[name, f][0]
                dve.wait_ge(tp_full, n + 1 + r)
                dve.tensor_copy(dst, bank(n)).then_inc(tp_done, 1)

            def scaled(dst, src, norm, t):
                return dve.tensor_scalar(dst, src, rs[:, RS[norm], t:t + 1], None, ALU.mult)

            def sum_squares(norm, squares_done, quarters=4):
                dve.wait_ge(sem("squares"), squares_done)
                dve.tensor_reduce(ssum[:, 0:TT], ssq[:, :, 0:quarters], AX, ALU.add).then_inc(sem(f"{norm}_ssum"), 1)

            def inverse_root(norm):
                dve.wait_ge(sem(f"{norm}_root"), 1)
                dve.reciprocal(rs[:, RS[norm.rstrip("01") if norm.startswith("post") else norm], 0:TT], root[:, 0:TT]).then_inc(sem(f"{norm}_rs"), 1)

            sq = [0]

            def norm_of(norm, n=8, quarters=4):
                sq[0] += n
                sum_squares(norm, sq[0], quarters)
                inverse_root(norm)

            dve.memset(eps[:, :], EPS).then_inc(sem("eps_set"), 1)
            n = BATCH["gcol", 0][0]
            dve.wait_ge(tp_full, n + 1)
            dve.tensor_copy(gcol[:, 0:98], tp[n % 2][:, 0:98]).then_inc(tp_done, 1)
            dve.wait_ge(tp_done, 1)
            for f in range(3):
                lo_batch("x0", f, ahi, alo, GC["pre0"])
                split_to(f + 1)
            s = S["qk"]
            for uu in range(1, s.units):
                if uu < 6:
                    lo_batch("x0", uu + 2, ahi, alo, GC["pre0"])
                else:
                    n, k = BATCH["p", uu - 6]
                    dve.wait_ge(tp_hi, k + 1)
                    dve.tensor_tensor(plo[:, uu - 6], bank(n), phi[:, uu - 6].bitcast(F32), ALU.subtract).then_inc(tp_done, 1)
                split_to(s.u0 + uu + 3)
            norm_of("pre0")
            dve.wait_ge(sem("pre0_rs"), 1)

            s = S["qk"]

            def qk_chunk(q, i=None):
                r = 0 if i is None else i * (2 * s.units)
                rb = 0 if i is None else i * 4
                def turned():
                    for f in (2 * q - 2, 2 * q - 1):
                        at = 2 * f if i is None else 2 * f + i * 8
                        copy_batch("qk", f, qkT[:, bass.ds(at, 2), :], rb)
                along(s, q, {4: [turned]} if q else {}, r)
                ended(s, q, r)
                scaled(stg[:, q % 2, 1, :], acc[q % 2][1][:, :], "pre0", 1).then_inc(evac_dve, 1)

            qk_chunk(0)
            qk_chunk(1)
            with dve.Fori(0, 3) as i:
                first = ptr[0]
                for q in (2, 3):
                    qk_chunk(q, i)
            ptr[0] = first + 3 * 2 * s.units

            def softplus(c):
                dve.wait_ge(sem("attA_t"), 2 * (c + 1))
                dve.scalar_tensor_tensor(out=tA[:, :, :], in0=zA[:, c % 2], scalar=0.0, in1=tA[:, :, :], op0=ALU.max,
                                         op1=ALU.add).then_inc(sem("attA_m"), 1)

            def less_sums(c):
                dve.wait_ge(sem("attA_sums"), c + 1)
                dve.wait_ge(sem("attA_n"), c + 1)
                for i in range(2):
                    m = dve.tensor_tensor(zA[:, c % 2, i, :], zA[:, c % 2, i, :], tp[i][:, 0:3 * P], ALU.subtract)
                m.then_inc(sem("attA_d"), 1)

            def outputs_out(c):
                dve.wait_ge(sem("attA_out"), c + 1)
                dve.tensor_copy(nat[:, :, 2 * c * HD:2 * (c + 1) * HD].rearrange("p t (i d) -> p i t d", i=2),
                                tp[0][:, :].rearrange("p (i t d) -> p i t d", i=2, t=TT)).then_inc(sem("attA_o"), 1)

            def attention_of(n):
                def part(m):
                    c, r = m // 6, m % 6
                    if r == 0 and 1 <= c <= HEADS // 2:
                        less_sums(c - 1)
                    if r == 3 and 1 <= c <= HEADS // 2:
                        outputs_out(c - 1)
                    if r == 4 and c < HEADS // 2:
                        softplus(c)
                return {uu: [lambda m=8 * n + uu: part(m)] for uu in range(8)}

            s = S["v"]
            for j in range(4):
                along(s, j, attention_of(j - 1) if j else copies("qk", qkT, {4: [14, 15]}))
                ended(s, j)
                scaled(vA[:, 1, j * CH:(j + 1) * CH], acc[(s.c0 + j) % 2][1][:, :], "pre0", 1).then_inc(evac_dve, 1)

            def gated(c, p, j, outputs_done, n):
                dve.wait_ge(evac_act, c + 1)
                dve.wait_ge(outputs_done, n)
                cols = slice(j * CH, (j + 1) * CH)
                dve.tensor_tensor(nat[:, :, cols], nat[:, :, cols], stg[:, p, :, :], ALU.mult).then_inc(evac_dve, 1)

            s = S["g"]
            for j in range(4):
                along(s, j, join(attention_of(3 + j), los("ogA", bhi, blo, None, OG_EARLY) if j == 3 else {}))
                gated(s.c0 + j, (s.c0 + j) % 2, j, sem("attA_o"), 2 * (j + 1))

            rsM = rs[0:META, 7, 0:1]

            def meta_in():
                n, k = BATCH["meta", 0]
                dve.wait_ge(tp_full, n + 1)
                dve.tensor_tensor(scaledM[:, :, :], tp[n % 2][:, 0:KT * META].rearrange("p (k m) -> p k m", m=META),
                                  gcol[:, GC["norm1"]:GC["norm1"] + KT][:, :, None].to_broadcast((P, KT, META)), ALU.mult).then_inc(sem("meta_scaled"), 1)
                dve.wait_ge(tp_hi, k + 1)
                dve.tensor_tensor(metaT[:, :, 32:32 + META], scaledM[:, :, :], metaT[:, :, 0:META].bitcast(F32), ALU.subtract).then_inc(tp_done, 1)
                sq[0] += 4
                dve.wait_ge(sem("squares"), sq[0] + 6)
                dve.tensor_reduce(ssumM[0:META, :], ssqM[0:META, :], AX, ALU.add).then_inc(sem("metan_ssum"), 1)

            def meta_rs():
                dve.wait_ge(sem("metan_root"), 1)
                dve.reciprocal(rsM, rootM[0:META, :]).then_inc(sem("metan_rs"), 1)

            def post(layer, y, x1, x2, gain, norms):
                s = S[f"out_{'ab'[layer]}"]
                for j in range(4):
                    p = (s.c0 + j) % 2
                    along(s, j, los(y, bhi, blo, None, OG_LATE if layer == 0 else SPREAD) if j == 0 else {})
                    ended(s, j)
                    dve.tensor_copy(nat[:, 1, j * CH:(j + 1) * CH], acc[p][1][:, :]).then_inc(evac_dve, 1)
                norm_of(f"post{layer}")
                dve.wait_ge(sem(f"post{layer}_rs"), 1)
                dve.wait_ge(sem(f"post_in{layer}"), 16)
                s = S[f"ple{layer}"]
                for j in range(4):
                    p = (s.c0 + j) % 2
                    split_to(s.u0 + j + 4)
                    ended(s, j)
                    dve.tensor_copy(pp[:, 1, j * CH:(j + 1) * CH], acc[p][1][:, :]).then_inc(evac_dve, 1)
                    for t in range(TT):
                        yq = nat[:, t, j * CH:(j + 1) * CH]
                        dve.scalar_tensor_tensor(out=yq, in0=yq, scalar=rs[:, RS["post"], t:t + 1], in1=gains[:, j * CH:(j + 1) * CH],
                                                 op0=ALU.mult, op1=ALU.mult).then_inc(sem(f"post{layer}_y"), 1)
                    for t in range(TT):
                        xq = x[:, t, j * CH:(j + 1) * CH]
                        dve.wait_ge(sem(f"post{layer}_y"), TT * j + t + 1)
                        m = dve.tensor_tensor(xq, xq, nat[:, t, j * CH:(j + 1) * CH], ALU.add)
                    m.then_inc(x_done, 1)
                for f in range(3):
                    lo_batch(x1, f, ahi, alo)
                s = S[f"gate{layer}"]
                for j in range(4):
                    c, p = s.c0 + j, (s.c0 + j) % 2
                    hooks = los(x2, bhi, blo, gain, ALONG[j]) if j else los(x1, ahi, alo, None, SPREAD)
                    along(s, j, join(hooks, {6: [meta_in], 7: [meta_rs]}) if layer and j == 3 else hooks)
                    dve.wait_ge(evac_act, c + 1)
                    cols = slice(j * CH, (j + 1) * CH)
                    dve.tensor_tensor(pp[:, :, cols], pp[:, :, cols], stg[:, p, :, :], ALU.mult).then_inc(evac_dve, 1)
                    dve.wait_ge(evac_dve, c + 1)
                    dve.tensor_tensor(x[:, :, cols], x[:, :, cols], pp[:, :, cols], ALU.add).then_inc(x_done, 1)

            post(0, "ogA", "x1", "x2a", GC["kv"], "pre1")

            def latent(s, norm):
                p = s.c0 % 2
                ended(s, 0)
                scaled(stg[:, p, 1, :], acc[p][1][:, :], "pre1", 1).then_inc(evac_dve, 1)
                norm_of(norm, 2, 1)

            s = S["ckv"]
            along(s, 0, join(los("x2b", ahi, alo, GC["pre1"], {0: [0, 1], 1: [2, 3]}), los("x2a", bhi, blo, GC["kv"], LAST), {4: [lambda: norm_of("pre1")]},
                             los("x2b", ahi, alo, GC["pre1"], {5: [4], 6: [5]})))
            dve.wait_ge(sem("pre1_rs"), 1)
            latent(s, "kvl")
            s = S["krope"]
            along(s, 0)
            ended(s, 0)
            scaled(kraw[:, 1, 0, :], acc[s.c0 % 2][1][:, 0:ROPE], "pre1", 1)
            scaled(kraw[:, 1, 1, :], acc[s.c0 % 2][1][:, 0:ROPE], "pre1", 1).then_inc(evac_dve, 1)
            s = S["cq"]
            n = BATCH["kr", 0][0]

            def k_rope_out():
                dve.wait_ge(tp_full, n + 1)
                dve.tensor_copy(krT[:, :], tp[n % 2][:, 0:SEQ]).then_inc(tp_done, 1)
            along(s, 0, join(los("x2b", ahi, alo, GC["pre1"], {0: [6], 1: [7]}), los("ckv", kvhi, kvlo, GC["kvl"], {4: [0], 5: [1]}), {7: [k_rope_out]}))
            latent(s, "ql")
            s = S["uk"]
            for j in range(4):
                p = (s.c0 + j) % 2
                along(s, j)
                ended(s, j)
                scaled(stg[:, p, 1, :], acc[p][1][:, :], "kvl", 1).then_inc(evac_dve, 1)
                if j:
                    for f in (2 * j - 2, 2 * j - 1):
                        copy_batch("uk", f, knT[:, 2 * f:2 * f + 2, :])
                if j == 0:
                    for f in range(2):
                        lo_batch("cq", f, cqhi, cqlo, GC["ql"])
            s = S["uv"]
            for j in range(4):
                p = (s.c0 + j) % 2
                along(s, j)
                ended(s, j)
                scaled(vB[:, 1, j * CH:(j + 1) * CH], acc[p][1][:, :], "kvl", 1).then_inc(evac_dve, 1)
                if j == 0:
                    for f in (6, 7):
                        copy_batch("uk", f, knT[:, 2 * f:2 * f + 2, :])

            def queries_out(j):
                if j >= 2:
                    dve.wait_ge(sem("q_roped"), j - 1)
                scaled(stg[:, j % 2, 1, 0:2 * QHEAD], acc[0][1][:, 0:2 * QHEAD], "ql", 1).then_inc(evac_dve, 1)

            def roped_out(j):
                n = BATCH["uq", 2 * j + 1][0]
                dve.wait_ge(tp_full, n + 1)
                dve.tensor_copy(qr[:, j % 2, :], tp[n % 2][:, 0:SEQ]).then_inc(tp_done, 1)

            def scores_out(c):
                for i in range(2):
                    h = 2 * c + i
                    dve.wait_ge(sem("attB_s"), h + 1)
                    if c:
                        dve.wait_ge(sem("attB_t"), h - 1)
                    dve.scalar_tensor_tensor(out=sB[:, i, :], in0=xb[i][:, 0:3 * P], scalar=QHEAD ** -0.5, in1=const_of("chunk_neg"),
                                             op0=ALU.mult, op1=ALU.add).then_inc(sem("attB_m"), 1)
                    dve.wait_ge(sem("attB_m"), h + 1)
                    dve.tensor_reduce(mx[:, i, 0:1], sB[:, i, 0:P], AX, ALU.max, negate=True)
                    dve.tensor_reduce(mx[:, i, 1:2], sB[:, i, P:3 * P], AX, ALU.max, negate=True).then_inc(sem("attB_mx"), 1)

            def outputs_over_sums(c):
                dve.wait_ge(sem("attB_out"), c + 1)
                dve.reciprocal(rden[:, c % 2, :], den[:, c % 2, :]).then_inc(sem("attB_r"), 1)
                dve.wait_ge(sem("attB_r"), c + 1)
                dve.tensor_tensor(nat[:, :, c * 2 * HD:(c + 1) * 2 * HD].rearrange("p t (i d) -> p i t d", i=2),
                                  acc[0][0][:, :].rearrange("p (i t d) -> p i t d", i=2, t=TT),
                                  rden[:, c % 2, :].rearrange("p (i t) -> p i t", i=2)[:, :, :, None].to_broadcast((P, 2, TT, HD)),
                                  ALU.mult).then_inc(sem("attB_o"), 1)

            along(S["uq"], 0)
            ended(S["uq"], 0)
            queries_out(0)
            copy_batch("uq", 0, qn[:, 0])
            roped_out(0)
            u = S["attb"].u0
            for c in range(SLOTS):
                more = c + 1 < SLOTS
                scores_out(c)
                for k, (query, uu) in enumerate(slot_units(c)):
                    split_to(u + 4)
                    u += 1
                    if query and uu == 1:
                        dve.wait_ge(unit_used, u)
                        queries_out(c + 1)
                    if more and k == 4:
                        if c:
                            dve.wait_ge(sem("attB_s"), 2 * c)
                        copy_batch("uq", 2 * c + 2, qn[:, (c + 1) % 2])
                    if more and k == 5:
                        roped_out(c + 1)
                outputs_over_sums(c)
                if c == SLOTS - 1:
                    lo_batch("ogB", 0, bhi, blo)
                if c % 2:
                    gated(gate_chunk_at(c // 2), 0, c // 2, sem("attB_o"), c + 1)
            for f in range(1, 3):
                lo_batch("ogB", f, bhi, blo)
            post(1, "ogB", "x3", "x4", GC["norm1"], "norm1")

            metas = [0]

            def plain(name, j, dst, meta=None, hooks={}):
                s = S[name]
                c = s.c0 + j
                along(s, j, hooks)
                ended(s, j)
                m = scaled(dst, acc[c % 2][1][:, 0:s.cols], "norm1", 1)
                if meta is not None:
                    k = metas[0]
                    metas[0] += 1
                    tmp = msc[0:META, 0:s.cols]
                    if k:
                        dve.wait_ge(evac_dve, c)
                    dve.tensor_copy(tmp, xb[c % 2][32:32 + META, 0:s.cols]).then_inc(sem("meta_step"), 1)
                    dve.wait_ge(sem("meta_step"), 2 * k + 1)
                    dve.tensor_tensor(tmp, xb[c % 2][0:META, 0:s.cols], tmp, ALU.add).then_inc(sem("meta_step"), 1)
                    dve.wait_ge(sem("meta_step"), 2 * k + 2)
                    m = dve.tensor_scalar(meta, tmp, rsM, None, ALU.mult)
                m.then_inc(evac_dve, 1)

            def k2_norm():
                norm_of("norm1")
                dve.wait_ge(sem("norm1_rs"), 1)
                dve.wait_ge(sem("metan_rs"), 1)
            plain("k2", 0, kend[:, 1, :], kendM[0:META, :], join(los("x4", bhi, blo, GC["norm1"], LAST), {5: [k2_norm]}))
            dve.wait_ge(sem("glr_zero"), 1)
            plain("glr", 0, glr[:, 1, 0:GRANK], glrM[0:META, 0:GRANK])

            def latents_out():
                n = BATCH["glr", 0][0]
                dve.wait_ge(tp_full, n + 1)
                dve.tensor_copy(glrT[:, :], tp[n % 2][:, 0:SEQ + META]).then_inc(tp_done, 1)
            other = xb[(S["pu0"].c0 + 1) % 2]

            def log_gates():
                for t in range(TT + 1):
                    src = (tp[0], tp[1], other[0:META, :])[t][:, :]
                    soft = stg[:, 1, t, :] if t < TT else msc[0:META, :]
                    dst = logg[:, t, :] if t < TT else loggM[0:META, :]
                    dve.wait_ge(sem("lg"), 2 * (TT + 1) + t + 1)
                    dve.scalar_tensor_tensor(out=dst, in0=src, scalar=0.0, in1=soft, op0=ALU.min, op1=ALU.subtract).then_inc(sem("logg"), 1)

            def keys_from_start():
                dve.wait_ge(sem("eG"), 4)
                dve.tensor_tensor(nat[:, :, 0:CH], nat[:, :, 0:CH], kend[:, :, :], ALU.mult).then_inc(sem("kinv"), 1)

            def keys_to_end():
                dve.wait_ge(sem("eG"), 7)
                dve.tensor_tensor(kend[:, :, :], kend[:, :, :], nat[:, :, CH:2 * CH], ALU.mult).then_inc(sem("kend"), 1)
                dve.tensor_tensor(kendM[0:META, :], kendM[0:META, :], oneM[0:META, :], ALU.mult).then_inc(sem("kend"), 1)

            s = S["pu0"]
            along(s, 0, {4: [latents_out]})
            ended(s, 0)
            dve.wait_ge(sem("metan_rs"), 1)
            scaled(nat[:, 1, 2 * CH:3 * CH], acc[s.c0 % 2][1][:, :], "norm1", 1)
            k = metas[0]
            metas[0] += 1
            dve.tensor_copy(puM[0:META, 0:CH], xb[s.c0 % 2][32:32 + META, :]).then_inc(sem("meta_step"), 1)
            dve.wait_ge(sem("meta_step"), 2 * k + 1)
            dve.tensor_tensor(puM[0:META, 0:CH], xb[s.c0 % 2][0:META, :], puM[0:META, 0:CH], ALU.add).then_inc(sem("meta_step"), 1)
            dve.wait_ge(sem("meta_step"), 2 * k + 2)
            dve.tensor_scalar(puM[0:META, 0:CH], puM[0:META, 0:CH], rsM, None, ALU.mult).then_inc(evac_dve, 1)
            plain("q2", 0, stg[:, 0, 1, :], None, {1: [log_gates], 4: [keys_from_start], 7: [keys_to_end]})

            def queries_from_start():
                dve.wait_ge(evac_act, S["q2"].c0 + 1)
                dve.wait_ge(evac_dve, S["q2"].c0 + 1)
                dve.scalar_tensor_tensor(out=stg[:, 0, :, :], in0=stg[:, 0, :, :], scalar=DK ** -0.5, in1=stg[:, 1, :, :],
                                         op0=ALU.mult, op1=ALU.mult).then_inc(sem("qdec"), 1)

            def decayed_queries_out(f):
                dve.wait_ge(sem("q_zero"), 1)
                n = BATCH["qdec", f][0]
                dve.wait_ge(tp_full, n + 1)
                src = tp[n % 2][:, :].rearrange("p (i t q) -> p i t q", i=2, t=TT)
                dve.tensor_copy(qA[:, 2 * f:2 * f + 2, :, 0:64], src[:, :, :, 0:64])
                dve.tensor_copy(qB[:, 2 * f:2 * f + 2, :, 64:P], src[:, :, :, 64:P]).then_inc(tp_done, 1)
            plain("pu1", 0, nat[:, 1, 3 * CH:4 * CH], puM[0:META, CH:2 * CH],
                  join({1: [queries_from_start]}, {3 + f: [lambda f=f: copy_batch("kinv", f, kTc[:, 2 * f:2 * f + 2, :])] for f in range(2)},
                       {5 + f: [lambda f=f: decayed_queries_out(f)] for f in range(2)}))
            for j in range(2):
                plain("v2", j, vC[:, 1, j * CH:(j + 1) * CH], vM[0:META, j * CH:(j + 1) * CH])

            def head_in(h):
                dve.wait_ge(sem("gla_scores"), h + 1)
                if h == 0:
                    dve.wait_ge(sem("decay"), 1)
                else:
                    dve.wait_ge(sem("gla_out"), h)
                dve.tensor_scalar(sc[:, :, :], tp[0][:, 0:SEQ].rearrange("p (t c) -> p t c", t=TT), 3e38, -3e38, ALU.min, ALU.max).then_inc(sem("gla_clip"), 1)
                dve.wait_ge(sem("gla_ds"), h + 1)
                st = state[:, h % 2]
                dve.tensor_copy(st[:, 0, :], xb[1][:, DV:2 * DV]).then_inc(sem("gla_step"), 1)
                for n, (src, half) in enumerate(((xb[0], 0), (xb[1], 0), (xb[0], 1))):
                    dve.wait_ge(sem("gla_step"), 3 * h + n + 1)
                    m = dve.scalar_tensor_tensor(out=st[:, n + 1, :], in0=st[:, n, :], scalar=decay[:, h, n:n + 1],
                                                 in1=src[:, half * DV:(half + 1) * DV], op0=ALU.mult, op1=ALU.add)
                    m.then_inc(sem("gla_step") if n < 2 else sem("gla_state"), 1)

            def heads_rs():
                dve.wait_ge(sem("gla_root"), 1)
                dve.reciprocal(rs[:, 6, :], root[:, :]).then_inc(sem("gla_rs"), 1)
                dve.wait_ge(sem("gla_rs"), 1)

            def heads_gated(j):
                c, p = S["r2"].c0 + j, (S["r2"].c0 + j) % 2
                dve.wait_ge(evac_act, c + 1)
                for t in range(TT):
                    for i in range(2):
                        h = 2 * j + i
                        o = nat[:, t, h * DV:(h + 1) * DV]
                        m = dve.scalar_tensor_tensor(out=o, in0=o, scalar=rs[:, 6, t * GLA_H + h:t * GLA_H + h + 1],
                                                     in1=stg[:, p, t, i * DV:(i + 1) * DV], op0=ALU.mult, op1=ALU.mult)
                m.then_inc(evac_dve, 1)
            mixed_gain = lambda f, i: GC["gla"] + i if f < 4 else GC["pool"] + 2 * (f - 4) + i
            along(S["r2"], 0, {2 * h: [lambda h=h: head_in(h)] for h in range(GLA_H)})
            sq[0] += 2 * GLA_H
            along(S["r2"], 1, join({1: [heads_rs, lambda: heads_gated(0)]}, {2 + f: [lambda f=f: lo_batch("pool", f, yhi, ylo)] for f in range(4)},
                                   los("mixed", ahi, alo, mixed_gain, {6: [0], 7: [1]})))
            heads_gated(1)
            s = S["pool"]
            for j in range(2):
                c = s.c0 + j
                split_to(s.u0 + j + 1 + 3)
                ended(s, j)
                dve.tensor_copy(nat[:, 1, (2 + j) * CH:(3 + j) * CH], acc[c % 2][1][:, :]).then_inc(evac_dve, 1)
            for f in (2, 3):
                lo_batch("mixed", f, ahi, alo, mixed_gain)

            def added(s, j):
                c, p = s.c0 + j, (s.c0 + j) % 2
                split_to(min(s.u0 + (j + 1) * s.units + 3, units))
                dve.wait_ge(evac_act, c + 1)
                x0, x1 = (x[:, t, j * CH:(j + 1) * CH] for t in range(TT))
                dve.tensor_tensor(x0, x0, stg[:, p, 0, :], ALU.add)
                dve.tensor_tensor(x1, x1, acc[p][1][:, :], ALU.add).then_inc(evac_dve, 1)

            for j in range(4):
                along(S["out2"], j, los("x5", bhi, blo, GC["norm2"], ALONG[j]) if j else los("mixed", ahi, alo, mixed_gain, MIXED_LATE))
                added(S["out2"], j)
            for q in range(DFF // D):
                s = S[f"up{q}"]
                for j in range(4):
                    p = (s.c0 + j) % 2
                    first_x = q == 0 and j == 0
                    along(s, j, los(f"mlp{q}", ahi, alo, None, ALONG[j]) if j else
                          join(los("x5", bhi, blo, GC["norm2"], LAST), {4: [lambda: norm_of("norm2")]}) if first_x else {})
                    if first_x:
                        dve.wait_ge(sem("norm2_rs"), 1)
                    ended(s, j)
                    n = 4 * q + j
                    dve.tensor_scalar(stg[:, p, 1, :], acc[p][1][:, :], rs[:, RS["norm2"], 1:2], 0.0, ALU.mult, ALU.max).then_inc(sem("relu_dve"), 1)
                    dve.wait_ge(sem("relu_dve"), n + 1)
                    dve.tensor_tensor(stg[:, p, 1, :], stg[:, p, 1, :], stg[:, p, 1, :], ALU.mult).then_inc(evac_dve, 1)
                for j in range(4):
                    along(S[f"down{q}"], j, los(f"mlp{q}", ahi, alo, None, LAST) if j == 0 else {})
                    added(S[f"down{q}"], j)
            norm_of("final")
            dve.wait_ge(sem("final_rs"), 1)
            dve.wait_ge(sem("final_in"), 16)
            for j in range(NCH):
                for t in range(TT):
                    dve.scalar_tensor_tensor(out=nat[:, t, j * CH:(j + 1) * CH], in0=x[:, t, j * CH:(j + 1) * CH],
                                             scalar=rs[:, RS["final"], t:t + 1], in1=gains[:, j * CH:(j + 1) * CH],
                                             op0=ALU.mult, op1=ALU.mult).then_inc(sem("final_y"), 1)

        @block.gpsimd
        def _(pool):
            step = [0]
            cos = const_of("cos").rearrange("p (t i c) -> p t i c", t=TT, i=2)
            sin = const_of("sin").rearrange("p (t i c) -> p t i c", t=TT, i=2)
            dst = roped[:, :, :].rearrange("p t (i c) -> p t i c", i=2)
            half = ROPE // 2

            def op(out_, a, b_, f):
                pool.tensor_tensor(out_, a, b_, f).then_inc(sem("rope_step"), 1)
                step[0] += 1
                pool.wait_ge(sem("rope_step"), step[0])

            def rotate(a, b_):
                op(dst[:, :, :, 0:half], a, cos, ALU.mult)
                op(turn[:, :, :, :], b_, sin, ALU.mult)
                op(dst[:, :, :, 0:half], dst[:, :, :, 0:half], turn[:, :, :, :], ALU.subtract)
                op(dst[:, :, :, half:ROPE], a, sin, ALU.mult)
                op(turn[:, :, :, :], b_, cos, ALU.mult)
                return pool.tensor_tensor(dst[:, :, :, half:ROPE], dst[:, :, :, half:ROPE], turn[:, :, :, :], ALU.add)

            pool.wait_ge(sem("tab_in"), 16)

            def diagonal(a):
                return a.rearrange("p h (b q) -> p h b q", b=3)[:, :, 0:3:2, :]

            def blocks(name):
                return const_of(name)[:, None, None, :].to_broadcast((P, 2, 2, P))

            def masked_softplus(c):
                pool.wait_ge(sem("attA_z"), c + 1)
                if c:
                    pool.wait_ge(sem("attA_sums"), c)
                z = zA[:, c % 2]
                pool.tensor_scalar(tA[:, :, :], z, 0.0, -2.0, ALU.max, ALU.mult).then_inc(sem("attA_abs"), 1)
                pool.wait_ge(sem("attA_abs"), 2 * c + 1)
                pool.tensor_tensor(tA[:, :, :], tA[:, :, :], z, ALU.add).then_inc(sem("attA_abs"), 1)
                pool.wait_ge(sem("attA_m"), c + 1)
                pool.tensor_tensor(diagonal(tA[:, :, :]), diagonal(tA[:, :, :]), blocks("strict"), ALU.mult).then_inc(sem("attA_sp"), 1)
                pool.tensor_tensor(diagonal(z), diagonal(z), blocks("strict_neg"), ALU.add).then_inc(sem("attA_n"), 1)

            for c in range(HEADS // 2):
                masked_softplus(c)

            s = S["krope"]
            pool.wait_ge(evac_act, s.c0 + 1)
            pool.wait_ge(evac_dve, s.c0 + 1)
            rotate(kraw[:, :, :, 0:half], kraw[:, :, :, half:ROPE]).then_inc(sem("k_roped"), 1)
            for j in range(SLOTS):
                pool.wait_ge(evac_act, q_chunk_at(j) + 1)
                pool.wait_ge(evac_dve, q_chunk_at(j) + 1)
                pool.wait_ge(sem("q_roped") if j else sem("k_roped"), max(j, 1))
                pool.wait_ge(tp_full, BATCH["uq", 2 * j][0] if j else BATCH["kr", 0][0] + 1)
                q = stg[:, j % 2, :, 0:2 * QHEAD].rearrange("p t (i c) -> p t i c", i=2)
                rotate(q[:, :, :, HD:HD + half], q[:, :, :, HD + half:QHEAD]).then_inc(sem("q_roped"), 1)
            pool.wait_ge(sem("attB_o"), SLOTS)
            pool.memset(metaT[:, :, :].bitcast(F32), 0.0).then_inc(sem("meta_zero"), 1)
            pool.wait_ge(x_done, 16)
            pool.memset(glr[:, :, :], 0.0)
            pool.memset(glrM[:, :], 0.0).then_inc(sem("glr_zero"), 1)
            pool.memset(qA[:, :, :, :], 0.0)
            pool.memset(qB[:, :, :, :], 0.0).then_inc(sem("q_zero"), 1)
            for h in range(GLA_H):
                pool.wait_ge(sem("gla_clip"), h + 1)
                pool.tensor_tensor(sc[:, :, :], sc[:, :, :], const_of("gla_causal")[:, None, :].to_broadcast((P, TT, P)), ALU.mult).then_inc(sem("gla_sc"), 1)


_INS = ["x", "p", "norm_pre", "norm_post", "w_in_a", "w_out_a", "w_in_b", "q_latent_norm", "w_uq", "w_out_b", "kv_norm",
        "w_dkv", "kv_latent_norm", "w_uk", "w_uv", "w_ple_proj", "w_ple_gate", "meta_tokens_2", "norm1_w_2", "w_in_2",
        "gate_w2_2", "gate_b_2", "gla_norm_w_2", "pool_w_2", "pool_scale_2", "w_out_2", "norm2_w_2", "mlp_w1_2",
        "mlp_w2_2", "final_norm_w_2"]


def kernel(**inputs):
    import numpy as _np
    import concourse.bacc as _bacc
    from concourse import mybir as _mybir
    from concourse.bass_utils import run_bass_kernel_spmd as _run

    nc = _bacc.Bacc("TRN2", target_bir_lowering=False, num_devices=1)
    arrays, w = {}, {}
    for name in _INS:
        a = _np.ascontiguousarray(inputs[name])
        arrays[f"in_{name}"] = a
        w[name] = nc.dram_tensor(f"in_{name}", a.shape, _mybir.dt.from_np(a.dtype), kind="ExternalInput").ap()
    table, _ = constants()
    arrays["tables"] = table
    const = nc.dram_tensor("tables", table.shape, F32, kind="ExternalInput").ap()
    out = nc.dram_tensor("out_0", (1, SEQ, D), F32, kind="ExternalOutput").ap()
    build(nc, w, const, out)
    r = _run(nc, [arrays], core_ids=[0])
    return r.results[0]["out_0"]
```
